# Optimizing a Trainium2 kernel written in Bass

```python
import jax, jax.numpy as jnp
from jax import lax
import numpy as np
import math
import jax
import jax.numpy as jnp

D_MODEL = 1024
BATCH = 1
SEQ = 256
DEPTH = 2

D_MIX = D_MODEL
GLA_HEADS = 4
GLA_DK = 64
GLA_DV = 128
GLA_QK = GLA_HEADS * GLA_DK
GLA_WIDTH = GLA_HEADS * GLA_DV
GLA_LOWRANK = 16
GLA_TAU = 16.0
GLA_CHUNK = 64
SSD_HEADS = 8
SSD_HEADDIM = 64
SSD_WIDTH = SSD_HEADS * SSD_HEADDIM
SSD_GROUPS = 2
SSD_STATE = 64
SSD_BC = SSD_GROUPS * SSD_STATE
SSD_CONV = 4
SSD_CONV_DIM = SSD_WIDTH + 2 * SSD_BC
SSD_CHUNK = 128
D_FF = 3584
N_EXPERTS = 8
TOP_K = 2
EPS = 1e-6

IN_SIZES = (GLA_QK, GLA_QK, GLA_WIDTH, GLA_WIDTH, GLA_LOWRANK,
            SSD_WIDTH, SSD_WIDTH, SSD_BC, SSD_BC, SSD_HEADS)
IN_SPLITS = [int(s) for s in np.cumsum(IN_SIZES)[:-1]]
D_IN_PROJ = int(sum(IN_SIZES))


def rmsnorm(x, w):
    x32 = x.astype(jnp.float32)
    r = x32 * lax.rsqrt(jnp.mean(x32 * x32, axis=-1, keepdims=True) + EPS)
    return (r * w.astype(jnp.float32)).astype(x.dtype)

def inter_chunk_states(decay, contrib):
    d = jnp.moveaxis(decay, 1, 0)
    u = jnp.moveaxis(contrib, 1, 0)

    def step(s, inp):
        dn, un = inp
        return dn * s + un, s

    _, prev = lax.scan(step, jnp.zeros_like(u[0]), (d, u))
    return jnp.moveaxis(prev, 0, 1)

def gla_chunked(q, k, v, log_a):
    bsz, seq, nh, dk = q.shape
    dv = v.shape[-1]
    nc = seq // GLA_CHUNK
    shp = lambda t: t.astype(jnp.float32).reshape(bsz, nc, GLA_CHUNK, nh, t.shape[-1])
    q, k, v, log_a = shp(q) * (dk ** -0.5), shp(k), shp(v), shp(log_a)
    b = jnp.cumsum(log_a, axis=2)
    qe = q * jnp.exp(b)
    ke = k * jnp.exp(-b)
    causal = jnp.tril(jnp.ones((GLA_CHUNK, GLA_CHUNK), bool))
    att = jnp.einsum('bnihd,bnjhd->bnhij', qe, ke)
    att = jnp.where(causal, att, 0.0)
    o_intra = jnp.einsum('bnhij,bnjhv->bnihv', att, v)
    b_last = b[:, :, -1]
    k_tail = k * jnp.exp(b_last[:, :, None] - b)
    contrib = jnp.einsum('bnjhd,bnjhv->bnhdv', k_tail, v)
    s_prev = inter_chunk_states(jnp.exp(b_last)[..., None], contrib)
    o_inter = jnp.einsum('bnihd,bnhdv->bnihv', qe, s_prev)
    return (o_intra + o_inter).reshape(bsz, seq, nh, dv)

def ssd_chunked(xh, dt, a, bm, cm):
    bsz, seq, nh, p = xh.shape
    rep = nh // bm.shape[2]
    nc = seq // SSD_CHUNK
    f = lambda t: t.astype(jnp.float32).reshape((bsz, nc, SSD_CHUNK) + t.shape[2:])
    xh, dt = f(xh), f(dt)
    bh = f(jnp.repeat(bm, rep, axis=2))
    ch = f(jnp.repeat(cm, rep, axis=2))
    cum = jnp.cumsum(dt * a, axis=2)
    causal = jnp.tril(jnp.ones((SSD_CHUNK, SSD_CHUNK), bool))[:, :, None]
    seg = cum[:, :, :, None, :] - cum[:, :, None, :, :]
    decay = jnp.exp(jnp.where(causal, seg, -jnp.inf))
    xdt = xh * dt[..., None]
    scores = jnp.einsum('bnihs,bnjhs->bnijh', ch, bh) * decay
    y_intra = jnp.einsum('bnijh,bnjhp->bnihp', scores, xdt)
    cum_last = cum[:, :, -1]
    contrib = jnp.einsum('bnjhs,bnjhp->bnhps',
                         bh * jnp.exp(cum_last[:, :, None] - cum)[..., None], xdt)
    s_prev = inter_chunk_states(jnp.exp(cum_last)[..., None, None], contrib)
    y_inter = jnp.einsum('bnihs,bnhps->bnihp', ch * jnp.exp(cum)[..., None], s_prev)
    return (y_intra + y_inter).reshape(bsz, seq, nh, p)

def causal_depthwise_conv(u, w, b):
    kw, cdim = w.shape
    out = lax.conv_general_dilated(u, w.astype(u.dtype)[:, None, :], window_strides=(1,),
                                   padding=[(kw - 1, 0)],
                                   dimension_numbers=('NWC', 'WIO', 'NWC'),
                                   feature_group_count=cdim)
    return out + b.astype(u.dtype)

def hybrid_mixer(h, w_in, gla_a_w, gla_a_b, gla_norm_w, conv_w, conv_b,
                 dt_bias, a_log, d_skip, ssd_norm_w, w_out):
    bsz, seq, _ = h.shape
    proj = h @ w_in
    q, k, v, g, alr, z, xs, bm, cm, dt = jnp.split(proj, IN_SPLITS, axis=-1)
    log_a = jax.nn.log_sigmoid((alr @ gla_a_w + gla_a_b).astype(jnp.float32)) / GLA_TAU
    o = gla_chunked(q.reshape(bsz, seq, GLA_HEADS, GLA_DK),
                    k.reshape(bsz, seq, GLA_HEADS, GLA_DK),
                    v.reshape(bsz, seq, GLA_HEADS, GLA_DV),
                    log_a.reshape(bsz, seq, GLA_HEADS, GLA_DK))
    o = rmsnorm(o, gla_norm_w) * jax.nn.silu(g.astype(jnp.float32).reshape(bsz, seq, GLA_HEADS, GLA_DV))
    o = o.reshape(bsz, seq, GLA_WIDTH)
    xbc = jax.nn.silu(causal_depthwise_conv(jnp.concatenate([xs, bm, cm], axis=-1), conv_w, conv_b))
    xs, bm, cm = jnp.split(xbc, [SSD_WIDTH, SSD_WIDTH + SSD_BC], axis=-1)
    dt = jax.nn.softplus(dt.astype(jnp.float32) + dt_bias.astype(jnp.float32))
    a = -jnp.exp(a_log.astype(jnp.float32))
    xh = xs.reshape(bsz, seq, SSD_HEADS, SSD_HEADDIM)
    y = ssd_chunked(xh, dt, a,
                    bm.reshape(bsz, seq, SSD_GROUPS, SSD_STATE),
                    cm.reshape(bsz, seq, SSD_GROUPS, SSD_STATE))
    y = y + d_skip.astype(jnp.float32)[:, None] * xh.astype(jnp.float32)
    y = y.reshape(bsz, seq, SSD_WIDTH) * jax.nn.silu(z.astype(jnp.float32))
    y = rmsnorm(y, ssd_norm_w)
    merged = jnp.concatenate([o, y], axis=-1).astype(h.dtype)
    return merged @ w_out

def swiglu(t, w_gate, w_up, w_down):
    return (jax.nn.silu(t @ w_gate) * (t @ w_up)) @ w_down

def moe_swiglu(h, router_w, w_gate, w_up, w_down):
    bsz, seq, d = h.shape
    t = h.reshape(bsz * seq, d)
    logits = (t @ router_w).astype(jnp.float32)
    top_v, top_i = lax.top_k(logits, TOP_K)
    top_p = jax.nn.softmax(top_v, axis=-1)
    gates = jnp.sum(jax.nn.one_hot(top_i, N_EXPERTS, dtype=jnp.float32) * top_p[..., None], axis=1)
    gates = gates.astype(h.dtype)
    out = jnp.zeros_like(t)
    for e in range(N_EXPERTS):
        out = out + gates[:, e:e + 1] * swiglu(t, w_gate[e], w_up[e], w_down[e])
    return out.reshape(bsz, seq, d)

def first_inputs(seed: int = 0) -> dict:
    key = jax.random.key(seed)
    ks = iter(list(jax.random.split(key, 40)))
    f32 = jnp.float32
    nrm = lambda shape, scale: jax.random.normal(next(ks), shape, f32) * scale
    n_dense = (DEPTH + 1) // 2
    n_moe = DEPTH // 2
    d = D_MODEL
    x = nrm((BATCH, SEQ, d), 1.0)
    c = nrm((BATCH, d), 1.0)
    ada_w = nrm((DEPTH, d, 6 * d), 0.5 * d ** -0.5)
    ada_b = nrm((DEPTH, 6 * d), 0.02)
    norm1_w = 1.0 + nrm((DEPTH, d), 0.02)
    w_in = nrm((DEPTH, d, D_IN_PROJ), d ** -0.5)
    gla_a_w = nrm((DEPTH, GLA_LOWRANK, GLA_QK), GLA_LOWRANK ** -0.5)
    gla_a_b = nrm((DEPTH, GLA_QK), 0.1)
    gla_norm_w = 1.0 + nrm((DEPTH, GLA_DV), 0.02)
    conv_w = nrm((DEPTH, SSD_CONV, SSD_CONV_DIM), SSD_CONV ** -0.5)
    conv_b = nrm((DEPTH, SSD_CONV_DIM), 0.02)
    dt0 = jnp.exp(jax.random.uniform(next(ks), (DEPTH, SSD_HEADS), f32,
                                     np.log(1e-3).astype(np.float32), np.log(1e-1).astype(np.float32)))
    dt_bias = dt0 + jnp.log(-jnp.expm1(-dt0))
    a_log = jnp.log(jax.random.uniform(next(ks), (DEPTH, SSD_HEADS), f32, 1.0, 16.0))
    d_skip = 1.0 + nrm((DEPTH, SSD_HEADS), 0.1)
    ssd_norm_w = 1.0 + nrm((DEPTH, SSD_WIDTH), 0.02)
    w_out = nrm((DEPTH, D_MIX, d), D_MIX ** -0.5)
    norm2_w = 1.0 + nrm((DEPTH, d), 0.02)
    ffn_w_gate = nrm((n_dense, d, D_FF), d ** -0.5)
    ffn_w_up = nrm((n_dense, d, D_FF), d ** -0.5)
    ffn_w_down = nrm((n_dense, D_FF, d), D_FF ** -0.5)
    router_w = nrm((n_moe, d, N_EXPERTS), d ** -0.5)
    moe_w_gate = nrm((n_moe, N_EXPERTS, d, D_FF), d ** -0.5)
    moe_w_up = nrm((n_moe, N_EXPERTS, d, D_FF), d ** -0.5)
    moe_w_down = nrm((n_moe, N_EXPERTS, D_FF, d), D_FF ** -0.5)
    final_norm_w = 1.0 + nrm((d,), 0.02)
    return {"x": x, "c": c, "ada_w": ada_w, "ada_b": ada_b, "norm1_w": norm1_w,
            "w_in": w_in, "gla_a_w": gla_a_w, "gla_a_b": gla_a_b, "gla_norm_w": gla_norm_w,
            "conv_w": conv_w, "conv_b": conv_b, "dt_bias": dt_bias, "a_log": a_log,
            "d_skip": d_skip, "ssd_norm_w": ssd_norm_w, "w_out": w_out, "norm2_w": norm2_w,
            "ffn_w_gate": ffn_w_gate, "ffn_w_up": ffn_w_up, "ffn_w_down": ffn_w_down,
            "router_w": router_w, "moe_w_gate": moe_w_gate, "moe_w_up": moe_w_up,
            "moe_w_down": moe_w_down, "final_norm_w": final_norm_w}

def first_block(x, c, ada_w, ada_b, norm1_w, w_in, gla_a_w, gla_a_b, gla_norm_w,
              conv_w, conv_b, dt_bias, a_log, d_skip, ssd_norm_w, w_out, norm2_w,
              ffn_w_gate, ffn_w_up, ffn_w_down, router_w, moe_w_gate, moe_w_up,
              moe_w_down, final_norm_w):
    s = jax.nn.silu(c)
    for l in range(DEPTH):
        mod = s @ ada_w[l] + ada_b[l]
        sh1, sc1, g1, sh2, sc2, g2 = [m[:, None, :] for m in jnp.split(mod, 6, axis=-1)]
        h = rmsnorm(x, norm1_w[l]) * (1.0 + sc1) + sh1
        mix = hybrid_mixer(h, w_in[l], gla_a_w[l], gla_a_b[l], gla_norm_w[l], conv_w[l],
                           conv_b[l], dt_bias[l], a_log[l], d_skip[l], ssd_norm_w[l], w_out[l])
        x = x + g1 * mix
        h = rmsnorm(x, norm2_w[l]) * (1.0 + sc2) + sh2
        if l % 2 == 0:
            i = l // 2
            ff = swiglu(h, ffn_w_gate[i], ffn_w_up[i], ffn_w_down[i])
        else:
            i = l // 2
            ff = moe_swiglu(h, router_w[i], moe_w_gate[i], moe_w_up[i], moe_w_down[i])
        x = x + g2 * ff
    return rmsnorm(x, final_norm_w)


DEPTH_2 = 1

GRID_W = 64
CTX_LEN = 256
N_MOD = 6

D_HY = 512
HY_ORDER = 2
HY_BANDS = 16
HY_EMB = 1 + 2 * HY_BANDS
HY_FFN = 64
HY_DECAY_TARGET = 1e-2
HY_FAST_PCT = 0.3
HY_SLOW_PCT = 1.5

NA_HEADS = 8
HEAD_DIM = 64
D_NA = NA_HEADS * HEAD_DIM
WIN_ROWS = 8
WIN_COLS = 16
ROPE_THETA = 10000.0
NEG_INF = -1e30

PEER_HEADS = 8
PEER_N_KEYS = 128
PEER_N_EXPERTS = PEER_N_KEYS * PEER_N_KEYS
PEER_TOPK = 16
PEER_D_KEY = 256
PEER_D_HALF = PEER_D_KEY // 2
PEER_BLOCK = 128

COL_HY = 0
COL_Q = COL_HY + 3 * D_HY
COL_K = COL_Q + D_NA
COL_V = COL_K + D_NA
COL_G_HY = COL_V + D_NA
COL_G_NA = COL_G_HY + D_MODEL
N_PROJ = COL_G_NA + D_MODEL


def rmsnorm_2(x, g):
    x32 = x.astype(jnp.float32)
    y = x32 * lax.rsqrt(jnp.mean(x32 * x32, axis=-1, keepdims=True) + EPS)
    return (y * g.astype(jnp.float32)).astype(x.dtype)

def modulate(x, g, shift, scale):
    return rmsnorm_2(x, g) * (1.0 + scale) + shift

def adaln(cond, p):
    m = jax.nn.silu(cond) @ p['w_ada'] + p['b_ada']
    return m.reshape(cond.shape[:-1] + (N_MOD, D_MODEL))

def hyena_filters(L, p):
    f32 = jnp.float32
    t = jnp.linspace(0.0, 1.0, L, dtype=f32)[:, None]
    w = (2.0 * math.pi / L) * jnp.arange(L, dtype=f32)[:, None]
    bands = jnp.linspace(1e-4, HY_BANDS - 1.0, HY_BANDS, dtype=f32)[None, :]
    feats = jnp.concatenate([t, jnp.cos(bands * w), -jnp.sin(bands * w)], axis=-1)
    freq = p['hy_sin_freq'].astype(f32)
    h = jnp.sin(freq * (feats @ p['hy_f1_w'].astype(f32) + p['hy_f1_b'].astype(f32)))
    h = jnp.sin(freq * (h @ p['hy_f2_w'].astype(f32) + p['hy_f2_b'].astype(f32)))
    h = jnp.sin(freq * (h @ p['hy_f3_w'].astype(f32) + p['hy_f3_b'].astype(f32)))
    h = (h @ p['hy_f4_w'].astype(f32)).reshape(L, HY_ORDER, 2, D_HY)
    deltas = jnp.abs(jnp.linspace(math.log(HY_DECAY_TARGET) / HY_SLOW_PCT,
                                  math.log(HY_DECAY_TARGET) / HY_FAST_PCT, D_HY, dtype=f32))
    h = h * jnp.exp(-t * deltas)[:, None, None, :]
    h = h / jnp.sum(jnp.abs(h), axis=(0, 2), keepdims=True)
    fwd, bwd = h[:, :, 0], h[:, :, 1]
    return jnp.concatenate([fwd, jnp.zeros_like(fwd[:1]), bwd[:0:-1]], axis=0)

def hyena(zh, p):
    B, L, _ = zh.shape
    cw = p['hy_conv_w']
    zp = jnp.pad(zh, ((0, 0), (1, 1), (0, 0)))
    zc = cw[0] * zp[:, :-2] + cw[1] * zp[:, 1:-1] + cw[2] * zp[:, 2:] + p['hy_conv_b']
    v, x1, x2 = jnp.split(zc.astype(jnp.float32), 3, axis=-1)
    kf = jnp.fft.rfft(hyena_filters(L, p), axis=0)
    skip = p['hy_skip'].astype(jnp.float32)
    y = v
    for o, gate in enumerate((x1, x2)):
        yf = jnp.fft.rfft(y, n=2 * L, axis=1)
        conv = jnp.fft.irfft(yf * kf[:, o][None], n=2 * L, axis=1)[:, :L]
        y = gate * (conv + skip[o] * y)
    return y.astype(zh.dtype)

def axial_rope(x):
    f32 = jnp.float32
    S = x.shape[1]
    pos = jnp.arange(S, dtype=jnp.int32)
    rows = (pos // GRID_W).astype(f32)
    cols = (pos % GRID_W).astype(f32)
    half = HEAD_DIM // 2
    nf = half // 2
    inv = ROPE_THETA ** (-jnp.arange(nf, dtype=f32) / nf)

    def rot(xp, ps):
        ang = ps[:, None] * inv[None, :]
        cos = jnp.cos(ang)[None, :, None, :]
        sin = jnp.sin(ang)[None, :, None, :]
        a, b = xp[..., :nf], xp[..., nf:]
        return jnp.concatenate([a * cos - b * sin, a * sin + b * cos], axis=-1)

    x32 = x.astype(f32)
    return jnp.concatenate([rot(x32[..., :half], rows), rot(x32[..., half:], cols)], axis=-1).astype(x.dtype)

def neighbourhood_attention(q, k, v, k_ctx, v_ctx, rpb):
    B, S, H, Dh = q.shape
    rows = S // GRID_W
    wr = min(WIN_ROWS, rows)
    r = np.arange(rows)
    row_start = np.clip(r - wr // 2, 0, rows - wr)
    row_idx = row_start[:, None] + np.arange(wr)[None, :]
    col = np.arange(GRID_W)
    col_start = np.clip(col - WIN_COLS // 2, 0, GRID_W - WIN_COLS)
    col_mask = (col[None, :] >= col_start[:, None]) & (col[None, :] < col_start[:, None] + WIN_COLS)
    dr_idx = row_idx - r[:, None] + (WIN_ROWS - 1)
    dc_idx = np.clip(col[None, :] - col[:, None], -(WIN_COLS - 1), WIN_COLS - 1) + (WIN_COLS - 1)
    bias = rpb[:, dr_idx[:, None, :, None], dc_idx[None, :, None, :]]

    qg = q.reshape(B, rows, GRID_W, H, Dh)
    kg = k.reshape(B, rows, GRID_W, H, Dh)[:, row_idx]
    vg = v.reshape(B, rows, GRID_W, H, Dh)[:, row_idx]
    scale = HEAD_DIM ** -0.5
    s_loc = jnp.einsum('brqhd,brikhd->bhrqik', qg, kg).astype(jnp.float32) * scale + bias.astype(jnp.float32)
    s_loc = jnp.where(col_mask[:, None, :], s_loc, NEG_INF).reshape(B, H, rows, GRID_W, wr * GRID_W)
    s_ctx = jnp.einsum('brqhd,bchd->bhrqc', qg, k_ctx).astype(jnp.float32) * scale
    p = jax.nn.softmax(jnp.concatenate([s_loc, s_ctx], axis=-1), axis=-1).astype(v.dtype)
    n_loc = wr * GRID_W
    p_loc = p[..., :n_loc].reshape(B, H, rows, GRID_W, wr, GRID_W)
    out = (jnp.einsum('bhrqik,brikhd->brqhd', p_loc, vg)
           + jnp.einsum('bhrqc,bchd->brqhd', p[..., n_loc:], v_ctx))
    return out.reshape(B, S, H, Dh)

def context_attention(q, k, v):
    s = jnp.einsum('bqhd,bkhd->bhqk', q, k).astype(jnp.float32) * (HEAD_DIM ** -0.5)
    p = jax.nn.softmax(s, axis=-1).astype(v.dtype)
    return jnp.einsum('bhqk,bkhd->bqhd', p, v)

def context_kv(h_ctx, p):
    B, C, _ = h_ctx.shape
    k = (h_ctx @ p['w_in'][:, COL_K:COL_V] + p['b_in'][COL_K:COL_V]).reshape(B, C, NA_HEADS, HEAD_DIM)
    v = (h_ctx @ p['w_in'][:, COL_V:COL_G_HY] + p['b_in'][COL_V:COL_G_HY]).reshape(B, C, NA_HEADS, HEAD_DIM)
    return rmsnorm_2(k, p['k_norm_g']), v

def token_mixer(h, p, attend):
    B, L, _ = h.shape
    z = h @ p['w_in'] + p['b_in']
    q = rmsnorm_2(z[..., COL_Q:COL_K].reshape(B, L, NA_HEADS, HEAD_DIM), p['q_norm_g'])
    k = rmsnorm_2(z[..., COL_K:COL_V].reshape(B, L, NA_HEADS, HEAD_DIM), p['k_norm_g'])
    v = z[..., COL_V:COL_G_HY].reshape(B, L, NA_HEADS, HEAD_DIM)
    y_hy = hyena(z[..., COL_HY:COL_Q], p) @ p['w_hy_out']
    y_na = attend(q, k, v).reshape(B, L, D_NA) @ p['w_na_out']
    gate = jax.nn.sigmoid(z[..., COL_G_HY:N_PROJ].astype(jnp.float32)).astype(h.dtype)
    merged = gate[..., :D_MODEL] * y_hy + gate[..., D_MODEL:] * y_na
    return merged @ p['w_out']

def peer(h, p):
    B, L, D = h.shape
    T = B * L
    hf = h.reshape(T, D)
    q = (hf @ p['peer_w_q']).reshape(T, PEER_HEADS, 2, PEER_D_HALF)
    s = jnp.einsum('thpd,hpnd->thpn', q, p['peer_keys']).astype(jnp.float32)
    top_s, top_i = lax.top_k(s, PEER_TOPK)
    cand_s = (top_s[:, :, 0, :, None] + top_s[:, :, 1, None, :]).reshape(T, PEER_HEADS, PEER_TOPK * PEER_TOPK)
    cand_i = (top_i[:, :, 0, :, None] * PEER_N_KEYS + top_i[:, :, 1, None, :]).reshape(T, PEER_HEADS, PEER_TOPK * PEER_TOPK)
    best_s, best_pos = lax.top_k(cand_s, PEER_TOPK)
    idx = jnp.take_along_axis(cand_i, best_pos, axis=-1)
    g = jax.nn.softmax(best_s, axis=-1).astype(h.dtype)
    nb = T // PEER_BLOCK
    u_tab, v_tab = p['peer_u'], p['peer_v']

    def block(args):
        xb, ib, gb = args
        act = jax.nn.gelu(jnp.einsum('td,thkd->thk', xb, u_tab[ib]), approximate=False)
        return jnp.einsum('thk,thkd->td', gb * act, v_tab[ib])

    out = lax.map(block, (hf.reshape(nb, PEER_BLOCK, D),
                          idx.reshape(nb, PEER_BLOCK, PEER_HEADS, PEER_TOPK),
                          g.reshape(nb, PEER_BLOCK, PEER_HEADS, PEER_TOPK)))
    return out.reshape(B, L, D)

def second_inputs(seed: int = 0) -> dict:
    key = jax.random.key(seed)
    ks = jax.random.split(key, 32)
    f32 = jnp.float32

    def nrm(k, shape, scale):
        return jax.random.normal(k, shape, f32) * scale

    Ld = DEPTH_2
    return {
        'x': nrm(ks[0], (BATCH, SEQ, D_MODEL), 1.0),
        'c': nrm(ks[1], (BATCH, D_MODEL), 1.0),
        'ctx': nrm(ks[2], (BATCH, CTX_LEN, D_MODEL), 1.0),
        'c_ctx': nrm(ks[3], (D_MODEL,), 1.0),
        'norm1_g': 1.0 + nrm(ks[4], (Ld, D_MODEL), 0.02),
        'norm2_g': 1.0 + nrm(ks[5], (Ld, D_MODEL), 0.02),
        'w_ada': nrm(ks[6], (Ld, D_MODEL, N_MOD * D_MODEL), D_MODEL ** -0.5),
        'b_ada': nrm(ks[7], (Ld, N_MOD * D_MODEL), 0.02),
        'w_in': nrm(ks[8], (Ld, D_MODEL, N_PROJ), D_MODEL ** -0.5),
        'b_in': nrm(ks[9], (Ld, N_PROJ), 0.02),
        'hy_conv_w': nrm(ks[10], (Ld, 3, 3 * D_HY), 3 ** -0.5),
        'hy_conv_b': nrm(ks[11], (Ld, 3 * D_HY), 0.02),
        'hy_f1_w': nrm(ks[12], (Ld, HY_EMB, HY_FFN), HY_EMB ** -0.5),
        'hy_f1_b': nrm(ks[13], (Ld, HY_FFN), 0.02),
        'hy_f2_w': nrm(ks[14], (Ld, HY_FFN, HY_FFN), HY_FFN ** -0.5),
        'hy_f2_b': nrm(ks[15], (Ld, HY_FFN), 0.02),
        'hy_f3_w': nrm(ks[16], (Ld, HY_FFN, HY_FFN), HY_FFN ** -0.5),
        'hy_f3_b': nrm(ks[17], (Ld, HY_FFN), 0.02),
        'hy_f4_w': nrm(ks[18], (Ld, HY_FFN, HY_ORDER * 2 * D_HY), HY_FFN ** -0.5),
        'hy_sin_freq': 1.0 + nrm(ks[19], (Ld, HY_FFN), 0.02),
        'hy_skip': nrm(ks[20], (Ld, HY_ORDER, D_HY), 0.5),
        'q_norm_g': 1.0 + nrm(ks[21], (Ld, HEAD_DIM), 0.02),
        'k_norm_g': 1.0 + nrm(ks[22], (Ld, HEAD_DIM), 0.02),
        'na_rpb': nrm(ks[23], (Ld, NA_HEADS, 2 * WIN_ROWS - 1, 2 * WIN_COLS - 1), 0.02),
        'w_hy_out': nrm(ks[24], (Ld, D_HY, D_MODEL), D_HY ** -0.5),
        'w_na_out': nrm(ks[25], (Ld, D_NA, D_MODEL), D_NA ** -0.5),
        'w_out': nrm(ks[26], (Ld, D_MODEL, D_MODEL), D_MODEL ** -0.5),
        'peer_w_q': nrm(ks[27], (Ld, D_MODEL, PEER_HEADS * PEER_D_KEY), D_MODEL ** -0.5),
        'peer_keys': nrm(ks[28], (Ld, PEER_HEADS, 2, PEER_N_KEYS, PEER_D_HALF), PEER_D_HALF ** -0.5),
        'peer_u': nrm(ks[29], (Ld, PEER_N_EXPERTS, D_MODEL), D_MODEL ** -0.5),
        'peer_v': nrm(ks[30], (Ld, PEER_N_EXPERTS, D_MODEL), 0.5),
    }

def second_block(x, c, ctx, c_ctx, norm1_g, norm2_g, w_ada, b_ada, w_in, b_in, hy_conv_w, hy_conv_b,
              hy_f1_w, hy_f1_b, hy_f2_w, hy_f2_b, hy_f3_w, hy_f3_b, hy_f4_w, hy_sin_freq, hy_skip,
              q_norm_g, k_norm_g, na_rpb, w_hy_out, w_na_out, w_out, peer_w_q, peer_keys, peer_u, peer_v):
    for layer in range(DEPTH_2):
        p = {
            'norm1_g': norm1_g[layer], 'norm2_g': norm2_g[layer],
            'w_ada': w_ada[layer], 'b_ada': b_ada[layer],
            'w_in': w_in[layer], 'b_in': b_in[layer],
            'hy_conv_w': hy_conv_w[layer], 'hy_conv_b': hy_conv_b[layer],
            'hy_f1_w': hy_f1_w[layer], 'hy_f1_b': hy_f1_b[layer],
            'hy_f2_w': hy_f2_w[layer], 'hy_f2_b': hy_f2_b[layer],
            'hy_f3_w': hy_f3_w[layer], 'hy_f3_b': hy_f3_b[layer],
            'hy_f4_w': hy_f4_w[layer], 'hy_sin_freq': hy_sin_freq[layer], 'hy_skip': hy_skip[layer],
            'q_norm_g': q_norm_g[layer], 'k_norm_g': k_norm_g[layer], 'na_rpb': na_rpb[layer],
            'w_hy_out': w_hy_out[layer], 'w_na_out': w_na_out[layer], 'w_out': w_out[layer],
            'peer_w_q': peer_w_q[layer], 'peer_keys': peer_keys[layer],
            'peer_u': peer_u[layer], 'peer_v': peer_v[layer],
        }
        m_lat = adaln(c, p)
        m_ctx = adaln(c_ctx, p)
        sh1, sc1, g1, sh2, sc2, g2 = [m_lat[:, i:i + 1] for i in range(N_MOD)]
        ch1, cs1, cg1, ch2, cs2, cg2 = [m_ctx[i:i + 1] for i in range(N_MOD)]

        h_ctx = modulate(ctx, p['norm1_g'], ch1, cs1)
        k_ctx, v_ctx = context_kv(h_ctx, p)

        def attend_latent(q, k, v, k_ctx=k_ctx, v_ctx=v_ctx, rpb=p['na_rpb']):
            return neighbourhood_attention(axial_rope(q), axial_rope(k), v, k_ctx, v_ctx, rpb)

        h = modulate(x, p['norm1_g'], sh1, sc1)
        x_next = x + g1 * token_mixer(h, p, attend_latent)
        x_next = x_next + g2 * peer(modulate(x_next, p['norm2_g'], sh2, sc2), p)

        if layer + 1 < DEPTH_2:
            ctx_next = ctx + cg1 * token_mixer(h_ctx, p, context_attention)
            ctx = ctx_next + cg2 * peer(modulate(ctx_next, p['norm2_g'], ch2, cs2), p)
        x = x_next
    return x


def setup_inputs(seed=0):
    out = dict(first_inputs(seed))
    for name, value in second_inputs(seed + 1).items():
        if name != "x":
            out[name + "_2"] = value
    return out


def reference(
    x, c, ada_w, ada_b, norm1_w, w_in, gla_a_w, gla_a_b, gla_norm_w, conv_w, conv_b, dt_bias,
    a_log, d_skip, ssd_norm_w, w_out, norm2_w, ffn_w_gate, ffn_w_up, ffn_w_down, router_w,
    moe_w_gate, moe_w_up, moe_w_down, final_norm_w, c_2, ctx_2, c_ctx_2, norm1_g_2, norm2_g_2,
    w_ada_2, b_ada_2, w_in_2, b_in_2, hy_conv_w_2, hy_conv_b_2, hy_f1_w_2, hy_f1_b_2, hy_f2_w_2,
    hy_f2_b_2, hy_f3_w_2, hy_f3_b_2, hy_f4_w_2, hy_sin_freq_2, hy_skip_2, q_norm_g_2,
    k_norm_g_2, na_rpb_2, w_hy_out_2, w_na_out_2, w_out_2, peer_w_q_2, peer_keys_2, peer_u_2,
    peer_v_2,
):
    x = first_block(
        x, c, ada_w, ada_b, norm1_w, w_in, gla_a_w, gla_a_b, gla_norm_w, conv_w, conv_b,
        dt_bias, a_log, d_skip, ssd_norm_w, w_out, norm2_w, ffn_w_gate, ffn_w_up, ffn_w_down,
        router_w, moe_w_gate, moe_w_up, moe_w_down, final_norm_w,
    )
    return second_block(
        x, c_2, ctx_2, c_ctx_2, norm1_g_2, norm2_g_2, w_ada_2, b_ada_2, w_in_2, b_in_2,
        hy_conv_w_2, hy_conv_b_2, hy_f1_w_2, hy_f1_b_2, hy_f2_w_2, hy_f2_b_2, hy_f3_w_2,
        hy_f3_b_2, hy_f4_w_2, hy_sin_freq_2, hy_skip_2, q_norm_g_2, k_norm_g_2, na_rpb_2,
        w_hy_out_2, w_na_out_2, w_out_2, peer_w_q_2, peer_keys_2, peer_u_2, peer_v_2,
    )


_drawn_inputs = setup_inputs


def setup_inputs(seed=0):
    import zlib

    import numpy as np

    out = dict(_drawn_inputs(seed))
    spreads = {}
    factors = {'gla_norm_w': 3.875,
     'conv_b': 3.036,
     'ssd_norm_w': 3.441,
     'norm1_g_2': 3.35,
     'b_in_2': 2.815,
     'hy_conv_b_2': 3.485,
     'hy_f1_b_2': 4.127,
     'hy_f2_b_2': 3.364,
     'hy_f3_b_2': 3.024,
     'hy_sin_freq_2': 6.095,
     'q_norm_g_2': 8.0,
     'k_norm_g_2': 22.097,
     'na_rpb_2': 64.0,
     'norm2_g_2': 8.0,
     'peer_u_2': 2.783}
    for name, (base, spread) in spreads.items():
        noise = np.random.default_rng([zlib.crc32(name.encode()), seed]).standard_normal(out[name].shape)
        drawn = base * np.exp(spread * noise) if base else spread * noise
        out[name] = jnp.asarray(drawn.astype(out[name].dtype))
    for name, factor in factors.items():
        out[name] = (out[name] * factor).astype(out[name].dtype)
    return out
```

```python
import math
from contextlib import ExitStack

import numpy as np

import concourse.bass as bass
from concourse import mybir

ALU = mybir.AluOpType
ACT = mybir.ActivationFunctionType
AX = mybir.AxisListType
F32 = mybir.dt.float32
U32 = mybir.dt.uint32

D = 1024
L = 256
EPS = 1e-6
SLOT = 4224
NSLOT = 5
ARENA = 23200
BIG = -3.0e38
STOP = None


def layout(items):
    at, out = 0, {}
    for name, n in items:
        out[name] = (at, n)
        at += n
    return out, at


PV, NPV = layout(
    [(f"{n}{l}", w) for l in range(2) for n, w in (
        ("ada_b", 48), ("norm1_w", 8), ("norm2_w", 8), ("gla_a_b", 2), ("gla_norm_w", 1),
        ("conv_w", 24), ("conv_b", 6), ("dt_bias", 1), ("a_log", 1), ("d_skip", 4), ("ssd_norm_w", 4),
        ("gla_a_w", 256))]
    + [("c", 8), ("c2", 16), ("final_w", 8), ("norm1_g", 8), ("norm2_g", 8), ("b_ada", 48), ("b_in", 40),
       ("hcw", 36), ("hcb", 12), ("f1b", 1), ("f2b", 1), ("f3b", 1), ("freq", 1), ("skip", 8),
       ("qg", 1), ("kg", 1), ("router", 64), ("f1w", 64), ("f2w", 64), ("f3w", 64), ("bv", 512)])
CS, NCS = layout([("ident", 128), ("ones", 128), ("bones", 128), ("perm", 128), ("sel", 1024),
                  ("iota", 128), ("iota16", 16), ("scan64", 256), ("scan128", 256), ("iota8", 8)])
MS, NMS = layout([("gla", 128), ("ssd", 128), ("col", 256)])
HC, NHC = layout([("C", 512), ("S", 512), ("CI", 512), ("SI", 512), ("dec", 1024), ("ropeC", 256),
                  ("ropeS", 256), ("feats", 256)])


class Eng:

    def __init__(self, e, sem, chained):
        self.e, self.sem, self.n, self.chained, self.seen = e, sem, 0, chained, {}

    def wait(self, toks):
        for t in toks:
            if t is None:
                continue
            sem, v = t
            if self.seen.get(id(sem), 0) < v:
                self.e.wait_ge(sem, v)
                self.seen[id(sem)] = v

    def __call__(self, fn, *args, w=(), inc=True, **kw):
        self.wait(w)
        if self.chained and self.n:
            self.wait([(self.sem, self.n)])
        ins = fn(*args, **kw)
        if not inc:
            return None
        self.n += 1
        ins.then_inc(self.sem, 1)
        return (self.sem, self.n)

    @property
    def last(self):
        return (self.sem, self.n) if self.n else None


class Banks:

    def __init__(self, banks):
        self.banks, self.free, self.at = banks, [[] for _ in banks], 0

    def get(self, among=None):
        if among is None:
            i = self.at % len(self.banks)
        else:
            i = among[self.at % len(among)]
        self.at += 1
        w, self.free[i] = self.free[i], []
        return self.banks[i], w, self.free[i]


class Ring:

    def __init__(self, eng, buf, sems):
        self.eng, self.buf, self.sems, self.n = eng, buf, sems, 0
        self.users = [[] for _ in sems]

    def load(self, parts):
        s = self.n % len(self.sems)
        self.n += 1
        self.eng.wait(self.users[s])
        self.users[s] = []
        base = self.buf[:, s * SLOT:(s + 1) * SLOT]
        for view, src in parts(base):
            self.eng.e.dma_start(view, src).then_inc(self.sems[s][0], 16)
            self.sems[s][1] += 16
        return base, (self.sems[s][0], self.sems[s][1]), self.users[s]


def program(nc, T):
    with ExitStack() as ctx:
        def sb(name, n, dt=F32):
            return ctx.enter_context(nc.sbuf_tensor(name, [128, n], dt))[:, :]

        def sem(name):
            return ctx.enter_context(nc.semaphore(name))

        te, ve, se, ge = nc.tensor, nc.vector, nc.scalar, nc.gpsimd
        P = Eng(te, sem("s_pe"), False)
        V = Eng(ve, sem("s_dve"), True)
        A = Eng(se, sem("s_act"), True)
        G = Eng(ge, sem("s_pool"), True)
        SP = Eng(nc.sync, sem("s_sp"), False)
        s_in = sem("s_in")
        s_out = sem("s_out")

        pv = sb("pv", NPV)
        cs = sb("cs", NCS)
        ms = sb("ms", NMS, U32)
        xT = sb("xT", 2048).rearrange("p (k t) -> p k t", k=8)
        hT = sb("hT", 2048).rearrange("p (k t) -> p k t", k=8)
        mods = sb("mods", 4 * 48)
        small = sb("small", 128)
        ringbuf = sb("ring", NSLOT * SLOT)
        arena = sb("arena", ARENA)
        hc = arena[:, ARENA - NHC:ARENA]
        ring = Ring(SP, ringbuf, [[sem(f"s_ring{i}"), 0] for i in range(NSLOT)])
        banks = Banks([ctx.enter_context(nc.psum_tensor(f"ps{i}", [128, 512], F32))[:, :] for i in range(8)])

        def pvc(name, i=0, n=1, rows=128):
            o = PV[name][0] + i
            return pv[0:rows, o:o + n]

        def cst(name, rows=128, cols=None):
            o, n = CS[name]
            return cs[0:rows, o:o + (cols or n)]

        def hcc(name, rows=128):
            o, n = HC[name]
            return hc[0:rows, o:o + n]

        class Arena:
            at = 0

        limit = [ARENA - NHC]

        def buf(n):
            a = Arena.at
            Arena.at += n
            assert Arena.at <= limit[0], (Arena.at, limit[0])
            return arena[:, a:a + n]

        def everyone():
            toks = [x.last for x in (P, V, A, G)]
            for x in (P, V, A, G):
                x.wait([t for t in toks if t and t[0] is not x.sem])
            V.wait([V.last])
            A.wait([A.last])

        def fresh():
            everyone()
            Arena.at = 0

        ident, ones, bones = cst("ident"), cst("ones"), cst("bones")

        loads = [(pv, T["pv"]), (cs, T["cs"]), (ms, T["ms"]),
                 (xT, T["xT"].rearrange("(k p) t -> p k t", p=128)), (hc, T["hc"])]
        for dst, src in loads:
            se.dma_start(dst, src).then_inc(s_in, 16)
        t_in = (s_in, 16 * len(loads))
        for x in (P, V, A, G):
            x.wait([t_in])

        def wtile(w, c0, n):
            def parts(base):
                v = base[:, 0:8 * n].rearrange("p (k n) -> p k n", k=8)
                return [(v, w[:, c0:c0 + n].rearrange("(k p) n -> p k n", p=128))]
            base, tok, users = ring.load(parts)
            return base[:, 0:8 * n].rearrange("p (k n) -> p k n", k=8), tok, users

        def rtile(w, r0, n, cols):
            def parts(base):
                v = base[:, 0:n * cols].rearrange("p (k n) -> p k n", k=n)
                return [(v, w[r0:r0 + 128 * n, :].rearrange("(k p) n -> p k n", p=128))]
            base, tok, users = ring.load(parts)
            return base[:, 0:n * cols].rearrange("p (k n) -> p k n", k=n), tok, users

        def accum(out, pairs, w=(), inc=True):
            tok = None
            for i, (a, b) in enumerate(pairs):
                tok = P(te.matmul, out, a, b, start=(i == 0), stop=(i == len(pairs) - 1),
                        w=w, inc=(inc and i == len(pairs) - 1))
            return tok

        def transposes(ins, w=()):
            b, fw, users = banks.get()
            tok = None
            at = 0
            for i, x in enumerate(ins):
                k, m = x.shape
                tok = P(te.transpose, b[0:m, at:at + k], x, ident[0:k, 0:k], w=[*w, *fw],
                        inc=(i == len(ins) - 1))
                at += k
            return b, tok, users

        def ada(w, b_name, cname, ncond, out, t_s):
            sv = small[:, 0:8 * ncond]
            b, fw, users = banks.get()
            ps = b[:, 0:48 * ncond].rearrange("p (m c) -> p m c", c=ncond)
            for n in range(12):
                tile, tt, tu = wtile(w, 512 * n, 512)
                for m in range(4):
                    tok = accum(ps[:, 4 * n + m, :],
                                [(tile[:, k, 128 * m:128 * m + 128], sv[:, ncond * k:ncond * k + ncond])
                                 for k in range(8)], w=[tt, t_s, *fw])
                tu.append(tok)
            for c in range(ncond):
                t = V(ve.tensor_tensor, out[:, c, :], ps[:, :, c], pvc(b_name, 0, 48), ALU.add, w=[tok])
            users.append(t)
            return t

        def silu_c(name, n, w=()):
            return A(se.activation, small[:, 0:n], pvc(name, 0, n), ACT.Silu, w=w)

        def rstd_of(ps, scale, n, out, tok):
            t0 = V(ve.tensor_scalar, out, ps, scale, EPS, ALU.mult, ALU.add, w=[tok])
            t1 = V(ve.reciprocal, out, out)
            return A(se.activation, out, out, ACT.Sqrt, w=[t1]), t0

        def norm_mod(src, g, sc, sh, dst, t_src, scratch, ncols=8):
            sq, r, gs = scratch[:, 0:2048].rearrange("p (k t) -> p k t", k=8), scratch[:, 2048:2304], \
                scratch[:, 2304:2312]
            t = A(se.activation, sq, src, ACT.Square, w=t_src)
            b, fw, users = banks.get()
            tok = accum(b[:, 0:256], [(ones, sq[:, k, :]) for k in range(8)], w=[t, *fw])
            tr, t0 = rstd_of(b[:, 0:256], 1.0 / D, 256, r, tok)
            users.append(t0)
            if sc is not None:
                V(ve.scalar_tensor_tensor, gs, sc, 1.0, g, ALU.add, ALU.mult, w=[tr])
            else:
                V(ve.tensor_copy, gs, g, w=[tr])
            t = None
            for k in range(8):
                t = V(ve.scalar_tensor_tensor, dst[:, k, :], src[:, k, :], gs[:, k:k + 1], r, ALU.mult, ALU.mult)
                if sc is not None:
                    t = A(se.activation, dst[:, k, :], dst[:, k, :], ACT.Identity, bias=sh[:, k:k + 1], w=[t])
            return t

        def proj(tile, tt, tu, c0, nch, rhs, w, take):
            tok = None
            for m0 in range(0, nch, 2):
                n = min(2, nch - m0)
                b, fw, users = banks.get()
                for j in range(n):
                    c = c0 + 128 * (m0 + j)
                    tok = accum(b[:, 256 * j:256 * j + 256],
                                [(tile[:, k, c:c + 128], rhs[:, k, :]) for k in range(8)], w=[tt, *w, *fw],
                                inc=(j == n - 1))
                users.append(take(b[:, 0:256 * n].rearrange("p (m t) -> p m t", m=n), m0, n, tok))
            tu.append(tok)
            return tok

        def proj_tm(tile, tt, tu, rhs, w, take, bias=None):
            for t in range(2):
                b, fw, users = banks.get()
                pairs = [(rhs[:, k, 128 * t:128 * t + 128], tile[:, k, 0:512]) for k in range(8)]
                if bias is not None:
                    pairs.append((ones[0:1, :], bias))
                tok = accum(b, pairs, w=[tt, *w, *fw])
                users.append(take(b, t, tok))
            tu.append(tok)

        def copy_to(dst, eng="A"):
            def take(b, m0, n, tok):
                if eng == "A":
                    return A(se.activation, dst[:, m0:m0 + n, :], b, ACT.Copy, w=[tok])
                return V(ve.tensor_copy, dst[:, m0:m0 + n, :], b, w=[tok])
            return take

        def residual(tile_c0, gate, n0):
            def take(b, m0, n, tok):
                for j in range(n):
                    m = n0 + m0 + j
                    t = V(ve.scalar_tensor_tensor, xT[:, m, :], b[:, j, :], gate[:, m:m + 1], xT[:, m, :],
                          ALU.mult, ALU.add, w=[tok])
                return t
            return take

        def log1pexp_neg_abs(x, tmp, w):
            t = A(se.activation, tmp, x, ACT.Abs, w=[V.last, *w])
            t = A(se.activation, tmp, tmp, ACT.Exp, scale=-1.0, w=[t])
            t = V(ve.tensor_scalar, tmp, tmp, 1.0, None, ALU.add, w=[t])
            return A(se.activation, tmp, tmp, ACT.Ln, w=[t])

        def mixer(l, mod):
            w_in, w_out = T["w_in"][l], T["w_out"][l]
            v4 = lambda x, k: x.rearrange("p (k t) -> p k t", k=k)
            zT = v4(buf(1024), 4)
            merged = v4(buf(2048), 8)
            xbc = buf(6 * 259).rearrange("p (k t) -> p k t", k=6)
            dts = buf(256)
            kept = Arena.at
            qT, kT, gT = (v4(buf(n * 256), n) for n in (2, 2, 4))
            v_tm = v4(buf(1024), 2)
            alr = buf(256)
            qe = v4(buf(512), 2)
            kep = v4(buf(1024), 4)
            la = v4(buf(512), 2)
            lt = v4(buf(512), 2)
            ktail = v4(buf(512), 2)
            ktp = v4(buf(1024), 4)
            spad = buf(4 * 3 * 128).rearrange("p (h n v) -> p h n v", h=4, n=3)
            attm = buf(1024).rearrange("p (h t i) -> p h t i", h=4, t=2)
            bl = buf(8).rearrange("p (c n) -> p c n", c=2)
            ebl = buf(8).rearrange("p (c n) -> p c n", c=2)

            for z in (kep, ktp, spad, attm, xbc[:, :, 0:3]):
                tz = G(ge.memset, z, 0.0)

            th = norm_mod(xT, pvc(f"norm1_w{l}", 0, 8), mod[:, 8:16], mod[:, 0:8], hT, [V.last, A.last],
                          arena[:, limit[0] - 2312:limit[0]])
            hw = [th]

            tile, tt, tu = wtile(w_in, 0, 512)

            def take_qk(b, m0, n, tok):
                if m0 == 0:
                    return A(se.activation, qT, b, ACT.Copy, scale=0.125, w=[tok])
                return A(se.activation, kT, b, ACT.Copy, w=[tok])
            proj(tile, tt, tu, 0, 4, hT, hw, take_qk)
            tile, tt, tu = wtile(w_in, 512, 512)
            proj_tm(tile, tt, tu, hT, hw, lambda b, t, tok: V(ve.tensor_copy, v_tm[:, t, :], b, w=[tok]))
            tile, tt, tu = wtile(w_in, 1024, 512)
            proj(tile, tt, tu, 0, 4, hT, hw,
                 lambda b, m0, n, tok: A(se.activation, gT[:, m0:m0 + n, :], b, ACT.Silu, w=[tok]))
            tile, tt, tu = wtile(w_in, 1536, 528)
            b, fw, users = banks.get()
            tok = accum(b[0:16, 0:256], [(tile[:, k, 0:16], hT[:, k, :]) for k in range(8)], w=[tt, *fw])
            t_alr = V(ve.tensor_copy, alr[0:16, :], b[0:16, 0:256], w=[tok])
            users.append(t_alr)
            proj(tile, tt, tu, 16, 4, hT, hw,
                 lambda b, m0, n, tok: A(se.activation, zT[:, m0:m0 + n, :], b, ACT.Silu, w=[tok]))
            xin = xbc[:, :, 3:259]
            tile, tt, tu = wtile(w_in, 2064, 512)
            proj(tile, tt, tu, 0, 4, hT, hw, copy_to(xin, "V"))
            tile, tt, tu = wtile(w_in, 2576, 264)
            b, fw, users = banks.get()
            tok = accum(b[0:8, 0:256], [(tile[:, k, 256:264], hT[:, k, :]) for k in range(8)], w=[tt, *fw])
            t_dt = V(ve.tensor_scalar, dts[0:8, :], b[0:8, 0:256], pvc(f"dt_bias{l}", rows=8), None, ALU.add,
                     w=[tok])
            users.append(t_dt)
            proj(tile, tt, tu, 0, 2, hT, hw, copy_to(xin[:, 4:6, :], "V"))

            b, fw, users = banks.get()
            for c in range(2):
                tok = P(te.matmul, b[:, 256 * c:256 * c + 256], pvc(f"gla_a_w{l}", 128 * c, 128, rows=16),
                        alr[0:16, :], start=True, stop=True, w=[t_alr, *fw])
            for c in range(2):
                t = V(ve.tensor_scalar, la[:, c, :], b[:, 256 * c:256 * c + 256], pvc(f"gla_a_b{l}", c), None,
                      ALU.add, w=[tok])
            users.append(t)
            t = log1pexp_neg_abs(la, lt, [t])
            V(ve.scalar_tensor_tensor, lt, la, 0.0, lt, ALU.min, ALU.subtract, w=[t])
            for c in range(2):
                t = V(ve.tensor_tensor_scan, la[:, c, :], cst("scan64"), lt[:, c, :], 0.0, ALU.mult, ALU.add)
            t = A(se.activation, lt, la, ACT.Exp, scale=1.0 / 16, w=[t])
            tq = V(ve.tensor_tensor, qe, qT, lt, ALU.mult, w=[t])
            t = A(se.activation, lt, la, ACT.Exp, scale=-1.0 / 16, w=[tq])
            for h in range(4):
                r = slice(64 * (h % 2), 64 * (h % 2) + 64)
                tk = V(ve.tensor_tensor, kep[r, h, :], kT[r, h // 2, :], lt[r, h // 2, :], ALU.mult, w=[t, tz])
            t = V(ve.tensor_scalar, bl, la[:, :, 63:256:64], 1.0 / 16, None, ALU.mult)
            A(se.activation, ebl, bl, ACT.Exp, w=[t])
            for c in range(2):
                for n in range(4):
                    t = A(se.activation, ktail[:, c, 64 * n:64 * n + 64], la[:, c, 64 * n:64 * n + 64], ACT.Exp,
                          bias=bl[:, c, n:n + 1], scale=-1.0 / 16)
            t = V(ve.tensor_tensor, ktail, ktail, kT, ALU.mult, w=[t])
            for o in range(2):
                b, fw, users = banks.get()
                for c in range(2):
                    for tt_ in range(2):
                        s = slice(128 * tt_, 128 * tt_ + 128)
                        at = 128 * (2 * c + tt_)
                        tok = P(te.matmul, b[:, at:at + 128], kep[:, 2 * c + o, s], qe[:, c, s],
                                start=True, stop=True, w=[tk, tq, *fw])
                for c in range(2):
                    for tt_ in range(2):
                        at = 128 * (2 * c + tt_)
                        ta = V(ve.copy_predicated, attm[:, 2 * c + o, tt_, :],
                               ms[:, MS["gla"][0]:MS["gla"][0] + 128], b[:, at:at + 128], w=[tok, tz])
                users.append(ta)
            b, tok, users = transposes([ktail[:, c, 128 * s:128 * s + 128] for s in range(2) for c in range(2)],
                                       w=[t])
            for n in range(4):
                r = slice(64 * (n % 2), 64 * (n % 2) + 64)
                tkt = V(ve.tensor_copy, ktp[r, n, :], b[r, 256 * (n // 2):256 * (n // 2) + 256], w=[tok, tz])
            users.append(tkt)
            for n in range(3):
                b, fw, users = banks.get()
                for c in range(2):
                    tok = P(te.matmul, b[:, 256 * c:256 * c + 256], ktp[:, n, 128 * c:128 * c + 128],
                            v_tm[:, n // 2, 256 * c:256 * c + 256], start=True, stop=True, w=[tkt, *fw])
                for h in range(4):
                    r = slice(64 * (h % 2), 64 * (h % 2) + 64)
                    src = b[r, 256 * (h // 2) + 128 * (h % 2):256 * (h // 2) + 128 * (h % 2) + 128]
                    if n == 0:
                        ts = V(ve.tensor_copy, spad[r, h, 0, :], src, w=[tok])
                    else:
                        ts = V(ve.scalar_tensor_tensor, spad[r, h, n, :], spad[r, h, n - 1, :],
                               ebl[r, h // 2, n:n + 1], src, ALU.mult, ALU.add, w=[tok, A.last])
                users.append(ts)
            oT = v4(buf(1024), 4)
            for h in range(4):
                b, fw, users = banks.get()
                for t in range(2):
                    s = slice(128 * t, 128 * t + 128)
                    P(te.matmul, b[:, s], v_tm[:, t, 128 * h:128 * h + 128], attm[:, h, t, :],
                      start=True, stop=False, w=[ta, ts, *fw], inc=False)
                    for n in range(max(1, 2 * t), 2 * t + 2):
                        tok = P(te.matmul, b[:, 64 * n:64 * n + 64], spad[:, h, n - 1, :],
                                qe[:, h // 2, 64 * n:64 * n + 64], start=False, stop=(n == 2 * t + 1))
                to = V(ve.tensor_copy, oT[:, h, :], b[:, 0:256], w=[tok])
                users.append(to)
            sq = v4(buf(1024), 4)
            rr = v4(buf(1024), 4)
            t = A(se.activation, sq, oT, ACT.Square, w=[to])
            for p in range(2):
                b, fw, users = banks.get()
                tok = accum(b, [(ones, sq[:, 2 * p:2 * p + 2, :])], w=[t, *fw])
                tr, t0 = rstd_of(b.rearrange("p (k t) -> p k t", k=2), 1.0 / 128, 0, rr[:, 2 * p:2 * p + 2, :], tok)
                users.append(t0)
            V(ve.scalar_tensor_tensor, oT, oT, pvc(f"gla_norm_w{l}"), rr, ALU.mult, ALU.mult, w=[tr])
            V(ve.tensor_tensor, merged[:, 0:4, :], oT, gT, ALU.mult)

            everyone()
            Arena.at = kept
            xc = v4(buf(1536), 6)
            for k in range(6):
                V(ve.tensor_scalar, xc[:, k, :], xbc[:, k, 0:256], pvc(f"conv_w{l}", k), pvc(f"conv_b{l}", k),
                  ALU.mult, ALU.add)
                for j in range(1, 4):
                    t = V(ve.scalar_tensor_tensor, xc[:, k, :], xbc[:, k, j:j + 256],
                          pvc(f"conv_w{l}", 6 * j + k), xc[:, k, :], ALU.mult, ALU.add)
            tx = A(se.activation, xc, xc, ACT.Silu, w=[t])
            sp = buf(256)
            cum = buf(256)
            av = buf(1)
            t = log1pexp_neg_abs(dts[0:8, :], sp[0:8, :], [])
            V(ve.scalar_tensor_tensor, dts[0:8, :], dts[0:8, :], 0.0, sp[0:8, :], ALU.max, ALU.add, w=[t])
            t = A(se.activation, av[0:8, :], pvc(f"a_log{l}", rows=8), ACT.Exp)
            V(ve.tensor_scalar, sp[0:8, :], dts[0:8, :], av[0:8, :], -1.0, ALU.mult, ALU.mult, w=[t])
            tc = V(ve.tensor_tensor_scan, cum[0:8, :], cst("scan128", rows=8), sp[0:8, :], 0.0,
                   ALU.mult, ALU.add)
            dc = buf(32).rearrange("p (t c) -> p t c", t=2)
            b, tok, users = transposes([x[0:8, 128 * t:128 * t + 128] for t in range(2) for x in (dts, cum)],
                                       w=[tc])
            users.append(V(ve.tensor_copy, dc, b[:, 0:32].rearrange("p (t c) -> p t c", t=2), w=[tok]))
            xdt = buf(1024).rearrange("p (t h q) -> p t h q", t=2, h=8)
            btm = buf(128)
            for t in range(2):
                b, tok, users = transposes([xc[:, k, 128 * t:128 * t + 128] for k in range(4)], w=[tx])
                users.append(V(ve.tensor_tensor, xdt[:, t], b.rearrange("p (h q) -> p h q", h=8),
                               dc[:, t, 0:8].unsqueeze(2).to_broadcast([128, 8, 64]), ALU.mult, w=[tok]))
            b, tok, users = transposes([xc[:, 4, 0:128]])
            users.append(V(ve.tensor_copy, btm, b[:, 0:128], w=[tok]))
            dec = buf(2048).rearrange("p (h t i) -> p h t i", h=8, t=2)
            ecb = buf(1024).rearrange("p (h i) -> p h i", h=8)
            fl = buf(8)
            sel = cst("sel", rows=8)
            for p in range(4):
                b, fw, users = banks.get()
                for j in range(2):
                    h = 2 * p + j
                    tok = P(te.matmul, b[:, 256 * j:256 * j + 256], sel[:, 128 * h:128 * h + 128], cum[0:8, :],
                            start=True, stop=True, w=[tc, *fw])
                for j in range(2):
                    h = 2 * p + j
                    for t in range(2):
                        V(ve.tensor_scalar, dec[:, h, t, :], b[:, 256 * j + 128 * t:256 * j + 128 * t + 128],
                          dc[:, t, 8 + h:9 + h], 0.0, ALU.subtract, ALU.min, w=[tok])
                    tv = V(ve.tensor_tensor, fl[:, h:h + 1], b[:, 256 * j + 127:256 * j + 128],
                           dc[:, 0, 8 + h:9 + h], ALU.subtract)
                te_ = A(se.activation, ecb[:, 2 * p:2 * p + 2, :],
                        b.rearrange("p (j t i) -> p j t i", j=2, t=2)[:, :, 1, :], ACT.Exp, w=[tok, tv])
                users += [tv, te_]
            A(se.activation, dec, dec, ACT.Exp, w=[tv])
            tf = A(se.activation, fl, fl, ACT.Exp)
            wx = buf(512).rearrange("p (h q) -> p h q", h=8)
            twx = V(ve.tensor_tensor, wx, xdt[:, 0], fl.unsqueeze(2).to_broadcast([128, 8, 64]), ALU.mult, w=[tf])
            bpad = v4(buf(512), 2)
            gm = buf(512).rearrange("p (g t i) -> p g t i", g=2, t=2)
            s1 = buf(512).rearrange("p (h q) -> p h q", h=8)
            ce = buf(1024).rearrange("p (h i) -> p h i", h=8)
            for z in (bpad, gm, s1):
                tz = V(ve.memset, z, 0.0)
            for g in range(2):
                r = slice(64 * g, 64 * g + 64)
                tb = V(ve.tensor_copy, bpad[r, g, :], xc[r, 4, :])
            b, fw, users = banks.get()
            for g in range(2):
                for t in range(2):
                    s = slice(128 * t, 128 * t + 128)
                    at = 128 * (2 * g + t)
                    tok = P(te.matmul, b[:, at:at + 128], bpad[:, g, s], xc[:, 5, s], start=True, stop=True,
                            w=[tb, *fw])
            for g in range(2):
                for t in range(2):
                    at = 128 * (2 * g + t)
                    tv = V(ve.copy_predicated, gm[:, g, t, :], ms[:, MS["ssd"][0]:MS["ssd"][0] + 128],
                           b[:, at:at + 128], w=[tok])
            users.append(tv)
            for g in range(2):
                for t in range(2):
                    td = V(ve.tensor_tensor, dec[:, 4 * g:4 * g + 4, t, :], dec[:, 4 * g:4 * g + 4, t, :],
                           gm[:, g, t, :].unsqueeze(1).to_broadcast([128, 4, 128]), ALU.mult)
            b, fw, users = banks.get()
            tok = accum(b, [(btm, wx)], w=[twx, *fw])
            for g in range(2):
                r = slice(64 * g, 64 * g + 64)
                ts = V(ve.tensor_copy, s1[r, 4 * g:4 * g + 4, :],
                       b[r, 256 * g:256 * g + 256].rearrange("p (h q) -> p h q", h=4), w=[tok])
            users.append(ts)
            tce = V(ve.tensor_tensor, ce, ecb, xc[:, 5, 128:256].unsqueeze(1).to_broadcast([128, 8, 128]),
                    ALU.mult)
            yT = v4(buf(1024), 4)
            for c in range(4):
                b, fw, users = banks.get()
                for h in (2 * c, 2 * c + 1):
                    r = slice(64 * (h % 2), 64 * (h % 2) + 64)
                    P(te.matmul, b[r, 0:128], xdt[:, 0, h, :], dec[:, h, 0, :], start=True, stop=True,
                      w=[tce, *fw], inc=False)
                    P(te.matmul, b[r, 128:256], xdt[:, 1, h, :], dec[:, h, 1, :], start=True, stop=False,
                      inc=False)
                    tok = P(te.matmul, b[r, 128:256], s1[:, h, :], ce[:, h, :], start=False, stop=True)
                ty = V(ve.scalar_tensor_tensor, yT[:, c, :], xc[:, c, :], pvc(f"d_skip{l}", c), b[:, 0:256],
                       ALU.mult, ALU.add, w=[tok])
                users.append(ty)
            ty = V(ve.tensor_tensor, yT, yT, zT, ALU.mult)
            sq = v4(buf(1024), 4)
            rr = buf(256)
            t = A(se.activation, sq, yT, ACT.Square, w=[ty])
            b, fw, users = banks.get()
            tok = accum(b[:, 0:256], [(ones, sq[:, k, :]) for k in range(4)], w=[t, *fw])
            tr, t0 = rstd_of(b[:, 0:256], 1.0 / 512, 0, rr, tok)
            users.append(t0)
            for c in range(4):
                tm = V(ve.scalar_tensor_tensor, merged[:, 4 + c, :], yT[:, c, :], pvc(f"ssd_norm_w{l}", c), rr,
                       ALU.mult, ALU.mult, w=[tr])
            for n in range(2):
                tile, tt, tu = wtile(w_out, 512 * n, 512)
                proj(tile, tt, tu, 0, 4, merged, [tm], residual(0, mod[:, 16:24], 4 * n))

        def acc(m):
            return banks.banks[m // 2][:, 256 * (m % 2):256 * (m % 2) + 256]

        WORK = [4, 5, 6, 7]

        class Down:

            def __init__(self):
                self.first = True
                self.waits = [t for i in range(4) for t in banks.free[i]]
                for i in range(4):
                    banks.free[i] = []

            def add(self, tile, tt, tu, act, ta, last):
                tok = None
                for j in range(4):
                    for m in range(8):
                        tok = P(te.matmul, acc(m), tile[:, j, 128 * m:128 * m + 128], act[:, j, :],
                                start=(self.first and j == 0 and m % 2 == 0), stop=(last and j == 3),
                                skip_group_check=True, w=[tt, ta, *self.waits], inc=(j == 3 and m == 7))
                    self.waits = []
                self.first = False
                tu.append(tok)
                return tok

        def ffn_all(experts, gbc, gate):
            acts = [buf(1024).rearrange("p (k t) -> p k t", k=4) for _ in range(2)]
            sil = [buf(256) for _ in range(2)]
            down = Down()
            pend = None
            t_act_read = [None, None]
            th = [A.last, V.last]
            i = 0
            n = 7 * len(experts)
            for e, (wg, wu, wd) in enumerate(experts):
                for f in range(7):
                    gt, tg, ug = wtile(wg, 512 * f, 512)
                    ut, tu_, uu = wtile(wu, 512 * f, 512)
                    dt, td, ud = rtile(wd, 512 * f, 4, D)
                    a = acts[i % 2]
                    for j in range(4):
                        b, fw, users = banks.get(WORK)
                        c = slice(128 * j, 128 * j + 128)
                        tk1 = accum(b[:, 0:256], [(gt[:, k, c], hT[:, k, :]) for k in range(8)], w=[tg, *th, *fw])
                        tk2 = accum(b[:, 256:512], [(ut[:, k, c], hT[:, k, :]) for k in range(8)], w=[tu_])
                        s = sil[j % 2]
                        t = A(se.activation, s, b[:, 0:256], ACT.Silu, w=[tk2, V.last])
                        if gbc is not None:
                            t = V(ve.tensor_tensor, s, s, gbc[:, e, :], ALU.mult, w=[t])
                        ta = V(ve.tensor_tensor, a[:, j, :], s, b[:, 256:512], ALU.mult,
                               w=[t, tk2, t_act_read[i % 2]])
                        users.append(ta)
                    ug.append(tk1)
                    uu.append(tk2)
                    if pend is not None:
                        t_act_read[(i - 1) % 2] = down.add(*pend, last=False)
                    pend = (dt, td, ud, a, ta)
                    i += 1
            tok = down.add(*pend, last=True)
            for m in range(8):
                t = V(ve.scalar_tensor_tensor, xT[:, m, :], acc(m), gate[:, m:m + 1], xT[:, m, :],
                      ALU.mult, ALU.add, w=[tok])
            for i in range(4):
                banks.free[i].append(t)

        def router(l):
            rw = pvc("router", 0, 64).rearrange("p (k e) -> p k e", k=8)
            gbc = buf(2048).rearrange("p (e t) -> p e t", e=8)
            lg, e8, g8, oh = buf(16), buf(16), buf(16), buf(16)
            ix, fx, sm = buf(16).bitcast(U32), buf(16), buf(8)
            gT = buf(256)
            b, fw, users = banks.get()
            for t in range(2):
                tok = accum(b[:, 8 * t:8 * t + 8],
                            [(hT[:, k, 128 * t:128 * t + 128], rw[:, k, :]) for k in range(8)],
                            w=[A.last, V.last, *fw])
            users.append(V(ve.tensor_copy, lg, b[:, 0:16], w=[tok]))
            for t in range(2):
                s = slice(8 * t, 8 * t + 8)
                V(ve.max, e8[:, s], lg[:, s])
                V(ve.max_index, ix[:, s], e8[:, s], lg[:, s])
                V(ve.tensor_copy, fx[:, s], ix[:, s])
                tv = V(ve.tensor_tensor, sm[:, 4 * t:4 * t + 1], e8[:, 8 * t + 1:8 * t + 2], e8[:, 8 * t:8 * t + 1],
                       ALU.subtract)
                ta = A(se.activation, sm[:, 4 * t + 1:4 * t + 2], sm[:, 4 * t:4 * t + 1], ACT.Exp, w=[tv])
                V(ve.tensor_scalar, sm[:, 4 * t:4 * t + 1], sm[:, 4 * t + 1:4 * t + 2], 1.0, None, ALU.add, w=[ta])
                V(ve.reciprocal, sm[:, 4 * t + 2:4 * t + 3], sm[:, 4 * t:4 * t + 1])
                V(ve.tensor_tensor, sm[:, 4 * t + 3:4 * t + 4], sm[:, 4 * t + 1:4 * t + 2],
                  sm[:, 4 * t + 2:4 * t + 3], ALU.mult)
                V(ve.tensor_scalar, g8[:, s], cst("iota8"), fx[:, 8 * t:8 * t + 1], sm[:, 4 * t + 2:4 * t + 3],
                  ALU.is_equal, ALU.mult)
                V(ve.tensor_scalar, oh[:, s], cst("iota8"), fx[:, 8 * t + 1:8 * t + 2],
                  sm[:, 4 * t + 3:4 * t + 4], ALU.is_equal, ALU.mult)
                tg = V(ve.tensor_tensor, g8[:, s], g8[:, s], oh[:, s], ALU.add)
            b, tok, users = transposes([g8[:, 0:8], g8[:, 8:16]], w=[tg])
            tg = V(ve.tensor_copy, gT[0:8, :], b[0:8, 0:256], w=[tok])
            users.append(tg)
            sel = cst("sel", rows=8)
            for p in range(4):
                b, fw, users = banks.get()
                for j in range(2):
                    e = 2 * p + j
                    tok = P(te.matmul, b[:, 256 * j:256 * j + 256], sel[:, 128 * e:128 * e + 128], gT[0:8, :],
                            start=True, stop=True, w=[tg, *fw])
                users.append(V(ve.tensor_copy, gbc[:, 2 * p:2 * p + 2, :],
                               b.rearrange("p (e t) -> p e t", e=2), w=[tok]))
            return gbc

        def finish():
            everyone()
            SP.wait([x.last for x in (P, V, A, G)])
            nc.sync.dma_start(T["out"].rearrange("(k p) t -> p k t", p=128), xT).then_inc(s_out, 16)
            nc.sync.wait_ge(s_out, 16)

        for l in range(2):
            fresh()
            mod = mods[:, 48 * l:48 * l + 48]
            t = silu_c("c", 8)
            ada(T["ada_w"][l], f"ada_b{l}", "c", 1, mod.rearrange("p (c m) -> p c m", c=1), t)
            if STOP == f"ada{l}":
                return finish()
            mixer(l, mod)
            if STOP == f"mix{l}":
                return finish()
            fresh()
            scr = arena[:, limit[0] - 2312:limit[0]]
            norm_mod(xT, pvc(f"norm2_w{l}", 0, 8), mod[:, 32:40], mod[:, 24:32], hT, [V.last], scr)
            if l == 0:
                ffn_all([(T["ffn_w_gate"], T["ffn_w_up"], T["ffn_w_down"])], None, mod[:, 40:48])
            else:
                gbc = router(l)
                ffn_all([(T["moe_w_gate"][e], T["moe_w_up"][e], T["moe_w_down"][e]) for e in range(8)],
                        gbc, mod[:, 40:48])
            if STOP == f"ffn{l}":
                return finish()
        fresh()
        scr = arena[:, limit[0] - 2312:limit[0]]
        norm_mod(xT, pvc("final_w", 0, 8), None, None, xT, [V.last], scr)
        if STOP == "first":
            return finish()

        everyone()
        t = silu_c("c2", 16)
        m2 = mods[:, 96:192].rearrange("p (c m) -> p c m", c=2)
        ada(T["w_ada"], "b_ada", "c2", 2, m2, t)
        mod, modc = m2[:, 0, :], m2[:, 1, :]
        fresh()
        v4 = lambda x, k: x.rearrange("p (k t) -> p k t", k=k)
        ctxT = v4(buf(2048), 8)
        zh = buf(12 * 258).rearrange("p (k t) -> p k t", k=12)
        qn, kn, kc = v4(buf(1024), 4), v4(buf(1024), 4), v4(buf(1024), 4)
        gate = v4(buf(4096), 16)
        v_tm, vc_tm = v4(buf(1024), 2), v4(buf(1024), 2)
        SP.wait([x.last for x in (P, V, A, G)])
        s_ctx = sem("s_ctx")
        nc.sync.dma_start(ctxT, T["ctxT"].rearrange("(k p) t -> p k t", p=128)).then_inc(s_ctx, 16)
        scr = arena[:, limit[0] - 2312:limit[0]]
        norm_mod(ctxT, pvc("norm1_g", 0, 8), modc[:, 8:16], modc[:, 0:8], ctxT, [(s_ctx, 16)], scr)
        th = norm_mod(xT, pvc("norm1_g", 0, 8), mod[:, 8:16], mod[:, 0:8], hT, [V.last], scr)
        tz = G(ge.memset, zh[:, :, 0:1], 0.0, w=[V.last])
        tz = G(ge.memset, zh[:, :, 257:258], 0.0)
        w_in = T["w_in2"]

        def biased(dst, col, func=ACT.Identity):
            def take(b, m0, n, tok):
                for j in range(n):
                    t = A(se.activation, dst[:, m0 + j, :], b[:, j, :], func, bias=pvc("b_in", col + m0 + j),
                          w=[tok])
                return t
            return take

        for n in range(3):
            tile, tt, tu = wtile(w_in, 512 * n, 512)
            proj(tile, tt, tu, 0, 4, hT, [th], biased(zh[:, 4 * n:4 * n + 4, 1:257], 4 * n))
        tile, tt, tu = wtile(w_in, 1536, 512)
        proj(tile, tt, tu, 0, 4, hT, [th], biased(qn, 12))
        tile, tt, tu = wtile(w_in, 2048, 512)
        proj(tile, tt, tu, 0, 4, hT, [th], biased(kn, 16))
        proj(tile, tt, tu, 0, 4, ctxT, [th], biased(kc, 16))
        tile, tt, tu = wtile(w_in, 2560, 512)
        bv = pvc("bv", 0, 512, rows=1)
        proj_tm(tile, tt, tu, hT, [th], lambda b, t, tok: V(ve.tensor_copy, v_tm[:, t, :], b, w=[tok]), bv)
        proj_tm(tile, tt, tu, ctxT, [th], lambda b, t, tok: V(ve.tensor_copy, vc_tm[:, t, :], b, w=[tok]), bv)
        for n in range(4):
            tile, tt, tu = wtile(w_in, 3072 + 512 * n, 512)
            proj(tile, tt, tu, 0, 4, hT, [th], biased(gate[:, 4 * n:4 * n + 4, :], 24 + 4 * n, ACT.Sigmoid))
        if STOP == "proj2":
            return finish()

        everyone()
        base = Arena.at
        ctx_space = [0]

        def cbuf(n):
            a = ctx_space[0]
            ctx_space[0] += n
            assert ctx_space[0] <= 2048
            return arena[:, a:a + n]

        zc = v4(buf(12 * 256), 12)
        for k in range(12):
            V(ve.tensor_scalar, zc[:, k, :], zh[:, k, 0:256], pvc("hcw", k), pvc("hcb", k), ALU.mult, ALU.add,
              w=[tz, A.last])
            for j in range(1, 3):
                V(ve.scalar_tensor_tensor, zc[:, k, :], zh[:, k, j:j + 256], pvc("hcw", 12 * j + k), zc[:, k, :],
                  ALU.mult, ALU.add)
        zspace = [2048]
        everyone()

        def zbuf(n):
            a = zspace[0]
            zspace[0] += n
            assert zspace[0] <= 2048 + 12 * 258
            return arena[:, a:a + n]

        ha, hb = cbuf(256), cbuf(256)
        src, t = hcc("feats", rows=33), None
        for i, (wname, bname, rows) in enumerate((("f1w", "f1b", 33), ("f2w", "f2b", 64), ("f3w", "f3b", 64))):
            b, fw, users = banks.get()
            tok = accum(b[0:64, 0:256], [(pvc(wname, 0, 64, rows=rows), src)], w=[t, *fw])
            x, y = ha[0:64, :], hb[0:64, :]
            users.append(V(ve.tensor_scalar, x, b[0:64, 0:256], pvc(bname, rows=64), pvc("freq", rows=64),
                           ALU.add, ALU.mult, w=[tok]))
            V(ve.tensor_scalar, y, x, 1.0 / (2 * math.pi), 12582912.0, ALU.mult, ALU.add)
            V(ve.tensor_scalar, y, y, 12582912.0, None, ALU.subtract)
            p1, p2 = 6.28125, 0.0019350051879882812
            p3 = 2 * math.pi - p1 - p2
            for part in (p1, p2, p3):
                V(ve.scalar_tensor_tensor, x, y, -part, x, ALU.mult, ALU.add)
            V(ve.tensor_scalar, x, x, 3.1415925, -3.1415925, ALU.min, ALU.max)
            t = A(se.activation, x, x, ACT.Sin, w=[V.last])
            src = x
        tsin = t

        def f4parts(base_):
            return [(base_[0:64, 0:2048], T["f4w"])]
        f4, tf4, uf4 = ring.load(f4parts)
        dec_t = hcc("dec").rearrange("p (t c) -> p t c", t=2)
        y_tm = v4(cbuf(1024), 2)

        fb = [zbuf(512) for _ in range(4)]
        kre, kim = [buf(512), buf(512)], [buf(512), cbuf(512)]
        hflat = hT.rearrange("p k t -> p (k t)")
        yre, yim = v4(hflat[:, 0:1024], 2), v4(hflat[:, 1024:2048], 2)
        rn = zbuf(512)
        tmp = zbuf(512)
        DC, DS, DCI, DSI = (v4(hcc(n), 2) for n in ("C", "S", "CI", "SI"))

        for o in range(2):
            for dr in range(2):
                for t in range(2):
                    b, fw, users = banks.get()
                    c0 = 1024 * o + 512 * dr
                    tok = accum(b, [(ha[0:64, 128 * t:128 * t + 128], f4[0:64, c0:c0 + 512])],
                                w=[tf4, tsin, *fw])
                    tv = V(ve.tensor_tensor, fb[2 * dr + t], b, dec_t[:, t, :], ALU.mult, w=[tok])
                    users.append(tv)
            if o == 1:
                uf4.append(tok)
            b, fw, users = banks.get()
            for i in range(4):
                ab = A(se.activation, tmp, fb[i], ACT.Abs, w=[V.last, P.last])
                tok = P(te.matmul, b, ones, tmp, start=(i == 0), stop=(i == 3), w=[ab, *fw])
            users.append(V(ve.reciprocal, rn, b, w=[tok]))
            V(ve.memset, fb[2][0:1, :], 0.0)
            for t in range(2):
                V(ve.tensor_tensor, tmp, fb[t], fb[2 + t], ALU.add)
                V(ve.tensor_tensor, fb[2 + t], fb[2 + t], fb[t], ALU.subtract)
                tv = V(ve.tensor_copy, fb[t], tmp)
            for k in range(2):
                s = slice(128 * k, 128 * k + 128)
                for dst, mat, x in ((kre, DC, 0), (kim, DS, 2)):
                    b, fw, users = banks.get()
                    tok = accum(b, [(mat[:, t, s], fb[x + t]) for t in range(2)], w=[tv, *fw])
                    users.append(V(ve.tensor_tensor, dst[k], b, rn, ALU.mult, w=[tok]))
            sig = [zc[:, c, :] for c in range(4)]
            for t in range(2):
                b, tok, users = transposes([x[:, 128 * t:128 * t + 128] for x in sig], w=[V.last])
                ty = V(ve.tensor_copy, y_tm[:, t, :], b, w=[tok])
                users.append(ty)
            for k in range(2):
                s = slice(128 * k, 128 * k + 128)
                br, fw, ur = banks.get()
                tok = accum(br, [(DC[:, t, s], y_tm[:, t, :]) for t in range(2)], w=[ty, *fw])
                bi, fw, ui = banks.get()
                tok = accum(bi, [(DS[:, t, s], y_tm[:, t, :]) for t in range(2)], w=[ty, *fw])
                V(ve.tensor_tensor, yre[:, k, :], br, kre[k], ALU.mult, w=[tok])
                V(ve.tensor_tensor, tmp, bi, kim[k], ALU.mult)
                V(ve.tensor_tensor, yre[:, k, :], yre[:, k, :], tmp, ALU.add)
                V(ve.tensor_tensor, yim[:, k, :], br, kim[k], ALU.mult)
                tv = V(ve.tensor_tensor, tmp, bi, kre[k], ALU.mult)
                ur.append(tv)
                ui.append(tv)
                tv = V(ve.tensor_tensor, yim[:, k, :], yim[:, k, :], tmp, ALU.subtract)
            for c in range(4):
                s = slice(128 * c, 128 * c + 128)
                b, fw, users = banks.get()
                tok = accum(b[:, 0:256], [(yre[:, k, s], DCI[:, k, :]) for k in range(2)]
                            + [(yim[:, k, s], DSI[:, k, :]) for k in range(2)], w=[tv, *fw])
                users.append(V(ve.scalar_tensor_tensor, zc[:, c, :], zc[:, c, :], pvc("skip", 4 * o + c),
                               b[:, 0:256], ALU.mult, ALU.add, w=[tok]))
                V(ve.tensor_tensor, zc[:, c, :], zc[:, c, :], zc[:, 4 + 4 * o + c, :], ALU.mult)
        thy = V.last
        for n in range(2):
            def parts(base_, n=n):
                v = base_[:, 0:2048].rearrange("p (k n) -> p k n", k=4)
                return [(v, T["w_hy"][:, 512 * n:512 * n + 512].rearrange("(k p) n -> p k n", p=128))]
            base_, tt, tu = ring.load(parts)
            wt = base_[:, 0:2048].rearrange("p (k n) -> p k n", k=4)
            for m in range(4):
                b, fw, users = banks.get()
                tok = accum(b[:, 0:256], [(wt[:, k, 128 * m:128 * m + 128], zc[:, k, :]) for k in range(4)],
                            w=[tt, thy, *fw])
                g = gate[:, 4 * n + m, :]
                users.append(V(ve.tensor_tensor, g, g, b[:, 0:256], ALU.mult, w=[tok]))
            tu.append(tok)
        if STOP == "hyena":
            return finish()

        everyone()
        Arena.at = base
        limit[0] = ARENA - NHC
        kp = v4(buf(2048), 8)
        zspace[0] = 2048
        kcp = v4(cbuf_reset(ctx_space, arena), 8)
        sq, rr = v4(zbuf(1024), 4), v4(zbuf(1024), 4)
        G(ge.memset, kp, 0.0)
        tz = G(ge.memset, kcp, 0.0)
        for x, g in ((qn, "qg"), (kn, "kg"), (kc, "kg")):
            t = A(se.activation, sq, x, ACT.Square, w=[V.last, P.last])
            for p in range(2):
                b, fw, users = banks.get()
                tok = accum(b, [(bones, sq[:, 2 * p:2 * p + 2, :])], w=[t, *fw])
                tr, t0 = rstd_of(b.rearrange("p (k t) -> p k t", k=2), 1.0 / 64, 0, rr[:, 2 * p:2 * p + 2, :], tok)
                users.append(t0)
            tv = V(ve.scalar_tensor_tensor, x, x, pvc(g), rr, ALU.mult, ALU.mult, w=[tr])
            if x is not kc:
                rc, rs = hcc("ropeC"), hcc("ropeS")
                for p in range(2):
                    b, fw, users = banks.get()
                    xx = x[:, 2 * p:2 * p + 2, :]
                    tok = accum(b, [(cst("perm"), xx)], w=[tv, *fw])
                    tv2 = V(ve.tensor_tensor, rr[:, 2 * p:2 * p + 2, :], b.rearrange("p (k t) -> p k t", k=2),
                            rs.unsqueeze(1).to_broadcast([128, 2, 256]), ALU.mult, w=[tok])
                    users.append(tv2)
                    V(ve.tensor_tensor, xx, xx, rc.unsqueeze(1).to_broadcast([128, 2, 256]), ALU.mult)
                    tv = V(ve.tensor_tensor, xx, xx, rr[:, 2 * p:2 * p + 2, :], ALU.add)
        for h in range(8):
            r = slice(64 * (h % 2), 64 * (h % 2) + 64)
            V(ve.tensor_copy, kp[r, h, :], kn[r, h // 2, :], w=[tz])
            tkp = V(ve.tensor_copy, kcp[r, h, :], kc[r, h // 2, :])
        sc = [kn.rearrange("p k t -> p (k t)")[:, 0:512], kn.rearrange("p k t -> p (k t)")[:, 512:1024]]
        pt = [kc.rearrange("p k t -> p (k t)")[:, 0:512], kc.rearrange("p k t -> p (k t)")[:, 512:1024]]
        zspace[0] = 2048
        tmpb, st = zbuf(256), zbuf(8)
        yna = v4(zbuf(1024), 4)
        for s in sc:
            V(ve.memset, s[:, 0:256], -1.0e30)
        bias_b, tbias, ubias = ring.load(lambda base_: [(base_[:, 0:4096], T["bias"])])
        biasv = bias_b[:, 0:4096].rearrange("p (t h k) -> p t h k", t=2, h=8)
        mcol = ms[:, MS["col"][0]:MS["col"][0] + 256]
        its = [(h, t) for h in range(8) for t in range(2)]

        def scores(i):
            h, t = its[i]
            b, fw, users = banks.get()
            q = qn[:, h // 2, 128 * t:128 * t + 128]
            P(te.matmul, b[:, 0:256], q, kp[:, h, :], start=True, stop=True, w=[tkp, *fw], inc=False)
            tok = P(te.matmul, b[:, 256:512], q, kcp[:, h, :], start=True, stop=True)
            return b, tok, users

        cur = scores(0)
        yb = None
        t_pt = [None, None]
        t_s = [None, None]
        for i, (h, t) in enumerate(its):
            b, tok, users = cur
            s, p_ = sc[i % 2], pt[i % 2]
            V(ve.scalar_tensor_tensor, tmpb, b[:, 0:256], 0.125, biasv[:, t, h, :], ALU.mult, ALU.add,
              w=[tok, tbias, t_s[i % 2]])
            V(ve.copy_predicated, s[:, 0:256], mcol, tmpb)
            users.append(V(ve.tensor_scalar, s[:, 256:512], b[:, 256:512], 0.125, None, ALU.mult))
            tv = V(ve.tensor_reduce, st[:, 0:1], s, AX.X, ALU.max, negate=True)
            ta = A(se.activation, p_, s, ACT.Exp, bias=st[:, 0:1], accum_out=st[:, 1:2], w=[tv, t_pt[i % 2]])
            V(ve.reciprocal, st[:, 2:3], st[:, 1:2], w=[ta])
            tp = V(ve.tensor_scalar, p_, p_, st[:, 2:3], None, ALU.mult)
            if i + 1 < len(its):
                cur = scores(i + 1)
            bt, tok, ut = transposes([p_[:, 128 * k:128 * k + 128] for k in range(4)], w=[tp])
            ta = A(se.activation, p_, bt, ACT.Copy, w=[tok])
            ut.append(ta)
            if i % 4 == 0:
                yb, fwy, uy = banks.get()
            r = slice(64 * (h % 2), 64 * (h % 2) + 64)
            vs = [v_tm[:, 0, :], v_tm[:, 1, :], vc_tm[:, 0, :], vc_tm[:, 1, :]]
            for k in range(4):
                tok = P(te.matmul, yb[r, 128 * t:128 * t + 128], vs[k][:, 64 * h:64 * h + 64],
                        p_[:, 128 * k:128 * k + 128], start=(k == 0), stop=(k == 3), w=[ta, *fwy], inc=(k == 3))
            t_pt[i % 2] = tok
            if i % 4 == 3:
                tyn = V(ve.tensor_copy, yna[:, h // 2, :], yb[:, 0:256], w=[tok])
                uy.append(tyn)
        ubias.append(V.last)
        for n in range(2):
            def parts(base_, n=n):
                v = base_[:, 0:2048].rearrange("p (k n) -> p k n", k=4)
                return [(v, T["w_na"][:, 512 * n:512 * n + 512].rearrange("(k p) n -> p k n", p=128))]
            base_, tt, tu = ring.load(parts)
            wt = base_[:, 0:2048].rearrange("p (k n) -> p k n", k=4)
            for m in range(4):
                b, fw, users = banks.get()
                tok = accum(b[:, 0:256], [(wt[:, k, 128 * m:128 * m + 128], yna[:, k, :]) for k in range(4)],
                            w=[tt, tyn, *fw])
                g, g2 = gate[:, 4 * n + m, :], gate[:, 8 + 4 * n + m, :]
                users.append(V(ve.tensor_tensor, g2, g2, b[:, 0:256], ALU.mult, w=[tok]))
                tm = V(ve.tensor_tensor, g, g, g2, ALU.add)
            tu.append(tok)
        for n in range(2):
            tile, tt, tu = wtile(T["w_out2"], 512 * n, 512)
            proj(tile, tt, tu, 0, 4, gate, [tm], residual(0, mod[:, 16:24], 4 * n))
        if STOP == "mix2":
            return finish()

        fresh()
        limit[0] = ARENA
        scr = arena[:, limit[0] - 2312:limit[0]]
        th = norm_mod(xT, pvc("norm2_g", 0, 8), mod[:, 32:40], mod[:, 24:32], hT, [V.last], scr)
        wbuf = [buf(8192).rearrange("p (i t) -> p i t", i=32) for _ in range(2)]
        gTt, i0T, i1T = buf(256), buf(256), buf(256)
        mark = Arena.at
        qt = v4(arena[:, 0:4096], 16)
        work = [8192]

        def wb(n):
            a = work[0]
            work[0] += n
            assert work[0] <= 16384
            return arena[:, a:a + n]

        for n in range(4):
            tile, tt, tu = wtile(T["w_pq"], 512 * n, 512)
            proj(tile, tt, tu, 0, 4, hT, [th], copy_to(qt[:, 4 * n:4 * n + 4, :], "A"))
        tq = A.last
        keys, tkeys, ukeys = ring.load(lambda base_: [(base_[:, 0:2048], T["keysT"])])
        sbuf = wb(2048).rearrange("p (g n) -> p g n", g=16)
        cand = wb(2048).rearrange("p (h n) -> p h n", h=8)
        tv16 = wb(256).rearrange("p (g k) -> p g k", g=16)
        ti16 = wb(256).bitcast(U32).rearrange("p (g k) -> p g k", g=16)
        tif = wb(256).rearrange("p (g k) -> p g k", g=16)
        bs = wb(128).rearrange("p (h k) -> p h k", h=8)
        bp = wb(128).bitcast(U32).rearrange("p (h k) -> p h k", h=8)
        pa = wb(128).bitcast(U32).rearrange("p (h k) -> p h k", h=8)
        pf = wb(128).rearrange("p (h k) -> p h k", h=8)
        res = [wb(128) for _ in range(3)]
        sm = wb(16)
        eq = arena[:, 4096:6144].rearrange("p (h k a) -> p h k a", h=8, k=16)

        def top16(vals, out_v, out_i):
            V(ve.max, out_v[:, 0:8], vals)
            V(ve.max_index, out_i[:, 0:8], out_v[:, 0:8], vals)
            V(ve.match_replace, vals, out_v[:, 0:8], vals, BIG)
            V(ve.max, out_v[:, 8:16], vals)
            V(ve.max_index, out_i[:, 8:16], out_v[:, 8:16], vals)

        for t in range(2):
            for g4 in range(4):
                b, fw, users = banks.get()
                for j in range(4):
                    g = 4 * g4 + j
                    tok = P(te.matmul, b[:, 128 * j:128 * j + 128], qt[:, g, 128 * t:128 * t + 128],
                            keys[:, 128 * g:128 * g + 128], start=True, stop=True, w=[tq, tkeys, *fw])
                ts = A(se.activation, sbuf[:, 4 * g4:4 * g4 + 4, :], b.rearrange("p (g n) -> p g n", g=4), ACT.Copy,
                       w=[tok, V.last])
                users.append(ts)
            if t == 1:
                ukeys.append(tok)
            V.wait([ts])
            for g in range(16):
                top16(sbuf[:, g, :], tv16[:, g, :], ti16[:, g, :])
            V(ve.tensor_copy, tif, ti16)
            for h in range(8):
                V(ve.tensor_tensor, cand[:, h, :].rearrange("p (a b) -> p a b", a=16),
                  tv16[:, 2 * h, :].unsqueeze(2).to_broadcast([128, 16, 16]),
                  tv16[:, 2 * h + 1, :].unsqueeze(1).to_broadcast([128, 16, 16]), ALU.add)
                top16(cand[:, h, :], bs[:, h, :], bp[:, h, :])
            tr4 = tif.rearrange("p (h q) k -> p h q k", q=2)
            for q, (sv, op) in enumerate(((4, ALU.logical_shift_right), (15, ALU.bitwise_and))):
                V(ve.tensor_scalar, pa, bp, sv, None, op)
                V(ve.tensor_copy, pf, pa)
                for h in range(8):
                    V(ve.tensor_tensor, eq[:, h], pf[:, h, :].unsqueeze(2).to_broadcast([128, 16, 16]),
                      cst("iota16").unsqueeze(1).to_broadcast([128, 16, 16]), ALU.is_equal)
                    V(ve.tensor_tensor, eq[:, h], eq[:, h],
                      tr4[:, h, q, :].unsqueeze(1).to_broadcast([128, 16, 16]), ALU.mult)
                V(ve.tensor_reduce, res[q].rearrange("p (h k) -> p h k", h=8), eq, AX.X, ALU.add)
            g3 = res[2].rearrange("p (h k) -> p h k", h=8)
            tv = V(ve.tensor_tensor, g3, bs, bs[:, :, 0:1].to_broadcast([128, 8, 16]), ALU.subtract)
            ta = A(se.activation, g3, g3, ACT.Exp, w=[tv])
            V(ve.tensor_reduce, sm[:, 0:8], g3, AX.X, ALU.add, w=[ta])
            V(ve.reciprocal, sm[:, 8:16], sm[:, 0:8])
            tv = V(ve.tensor_tensor, g3, g3, sm[:, 8:16].unsqueeze(2).to_broadcast([128, 8, 16]), ALU.mult)
            b, tok, users = transposes(res, w=[tv])
            for n, dst in enumerate((i0T, i1T, gTt)):
                tv = V(ve.tensor_copy, dst[:, 128 * t:128 * t + 128], b[:, 128 * n:128 * n + 128], w=[tok])
            users.append(tv)
        if STOP == "topk":
            return finish()
        everyone()
        Arena.at = mark
        acts = [v4(buf(1024), 4) for _ in range(2)]
        oj = buf(2048).rearrange("p (t j) -> p t j", t=16)
        oi = buf(512).rearrange("p (t i) -> p t i", t=16)
        t_oh = [None]

        def build_w(qd, bt):
            t0 = 16 * bt
            i1 = i1T[:, t0:t0 + 16].unsqueeze(2)
            i0 = i0T[:, t0:t0 + 16].unsqueeze(2).to_broadcast([128, 16, 32])
            gg = gTt[:, t0:t0 + 16].unsqueeze(2).to_broadcast([128, 16, 32])
            V(ve.tensor_tensor, oj, i1.to_broadcast([128, 16, 128]),
              cst("iota").unsqueeze(1).to_broadcast([128, 16, 128]), ALU.is_equal, w=[t_oh[0]])
            V(ve.tensor_tensor, oi, i0,
              cs[:, CS["iota"][0] + 32 * qd:CS["iota"][0] + 32 * qd + 32].unsqueeze(1).to_broadcast([128, 16, 32]),
              ALU.is_equal)
            tv = V(ve.tensor_tensor, oi, oi, gg, ALU.mult)

            def rest():
                b, fw, users = banks.get(WORK)
                for j in range(16):
                    tok = P(te.matmul, b[:, 32 * j:32 * j + 32], oj[:, j, :], oi[:, j, :], start=True, stop=True,
                            w=[tv, *fw], inc=(j == 15))
                t_oh[0] = tok
                users.append(V(ve.tensor_copy, wbuf[qd % 2][:, :, t0:t0 + 16],
                               b.rearrange("p (t i) -> p i t", t=16), w=[tok]))
            return rest

        for bt in range(16):
            build_w(0, bt)()
        down = Down()
        pend = None
        t_act_read = [None, None]
        i = 0
        for qd in range(4):
            for gq in range(8):
                e0 = 128 * (32 * qd + 4 * gq)
                ut, tu_, uu = wtile(T["uT"], e0, 512)
                vt, tv_, uv = rtile(T["v"], e0, 4, D)
                rest = build_w(qd + 1, 2 * gq) if qd < 3 else None
                a = acts[i % 2]
                for p in range(2):
                    b, fw, users = banks.get(WORK)
                    for j in range(2):
                        c = slice(128 * (2 * p + j), 128 * (2 * p + j) + 128)
                        tok = accum(b[:, 256 * j:256 * j + 256], [(ut[:, k, c], hT[:, k, :]) for k in range(8)],
                                    w=[tu_, *fw])
                    ta = A(se.activation, a[:, 2 * p:2 * p + 2, :], b.rearrange("p (m t) -> p m t", m=2), ACT.Gelu,
                           w=[tok, t_act_read[i % 2]])
                    users.append(ta)
                    ta = V(ve.tensor_tensor, a[:, 2 * p:2 * p + 2, :], a[:, 2 * p:2 * p + 2, :],
                           wbuf[qd % 2][:, 4 * gq + 2 * p:4 * gq + 2 * p + 2, :], ALU.mult, w=[ta])
                uu.append(tok)
                if rest is not None:
                    rest()
                    rest = build_w(qd + 1, 2 * gq + 1)
                if pend is not None:
                    t_act_read[(i - 1) % 2] = down.add(*pend, last=False)
                if rest is not None:
                    rest()
                pend = (vt, tv_, uv, a, ta)
                i += 1
        tok = down.add(*pend, last=True)
        for m in range(8):
            V(ve.scalar_tensor_tensor, xT[:, m, :], acc(m), mod[:, 40 + m:41 + m], xT[:, m, :], ALU.mult, ALU.add,
              w=[tok])
        finish()


def cbuf_reset(space, arena):
    space[0] = 2048
    return arena[:, 0:2048]


def constants():
    f = np.float32
    cs = np.zeros((128, NCS), f)

    def put(dst, table, name, x):
        o, n = table[name]
        dst[:x.shape[0], o:o + n] = x
    p = np.arange(128)
    put(cs, CS, "ident", np.eye(128, dtype=f))
    put(cs, CS, "ones", np.ones((128, 128), f))
    put(cs, CS, "bones", (p[:, None] // 64 == p[None, :] // 64).astype(f))
    partner = np.where(p % 32 < 16, p + 16, p - 16)
    put(cs, CS, "perm", (p[:, None] == partner[None, :]).astype(f))
    sel = np.zeros((8, 8, 128), f)
    for h in range(8):
        sel[h, h] = 1
    put(cs, CS, "sel", sel.reshape(8, 1024))
    put(cs, CS, "iota", np.tile(np.arange(128, dtype=f), (128, 1)))
    put(cs, CS, "iota16", np.tile(np.arange(16, dtype=f), (128, 1)))
    put(cs, CS, "iota8", np.tile(np.arange(8, dtype=f), (128, 1)))
    t = np.arange(256)
    put(cs, CS, "scan64", np.tile((t % 64 != 0).astype(f), (128, 1)))
    put(cs, CS, "scan128", np.tile((t % 128 != 0).astype(f), (128, 1)))
    ms = np.zeros((128, NMS), np.uint32)
    j, i = p[:, None], p[None, :]
    put(ms, MS, "gla", ((j <= i) & (j // 64 == i // 64)).astype(np.uint32))
    put(ms, MS, "ssd", (j <= i).astype(np.uint32))
    col = np.arange(64)
    start = np.clip(col - 8, 0, 48)
    cm = (col[None, :] >= start[:, None]) & (col[None, :] < start[:, None] + 16)
    put(ms, MS, "col", np.tile(cm, (2, 4)).astype(np.uint32))
    hc = np.zeros((128, NHC), f)
    w = np.pi * np.outer(t, 2 * t + 1) / 512.0
    for name, m in (("C", np.cos(w)), ("S", np.sin(w)), ("CI", np.cos(w).T / 256), ("SI", -np.sin(w).T / 256)):
        put(hc, HC, name, m.reshape(2, 128, 256).transpose(1, 0, 2).reshape(128, 512).astype(f))
    tt = np.linspace(0.0, 1.0, L, dtype=f)
    deltas = np.abs(np.linspace(math.log(1e-2) / 1.5, math.log(1e-2) / 0.3, 512, dtype=f))
    dec = np.exp(-tt[:, None] * deltas)
    put(hc, HC, "dec", dec.reshape(2, 128, 512).transpose(1, 0, 2).reshape(128, 1024).astype(f))
    wv = f(2.0 * math.pi / L) * np.arange(L, dtype=f)[:, None]
    bands = np.linspace(1e-4, 15.0, 16, dtype=f)[None, :]
    feats = np.concatenate([tt[:, None], np.cos(bands * wv), -np.sin(bands * wv)], axis=-1)
    put(hc, HC, "feats", feats.T.astype(f))
    inv = (f(10000.0) ** (-np.arange(16, dtype=f) / 16)).astype(f)
    d = p % 64
    pos = np.where((d < 32)[:, None], (t // 64)[None, :], (t % 64)[None, :]).astype(f)
    ang = pos * inv[d % 16][:, None]
    put(hc, HC, "ropeC", np.cos(ang).astype(f))
    put(hc, HC, "ropeS", (np.where((d % 32 < 16)[:, None], -1, 1) * np.sin(ang)).astype(f))
    return cs, ms, hc


def kernel(**x):
    import concourse.bacc as bacc
    from concourse.bass_utils import run_bass_kernel_spmd

    x = {k: np.asarray(v) for k, v in x.items()}
    f = np.float32
    cs, ms, hc = constants()
    pv = np.zeros((128, NPV), f)

    def vec(name, v):
        v = v.reshape(-1)
        o, n = PV[name]
        pv[:, o:o + n] = v.reshape(n, 128).T

    def rows(name, m):
        o, n = PV[name]
        pv[:m.shape[0], o:o + n] = m

    for l in range(2):
        vec(f"ada_b{l}", x["ada_b"][l])
        vec(f"norm1_w{l}", x["norm1_w"][l])
        vec(f"norm2_w{l}", x["norm2_w"][l])
        vec(f"gla_a_b{l}", x["gla_a_b"][l])
        vec(f"gla_norm_w{l}", x["gla_norm_w"][l])
        vec(f"conv_w{l}", x["conv_w"][l])
        vec(f"conv_b{l}", x["conv_b"][l])
        rows(f"dt_bias{l}", x["dt_bias"][l][:, None])
        rows(f"a_log{l}", x["a_log"][l][:, None])
        vec(f"d_skip{l}", np.repeat(x["d_skip"][l], 64))
        vec(f"ssd_norm_w{l}", x["ssd_norm_w"][l])
        rows(f"gla_a_w{l}", x["gla_a_w"][l])
    vec("c", x["c"][0])
    o, n = PV["c2"]
    pv[:, o:o + n:2] = x["c_2"][0].reshape(8, 128).T
    pv[:, o + 1:o + n:2] = x["c_ctx_2"].reshape(8, 128).T
    vec("final_w", x["final_norm_w"])
    vec("norm1_g", x["norm1_g_2"][0])
    vec("norm2_g", x["norm2_g_2"][0])
    vec("b_ada", x["b_ada_2"][0])
    vec("b_in", x["b_in_2"][0])
    vec("hcw", x["hy_conv_w_2"][0])
    vec("hcb", x["hy_conv_b_2"][0])
    for name, key in (("f1b", "hy_f1_b_2"), ("f2b", "hy_f2_b_2"), ("f3b", "hy_f3_b_2"), ("freq", "hy_sin_freq_2")):
        rows(name, x[key][0][:, None])
    vec("skip", x["hy_skip_2"][0])
    vec("qg", np.concatenate([x["q_norm_g_2"][0]] * 2))
    vec("kg", np.concatenate([x["k_norm_g_2"][0]] * 2))
    rows("router", x["router_w"][0].reshape(8, 128, 8).transpose(1, 0, 2).reshape(128, 64))
    rows("f1w", x["hy_f1_w_2"][0])
    rows("f2w", x["hy_f2_w_2"][0])
    rows("f3w", x["hy_f3_w_2"][0])
    rows("bv", x["b_in_2"][0][None, 2560:3072])

    r, qc, i, kc = np.arange(4), np.arange(64), np.arange(4), np.arange(64)
    dr = (i[None, :] - r[:, None] + 7)[:, None, :, None]
    dcx = (np.clip(kc[None, :] - qc[:, None], -15, 15) + 15)[None, :, None, :]
    bias = x["na_rpb_2"][0][:, dr, dcx].reshape(8, 2, 128, 256).transpose(2, 1, 0, 3).reshape(128, 4096)

    arrays = {
        "pv": pv, "cs": cs, "ms": ms, "hc": hc, "xT": x["x"][0].T, "ctxT": x["ctx_2"][0].T,
        "ada_w": x["ada_w"], "w_in": x["w_in"], "w_out": x["w_out"],
        "ffn_w_gate": x["ffn_w_gate"][0], "ffn_w_up": x["ffn_w_up"][0], "ffn_w_down": x["ffn_w_down"][0],
        "moe_w_gate": x["moe_w_gate"][0], "moe_w_up": x["moe_w_up"][0], "moe_w_down": x["moe_w_down"][0],
        "w_ada": x["w_ada_2"][0], "w_in2": x["w_in_2"][0], "f4w": x["hy_f4_w_2"][0],
        "w_hy": x["w_hy_out_2"][0], "w_na": x["w_na_out_2"][0], "w_out2": x["w_out_2"][0],
        "w_pq": x["peer_w_q_2"][0],
        "keysT": x["peer_keys_2"][0].transpose(3, 0, 1, 2).reshape(128, 2048),
        "uT": x["peer_u_2"][0].T, "v": x["peer_v_2"][0], "bias": bias,
    }
    nc = bacc.Bacc("TRN2", target_bir_lowering=False, num_devices=1)
    ins, T = {}, {}
    for name, a in arrays.items():
        a = np.ascontiguousarray(a)
        ins[f"in_{name}"] = a
        T[name] = nc.dram_tensor(f"in_{name}", a.shape, mybir.dt.from_np(a.dtype), kind="ExternalInput").ap()
    T["out"] = nc.dram_tensor("out_x", (1024, 256), F32, kind="ExternalOutput").ap()
    program(nc, T)
    res = run_bass_kernel_spmd(nc, [ins], core_ids=[0])
    return np.ascontiguousarray(res.results[0]["out_x"].T)[None]
```

```python
import math
from contextlib import ExitStack

import numpy as np

import concourse.bass as bass
from concourse import mybir

ALU = mybir.AluOpType
ACT = mybir.ActivationFunctionType
AX = mybir.AxisListType
F32 = mybir.dt.float32
U32 = mybir.dt.uint32
BF16 = mybir.dt.bfloat16
I32 = mybir.dt.int32

D = 1024
L = 256
EPS = 1e-6
SLOT = 4224
NSLOT = 5
ARENA = 22208
BIG = -3.0e38
STOP = None


def layout(items):
    at, out = 0, {}
    for name, n in items:
        out[name] = (at, n)
        at += n
    return out, at


NARROW = ([("c", 8), ("c2", 16)]
          + [(f"{n}{l}", w) for l in range(2) for n, w in (
              ("norm1_w", 8), ("ada_b", 48), ("norm2_w", 8), ("gla_a_b", 2), ("gla_norm_w", 1), ("conv_w", 24),
              ("conv_b", 6), ("dt_bias", 1), ("a_log", 1), ("d_skip", 4), ("ssd_norm_w", 4))]
          + [("final_w", 8), ("norm1_g", 8), ("norm2_g", 8), ("b_ada", 48), ("b_in", 40), ("hcw", 36), ("hcb", 12),
             ("f1b", 1), ("f2b", 1), ("f3b", 1), ("freq", 1), ("skip", 8), ("qg", 1), ("kg", 1), ("router", 64)])
WIDE = [("gla_a_w0", 256), ("gla_a_w1", 256), ("f1w", 64), ("f2w", 64), ("f3w", 64), ("bv", 512)]
PV, NPV = layout(NARROW + WIDE)
NNARROW = sum(n for _, n in NARROW)
CS, NCS = layout([("ident", 128), ("ones", 128), ("bones", 128), ("perm", 128), ("tri", 128), ("iota", 128),
                  ("iota16", 16), ("scan64", 256), ("scan128", 256), ("iota8", 8)])
MS, NMS = layout([("gla", 128), ("ssd", 128), ("col", 256)])
HC, NHC = layout([("C", 512), ("S", 512), ("CI", 512), ("SI", 512), ("dec", 1024), ("ropeC", 256),
                  ("ropeS", 256), ("feats", 256)])


class Eng:

    def __init__(self, e, sem, chained):
        self.e, self.sem, self.n, self.chained, self.seen = e, sem, 0, chained, {}
        self.queue = []

    def emit(self, queue=None):
        for instruction in self.queue if queue is None else queue:
            instruction()

    def dma(self, out, in_, sem):
        self.queue.append(lambda: self.e.dma_start(out, in_).then_inc(sem, 16))

    def wait(self, toks):
        for t in toks:
            if t is None:
                continue
            sem, v = t
            if self.seen.get(id(sem), 0) < v:
                self.queue.append(lambda sem=sem, v=v: self.e.wait_ge(sem, v))
                self.seen[id(sem)] = v

    def __call__(self, fn, *args, w=(), inc=True, **kw):
        self.wait(w)
        if self.chained and self.n:
            self.wait([(self.sem, self.n)])
        if not inc:
            self.queue.append(lambda: fn(*args, **kw))
            return None
        self.n += 1
        self.queue.append(lambda: fn(*args, **kw).then_inc(self.sem, 1))
        return (self.sem, self.n)

    @property
    def last(self):
        return (self.sem, self.n) if self.n else None


class Banks:

    def __init__(self, banks):
        self.banks, self.free, self.at = banks, [[] for _ in banks], 0

    def get(self, among=None):
        if among is None:
            i = self.at % len(self.banks)
        else:
            i = among[self.at % len(among)]
        self.at += 1
        w, self.free[i] = self.free[i], []
        return self.banks[i], w, self.free[i]


class Ring:

    def __init__(self, eng, buf, sems):
        self.eng, self.buf, self.sems, self.n = eng, buf, sems, 0
        self.users = [[] for _ in sems]

    def load(self, parts):
        s = self.n % len(self.sems)
        self.n += 1
        assert self.users[s] or self.n <= len(self.sems), "a slot that nobody has freed"
        self.eng.wait(self.users[s])
        self.users[s] = []
        base = self.buf[:, s * SLOT:(s + 1) * SLOT]
        for view, src in parts(base):
            self.eng.dma(view, src, self.sems[s][0])
            self.sems[s][1] += 16
        return base, (self.sems[s][0], self.sems[s][1]), self.users[s]


def program(nc, T):
    with ExitStack() as ctx:
        def sb(name, n, dt=F32):
            return ctx.enter_context(nc.sbuf_tensor(name, [128, n], dt))[:, :]

        def sem(name):
            return ctx.enter_context(nc.semaphore(name))

        te, ve, se, ge = nc.tensor, nc.vector, nc.scalar, nc.gpsimd
        P = Eng(te, sem("s_pe"), False)
        V = Eng(ve, sem("s_dve"), True)
        A = Eng(se, sem("s_act"), True)
        G = Eng(ge, sem("s_pool"), True)
        SP = Eng(nc.sync, sem("s_sp"), False)
        s_in = sem("s_in")
        s_out = sem("s_out")

        pv = sb("pv", NPV)
        cs = sb("cs", NCS)
        ms = sb("ms", NMS, U32)
        xT = sb("xT", 2048).rearrange("p (k t) -> p k t", k=8)
        hT = sb("hT", 2048).rearrange("p (k t) -> p k t", k=8)
        mods = sb("mods", 4 * 48)
        small = sb("small", 32)
        accb = sb("accb", 1024)
        selb = sb("sel", 1024)
        ringbuf = sb("ring", NSLOT * SLOT)
        arena = sb("arena", ARENA)
        hc = arena[:, ARENA - NHC:ARENA]
        ring = Ring(SP, ringbuf, [[sem(f"s_ring{i}"), 0] for i in range(NSLOT)])
        banks = Banks([ctx.enter_context(nc.psum_tensor(f"ps{i}", [128, 512], F32))[:, :] for i in range(8)])

        def pvc(name, i=0, n=1, rows=128):
            o = PV[name][0] + i
            return pv[0:rows, o:o + n]

        def cst(name, rows=128, cols=None):
            o, n = CS[name]
            return cs[0:rows, o:o + (cols or n)]

        def hcc(name, rows=128):
            o, n = HC[name]
            return hc[0:rows, o:o + n]

        class Arena:
            at = 0

        limit = [ARENA]

        def buf(n):
            a = Arena.at
            Arena.at += n
            assert Arena.at <= limit[0], (Arena.at, limit[0])
            return arena[:, a:a + n]

        def everyone():
            toks = [x.last for x in (P, V, A, G)]
            for x in (P, V, A, G):
                x.wait([t for t in toks if t and t[0] is not x.sem])
            V.wait([V.last])
            A.wait([A.last])

        def everyone_but_pool():
            toks = [x.last for x in (P, V, A)]
            for x in (P, V, A, SP):
                x.wait([t for t in toks if t and t[0] is not x.sem])
            for x in (P, V, A):
                x.wait([x.last])

        def fresh():
            everyone()
            Arena.at = 0

        def v4(x, k):
            return x.rearrange("p (k t) -> p k t", k=k)

        ident, ones, bones = cst("ident"), cst("ones"), cst("bones")

        s_in = [sem(f"s_in{i}") for i in range(6)]
        for q, (dst, src) in zip(s_in, (
                (pv[:, 0:NNARROW], T["pv"][:, 0:NNARROW]), (xT, T["xT"].rearrange("(k p) t -> p k t", p=128)),
                (cs, T["cs"]), (pv[:, NNARROW:NPV], T["pv"][:, NNARROW:NPV]), (selb[0:8, :], T["sel"]),
                (ms, T["ms"]))):
            A.dma(dst, src, q)
        t_pv, t_x, t_cs, t_wide, t_sel, t_ms = [(q, 16) for q in s_in]
        V.wait([t_pv])
        A.wait([t_pv])

        def wtile(w, c0, n):
            def parts(base):
                v = base[:, 0:8 * n].rearrange("p (k n) -> p k n", k=8)
                return [(v, w[:, c0:c0 + n].rearrange("(k p) n -> p k n", p=128))]
            base, tok, users = ring.load(parts)
            return base[:, 0:8 * n].rearrange("p (k n) -> p k n", k=8), tok, users

        def rtile(w, r0, n, cols):
            def parts(base):
                v = base[:, 0:n * cols].rearrange("p (k n) -> p k n", k=n)
                return [(v, w[r0:r0 + 128 * n, :].rearrange("(k p) n -> p k n", p=128))]
            base, tok, users = ring.load(parts)
            return base[:, 0:n * cols].rearrange("p (k n) -> p k n", k=n), tok, users

        def accum(out, pairs, w=(), inc=True):
            tok = None
            for i, (a, b) in enumerate(pairs):
                tok = P(te.matmul, out, a, b, start=(i == 0), stop=(i == len(pairs) - 1),
                        w=w, inc=(inc and i == len(pairs) - 1))
            return tok

        def transposes(ins, w=()):
            b, fw, users = banks.get()
            tok = None
            at = 0
            for i, x in enumerate(ins):
                k, m = x.shape
                tok = P(te.transpose, b[0:m, at:at + k], x, ident[0:k, 0:k], w=[*w, *fw],
                        inc=(i == len(ins) - 1))
                at += k
            return b, tok, users

        def ada_tile(w, n, s, stride, ncond, bias, outs, t_s):
            state = {}

            def rows_():
                tile, tt, tu = wtile(w, 512 * n, 512)
                for c in range(ncond):
                    a = accb[:, 512 * c:512 * c + 512]
                    V(ve.tensor_scalar, a, tile[:, 0, :], s[:, c:c + 1], None, ALU.mult, w=[tt, t_s, t_acc[0]])
                    for k in range(1, 8):
                        t = V(ve.scalar_tensor_tensor, a, tile[:, k, :], s[:, stride * k + c:stride * k + c + 1], a,
                              ALU.mult, ALU.add)
                tu.append(t)
                state["t"] = t

            def columns(among=None):
                b, fw, users = banks.get(among)
                for c in range(ncond):
                    for m in range(4):
                        tok = P(te.matmul, b[:, 4 * c + m:4 * c + m + 1],
                                accb[:, 512 * c + 128 * m:512 * c + 128 * m + 128], ones[:, 0:1],
                                start=True, stop=True, w=[state["t"], t_cs, *fw])
                t_acc[0] = tok
                for c in range(ncond):
                    t = V(ve.tensor_tensor, outs[c][:, 4 * n:4 * n + 4], b[:, 4 * c:4 * c + 4],
                          pvc(bias, 4 * n, 4), ALU.add, w=[tok])
                users.append(t)
                return t
            return rows_, columns

        t_acc = [None]

        class Background:
            todo, half = [], None

        def background(among=None):
            if Background.half is not None:
                Background.half(among)
                Background.half = None
            if Background.todo:
                rows_, Background.half = Background.todo.pop(0)
                rows_()

        def background_end():
            while Background.todo or Background.half is not None:
                background()

        def rstd_of(ps, scale, n, out, tok):
            t0 = V(ve.tensor_scalar, out, ps, scale, EPS, ALU.mult, ALU.add, w=[tok])
            t1 = V(ve.reciprocal, out, out)
            return A(se.activation, out, out, ACT.Sqrt, w=[t1]), t0

        def norm_stats(src, t_src, scratch):
            sq, r = scratch[:, 0:2048].rearrange("p (k t) -> p k t", k=8), scratch[:, 2048:2304]
            t = A(se.activation, sq, src, ACT.Square, w=t_src)
            b, fw, users = banks.get()
            tok = accum(b[:, 0:256], [(ones, sq[:, k, :]) for k in range(8)], w=[t, t_cs, *fw])
            tr, t0 = rstd_of(b[:, 0:256], 1.0 / D, 256, r, tok)
            users.append(t0)
            return tr

        def norm_apply(src, g, sc, sh, dst, tr, scratch):
            r, gs = scratch[:, 2048:2304], scratch[:, 2304:2312]
            if sc is not None:
                V(ve.scalar_tensor_tensor, gs, sc, 1.0, g, ALU.add, ALU.mult, w=[tr])
            else:
                V(ve.tensor_copy, gs, g, w=[tr])
            t = None
            for k in range(8):
                t = V(ve.scalar_tensor_tensor, dst[:, k, :], src[:, k, :], gs[:, k:k + 1], r, ALU.mult, ALU.mult)
                if sc is not None:
                    t = A(se.activation, dst[:, k, :], dst[:, k, :], ACT.Identity, bias=sh[:, k:k + 1], w=[t])
            return t

        def norm_mod(src, g, sc, sh, dst, t_src, scratch):
            return norm_apply(src, g, sc, sh, dst, norm_stats(src, t_src, scratch), scratch)

        def proj(tile, tt, tu, c0, nch, rhs, w, take):
            tok = None
            for m0 in range(0, nch, 2):
                n = min(2, nch - m0)
                b, fw, users = banks.get()
                for j in range(n):
                    c = c0 + 128 * (m0 + j)
                    tok = accum(b[:, 256 * j:256 * j + 256],
                                [(tile[:, k, c:c + 128], rhs[:, k, :]) for k in range(8)], w=[tt, *w, *fw],
                                inc=(j == n - 1))
                users.append(take(b[:, 0:256 * n].rearrange("p (m t) -> p m t", m=n), m0, n, tok))
            tu.append(tok)
            return tok

        def proj_tm(tile, tt, tu, rhs, w, take, bias=None):
            for t in range(2):
                b, fw, users = banks.get()
                pairs = [(rhs[:, k, 128 * t:128 * t + 128], tile[:, k, 0:512]) for k in range(8)]
                if bias is not None:
                    pairs.append((ones[0:1, :], bias))
                tok = accum(b, pairs, w=[tt, *w, *fw])
                users.append(take(b, t, tok))
            tu.append(tok)

        def copy_to(dst, eng="A"):
            def take(b, m0, n, tok):
                if eng == "A":
                    return A(se.activation, dst[:, m0:m0 + n, :], b, ACT.Copy, w=[tok])
                return V(ve.tensor_copy, dst[:, m0:m0 + n, :], b, w=[tok])
            return take

        def residual(tile_c0, gate, n0):
            def take(b, m0, n, tok):
                for j in range(n):
                    m = n0 + m0 + j
                    t = V(ve.scalar_tensor_tensor, xT[:, m, :], b[:, j, :], gate[:, m:m + 1], xT[:, m, :],
                          ALU.mult, ALU.add, w=[tok])
                return t
            return take

        def log1pexp_neg_abs(x, tmp, w):
            t = A(se.activation, tmp, x, ACT.Abs, w=[V.last, *w])
            t = A(se.activation, tmp, tmp, ACT.Exp, scale=-1.0, w=[t])
            t = V(ve.tensor_scalar, tmp, tmp, 1.0, None, ALU.add, w=[t])
            return A(se.activation, tmp, tmp, ACT.Ln, w=[t])

        WORK = [4, 5, 6, 7]

        def mixer(l, mod, th):
            w_in, w_out = T["w_in"][l], T["w_out"][l]
            zT = v4(buf(1024), 4)
            merged = v4(buf(2048), 8)
            xbc = buf(6 * 259).rearrange("p (k t) -> p k t", k=6)
            dts, sp, cum, alr, btm = buf(256), buf(256), buf(256), buf(256), buf(128)
            qkT = buf(1024)
            qT, kT, oT = v4(qkT[:, 0:512], 2), v4(qkT[:, 512:1024], 2), v4(qkT, 4)
            gT = v4(buf(1024), 4)
            v_tm = v4(buf(1024), 2)
            qe_, la_, lt_, ktail_ = (buf(512) for _ in range(4))
            qe, la, lt, ktail = (v4(x, 2) for x in (qe_, la_, lt_, ktail_))
            kep_, ktp_ = buf(1024), buf(1024)
            kep, ktp = v4(kep_, 4), v4(ktp_, 4)
            spad = buf(4 * 3 * 128).rearrange("p (h n v) -> p h n v", h=4, n=3)
            attm = buf(1024).rearrange("p (h t i) -> p h t i", h=4, t=2)
            bl = buf(8).rearrange("p (c n) -> p c n", c=2)
            ebl = buf(8).rearrange("p (c n) -> p c n", c=2)
            xc = v4(buf(1536), 6)
            av = buf(1)
            dc = buf(32).rearrange("p (t c) -> p t c", t=2)
            xdt_ = buf(1024)
            xdt = xdt_.rearrange("p (t h q) -> p t h q", t=2, h=8)
            dec = buf(2048).rearrange("p (h t i) -> p h t i", h=8, t=2)
            ecb = buf(1024).rearrange("p (h i) -> p h i", h=8)
            fl = buf(8)
            hflat = hT.rearrange("p k t -> p (k t)")
            wx = la_.rearrange("p (h q) -> p h q", h=8)
            bpad = v4(lt_, 2)
            gm = hflat[:, 0:512].rearrange("p (g t i) -> p g t i", g=2, t=2)
            s1 = ktail_.rearrange("p (h q) -> p h q", h=8)
            rr1 = hflat[:, 512:768]
            yT = v4(xbc.rearrange("p k t -> p (k t)")[:, 0:1024], 4)

            for z in (xbc[:, :, 0:3], kep, ktp, attm, spad):
                tz = G(ge.memset, z, 0.0, w=[th])
            hw = [th]

            tile, tt, tu = wtile(w_in, 1536, 528)
            b, fw, users = banks.get()
            tok = accum(b[0:16, 0:256], [(tile[:, k, 0:16], hT[:, k, :]) for k in range(8)], w=[tt, *hw, *fw])
            t_alr = V(ve.tensor_copy, alr[0:16, :], b[0:16, 0:256], w=[tok])
            users.append(t_alr)
            proj(tile, tt, tu, 16, 4, hT, hw,
                 lambda b, m0, n, tok: A(se.activation, zT[:, m0:m0 + n, :], b, ACT.Silu, w=[tok]))
            b, fw, users = banks.get()
            for c in range(2):
                tok = P(te.matmul, b[:, 256 * c:256 * c + 256], pvc(f"gla_a_w{l}", 128 * c, 128, rows=16),
                        alr[0:16, :], start=True, stop=True, w=[t_alr, t_wide, *fw])
            for c in range(2):
                t = V(ve.tensor_scalar, la[:, c, :], b[:, 256 * c:256 * c + 256], pvc(f"gla_a_b{l}", c), None,
                      ALU.add, w=[tok])
            users.append(t)
            background()

            tile, tt, tu = wtile(w_in, 0, 512)

            def take_qk(b, m0, n, tok):
                if m0 == 0:
                    return V(ve.tensor_scalar, qT, b, 0.125, None, ALU.mult, w=[tok])
                return V(ve.tensor_copy, kT, b, w=[tok])
            proj(tile, tt, tu, 0, 4, hT, hw, take_qk)
            background()
            t = log1pexp_neg_abs(la, lt, [t])
            V(ve.scalar_tensor_tensor, lt, la, 0.0, lt, ALU.min, ALU.subtract, w=[t])
            for c in range(2):
                t = V(ve.tensor_tensor_scan, la[:, c, :], cst("scan64"), lt[:, c, :], 0.0, ALU.mult, ALU.add,
                      w=[t_cs])
            tla = t
            t = A(se.activation, lt, la, ACT.Exp, scale=1.0 / 16, w=[t])
            tq = V(ve.tensor_tensor, qe, qT, lt, ALU.mult, w=[t])
            t = A(se.activation, lt, la, ACT.Exp, scale=-1.0 / 16, w=[tq])
            for h in range(4):
                r = slice(64 * (h % 2), 64 * (h % 2) + 64)
                tk = V(ve.tensor_tensor, kep[r, h, :], kT[r, h // 2, :], lt[r, h // 2, :], ALU.mult, w=[t, tz])
            t = V(ve.tensor_scalar, bl, la[:, :, 63:256:64], 1.0 / 16, None, ALU.mult)
            tebl = A(se.activation, ebl, bl, ACT.Exp, w=[t])
            for c in range(2):
                for n in range(4):
                    t = A(se.activation, ktail[:, c, 64 * n:64 * n + 64], la[:, c, 64 * n:64 * n + 64], ACT.Exp,
                          bias=bl[:, c, n:n + 1], scale=-1.0 / 16)
            tkl = V(ve.tensor_tensor, ktail, ktail, kT, ALU.mult, w=[t])

            tile, tt, tu = wtile(w_in, 512, 512)
            proj_tm(tile, tt, tu, hT, hw, lambda b, t, tok: V(ve.tensor_copy, v_tm[:, t, :], b, w=[tok]))
            tv_tm = V.last
            background()
            xin = xbc[:, :, 3:259]
            tile, tt, tu = wtile(w_in, 2576, 264)
            b, fw, users = banks.get()
            tok = accum(b[0:8, 0:256], [(tile[:, k, 256:264], hT[:, k, :]) for k in range(8)], w=[tt, *fw])
            t_dt = V(ve.tensor_scalar, dts[0:8, :], b[0:8, 0:256], pvc(f"dt_bias{l}", rows=8), None, ALU.add,
                     w=[tok])
            users.append(t_dt)
            proj(tile, tt, tu, 0, 2, hT, hw, copy_to(xin[:, 4:6, :], "A"))
            background()
            tile, tt, tu = wtile(w_in, 2064, 512)
            proj(tile, tt, tu, 0, 4, hT, hw, copy_to(xin, "A"))
            txin = A.last
            background()

            for o in range(2):
                b, fw, users = banks.get()
                for c in range(2):
                    for t_ in range(2):
                        s = slice(128 * t_, 128 * t_ + 128)
                        at = 128 * (2 * c + t_)
                        tok = P(te.matmul, b[:, at:at + 128], kep[:, 2 * c + o, s], qe[:, c, s],
                                start=True, stop=True, w=[tk, tq, *fw])
                for c in range(2):
                    for t_ in range(2):
                        at = 128 * (2 * c + t_)
                        ta = V(ve.copy_predicated, attm[:, 2 * c + o, t_, :],
                               ms[:, MS["gla"][0]:MS["gla"][0] + 128], b[:, at:at + 128], w=[tok, tz, t_ms])
                users.append(ta)
            b, tok, users = transposes([ktail[:, c, 128 * s:128 * s + 128] for s in range(2) for c in range(2)],
                                       w=[tkl])
            for n in range(4):
                r = slice(64 * (n % 2), 64 * (n % 2) + 64)
                tkt = V(ve.tensor_copy, ktp[r, n, :], b[r, 256 * (n // 2):256 * (n // 2) + 256], w=[tok, tz])
            users.append(tkt)

            t = log1pexp_neg_abs(dts[0:8, :], sp[0:8, :], [t_dt])
            ta_ = A(se.activation, av[0:8, :], pvc(f"a_log{l}", rows=8), ACT.Exp)
            V(ve.scalar_tensor_tensor, dts[0:8, :], dts[0:8, :], 0.0, sp[0:8, :], ALU.max, ALU.add, w=[t])
            V(ve.tensor_scalar, sp[0:8, :], dts[0:8, :], av[0:8, :], -1.0, ALU.mult, ALU.mult, w=[ta_])
            tc = V(ve.tensor_tensor_scan, cum[0:8, :], cst("scan128", rows=8), sp[0:8, :], 0.0,
                   ALU.mult, ALU.add)

            tile, tt, tu = wtile(w_in, 1024, 512)
            proj(tile, tt, tu, 0, 4, hT, hw,
                 lambda b, m0, n, tok: A(se.activation, gT[:, m0:m0 + n, :], b, ACT.Silu, w=[tok]))
            tg = A.last
            for z, t in ((bpad, tkl), (s1, tkt), (gm, P.last)):
                tz2 = G(ge.memset, z, 0.0, w=[t])
            background()
            for n in range(3):
                b, fw, users = banks.get()
                for c in range(2):
                    tok = P(te.matmul, b[:, 256 * c:256 * c + 256], ktp[:, n, 128 * c:128 * c + 128],
                            v_tm[:, n // 2, 256 * c:256 * c + 256], start=True, stop=True, w=[tkt, *fw])
                for h in range(4):
                    r = slice(64 * (h % 2), 64 * (h % 2) + 64)
                    src = b[r, 256 * (h // 2) + 128 * (h % 2):256 * (h // 2) + 128 * (h % 2) + 128]
                    if n == 0:
                        ts = V(ve.tensor_copy, spad[r, h, 0, :], src, w=[tok, tz])
                    else:
                        ts = V(ve.scalar_tensor_tensor, spad[r, h, n, :], spad[r, h, n - 1, :],
                               ebl[r, h // 2, n:n + 1], src, ALU.mult, ALU.add, w=[tok, tebl])
                users.append(ts)
            b, tok, users = transposes([x[0:8, 128 * t:128 * t + 128] for t in range(2) for x in (dts, cum)],
                                       w=[tc])
            users.append(V(ve.tensor_copy, dc, b[:, 0:32].rearrange("p (t c) -> p t c", t=2), w=[tok]))
            for p in range(4):
                b, fw, users = banks.get()
                for j in range(2):
                    h = 2 * p + j
                    tok = P(te.matmul, b[:, 256 * j:256 * j + 256], selb[0:8, 128 * h:128 * h + 128], cum[0:8, :],
                            start=True, stop=True, w=[tc, t_sel, *fw])
                for j in range(2):
                    h = 2 * p + j
                    for t in range(2):
                        V(ve.tensor_scalar, dec[:, h, t, :], b[:, 256 * j + 128 * t:256 * j + 128 * t + 128],
                          dc[:, t, 8 + h:9 + h], 0.0, ALU.subtract, ALU.min, w=[tok])
                    tv = V(ve.tensor_tensor, fl[:, h:h + 1], b[:, 256 * j + 127:256 * j + 128],
                           dc[:, 0, 8 + h:9 + h], ALU.subtract)
                te_ = A(se.activation, ecb[:, 2 * p:2 * p + 2, :],
                        b.rearrange("p (j t i) -> p j t i", j=2, t=2)[:, :, 1, :], ACT.Exp, w=[tok, tv])
                users += [tv, te_]
                if p == 1:
                    for h in range(4):
                        b, fw, users = banks.get()
                        for t in range(2):
                            s = slice(128 * t, 128 * t + 128)
                            P(te.matmul, b[:, s], v_tm[:, t, 128 * h:128 * h + 128], attm[:, h, t, :],
                              start=True, stop=False, w=[ta, ts, tv_tm, *fw], inc=False)
                            for n in range(max(1, 2 * t), 2 * t + 2):
                                tok = P(te.matmul, b[:, 64 * n:64 * n + 64], spad[:, h, n - 1, :],
                                        qe[:, h // 2, 64 * n:64 * n + 64], start=False, stop=(n == 2 * t + 1))
                        to = A(se.activation, oT[:, h, :], b[:, 0:256], ACT.Copy, w=[tok, tkl])
                        users.append(to)
            tdec = A(se.activation, dec, dec, ACT.Exp, w=[tv])
            tf = A(se.activation, fl, fl, ACT.Exp)
            background()
            for k in (4, 5, 0, 1, 2, 3):
                V(ve.tensor_scalar, xc[:, k, :], xbc[:, k, 0:256], pvc(f"conv_w{l}", k), pvc(f"conv_b{l}", k),
                  ALU.mult, ALU.add, w=[txin])
                for j in range(1, 4):
                    t = V(ve.scalar_tensor_tensor, xc[:, k, :], xbc[:, k, j:j + 256],
                          pvc(f"conv_w{l}", 6 * j + k), xc[:, k, :], ALU.mult, ALU.add)
                if k in (5, 1, 3):
                    tx = A(se.activation, xc[:, k - 1:k + 1, :], xc[:, k - 1:k + 1, :], ACT.Silu, w=[t])
                if k == 5:
                    tx45 = tx
            sq, rr = v4(kep_, 4), v4(ktp_, 4)
            t = A(se.activation, sq, oT, ACT.Square, w=[to])
            for p in range(2):
                b, fw, users = banks.get()
                tok = accum(b, [(ones, sq[:, 2 * p:2 * p + 2, :])], w=[t, *fw])
                tr, t0 = rstd_of(b.rearrange("p (k t) -> p k t", k=2), 1.0 / 128, 0, rr[:, 2 * p:2 * p + 2, :], tok)
                users.append(t0)
            for g in range(2):
                r = slice(64 * g, 64 * g + 64)
                tb = V(ve.tensor_copy, bpad[r, g, :], xc[r, 4, :], w=[tx45, tz2])
            V(ve.scalar_tensor_tensor, oT, oT, pvc(f"gla_norm_w{l}"), rr, ALU.mult, ALU.mult, w=[tr])
            tm = V(ve.tensor_tensor, merged[:, 0:4, :], oT, gT, ALU.mult, w=[tg])

            b, fw, users = banks.get()
            for g in range(2):
                for t in range(2):
                    s = slice(128 * t, 128 * t + 128)
                    at = 128 * (2 * g + t)
                    tok = P(te.matmul, b[:, at:at + 128], bpad[:, g, s], xc[:, 5, s], start=True, stop=True,
                            w=[tb, *fw])
            for g in range(2):
                for t in range(2):
                    at = 128 * (2 * g + t)
                    tv = V(ve.copy_predicated, gm[:, g, t, :], ms[:, MS["ssd"][0]:MS["ssd"][0] + 128],
                           b[:, at:at + 128], w=[tok])
            users.append(tv)
            for t in range(2):
                b, tok, users = transposes([xc[:, k, 128 * t:128 * t + 128] for k in range(4)], w=[tx])
                users.append(V(ve.tensor_tensor, xdt[:, t], b.rearrange("p (h q) -> p h q", h=8),
                               dc[:, t, 0:8].unsqueeze(2).to_broadcast([128, 8, 64]), ALU.mult, w=[tok]))
            b, tok, users = transposes([xc[:, 4, 0:128]])
            tbt = A(se.activation, btm, b[:, 0:128], ACT.Copy, w=[tok])
            users.append(tbt)
            twx = V(ve.tensor_tensor, wx, xdt[:, 0], fl.unsqueeze(2).to_broadcast([128, 8, 64]), ALU.mult, w=[tf])
            b, fw, users = banks.get(WORK)
            tok = accum(b, [(btm, wx)], w=[twx, tbt, *fw])
            background_end()
            wo = []
            ob = [banks.get([i]) for i in range(4)]
            ov = [ob[m // 2][0][:, 256 * (m % 2):256 * (m % 2) + 256] for m in range(8)]
            for n in range(2):
                tile, tt, tu = wtile(w_out, 512 * n, 512)
                wo.append((tile, tu))
                for m in range(4):
                    mm = 4 * n + m
                    for k in range(4):
                        P(te.matmul, ov[mm], tile[:, k, 128 * m:128 * m + 128], merged[:, k, :],
                          start=(k == 0 and mm % 2 == 0), stop=False, skip_group_check=True,
                          w=[tt, tm, *ob[mm // 2][1]], inc=False)
            for g in range(2):
                r = slice(64 * g, 64 * g + 64)
                ts = V(ve.tensor_copy, s1[r, 4 * g:4 * g + 4, :],
                       b[r, 256 * g:256 * g + 256].rearrange("p (h q) -> p h q", h=4), w=[tok, tz2])
            users.append(ts)
            tce = V(ve.tensor_tensor, ecb, ecb, xc[:, 5, 128:256].unsqueeze(1).to_broadcast([128, 8, 128]),
                    ALU.mult, w=[te_])
            for g in range(2):
                for t in range(2):
                    td = V(ve.tensor_tensor, dec[:, 4 * g:4 * g + 4, t, :], dec[:, 4 * g:4 * g + 4, t, :],
                           gm[:, g, t, :].unsqueeze(1).to_broadcast([128, 4, 128]), ALU.mult, w=[tdec])
            for c in range(4):
                b, fw, users = banks.get(WORK)
                for h in (2 * c, 2 * c + 1):
                    r = slice(64 * (h % 2), 64 * (h % 2) + 64)
                    P(te.matmul, b[r, 0:128], xdt[:, 0, h, :], dec[:, h, 0, :], start=True, stop=True,
                      w=[td, *fw], inc=False)
                    P(te.matmul, b[r, 128:256], xdt[:, 1, h, :], dec[:, h, 1, :], start=True, stop=False,
                      inc=False)
                    tok = P(te.matmul, b[r, 128:256], s1[:, h, :], ecb[:, h, :], start=False, stop=True)
                V(ve.scalar_tensor_tensor, yT[:, c, :], xc[:, c, :], pvc(f"d_skip{l}", c), b[:, 0:256],
                  ALU.mult, ALU.add, w=[tok])
                ty = V(ve.tensor_tensor, yT[:, c, :], yT[:, c, :], zT[:, c, :], ALU.mult)
                users.append(ty)
            sq = v4(xdt_, 4)
            t = A(se.activation, sq, yT, ACT.Square, w=[ty])
            b, fw, users = banks.get(WORK)
            tok = accum(b[:, 0:256], [(ones, sq[:, k, :]) for k in range(4)], w=[t, *fw])
            tr, t0 = rstd_of(b[:, 0:256], 1.0 / 512, 0, rr1, tok)
            users.append(t0)
            for c in range(4):
                tm = V(ve.scalar_tensor_tensor, merged[:, 4 + c, :], yT[:, c, :], pvc(f"ssd_norm_w{l}", c), rr1,
                       ALU.mult, ALU.mult, w=[tr])
            for mm in range(8):
                tile, tu = wo[mm // 4]
                m = mm % 4
                for k in range(4, 8):
                    tok = P(te.matmul, ov[mm], tile[:, k, 128 * m:128 * m + 128], merged[:, k, :],
                            start=False, stop=(k == 7), skip_group_check=True, w=[tm], inc=(k == 7))
                if m == 3:
                    tu.append(tok)
                if mm % 2:
                    for i in (mm - 1, mm):
                        t = V(ve.scalar_tensor_tensor, xT[:, i, :], ov[i], mod[:, 16 + i:17 + i], xT[:, i, :],
                              ALU.mult, ALU.add, w=[tok])
                    ob[mm // 2][2].append(t)

        def acc(m):
            return banks.banks[m // 2][:, 256 * (m % 2):256 * (m % 2) + 256]

        class Down:

            def __init__(self):
                self.first = True
                self.waits = [t for i in range(4) for t in banks.free[i]]
                for i in range(4):
                    banks.free[i] = []

            def add(self, tile, tt, tu, act, ta, last):
                tok = None
                for j in range(4):
                    for m in range(8):
                        tok = P(te.matmul, acc(m), tile[:, j, 128 * m:128 * m + 128], act[:, j, :],
                                start=(self.first and j == 0 and m % 2 == 0), stop=(last and j == 3),
                                skip_group_check=True, w=[tt, ta, *self.waits], inc=(j == 3 and m == 7))
                    self.waits = []
                self.first = False
                tu.append(tok)
                return tok

        def dense_ffn(wg, wu, wd, gate):
            acts = [v4(buf(1024), 4) for _ in range(2)]
            sil = [buf(256) for _ in range(2)]
            down = Down()
            pend = None
            t_act_read = [None, None]
            t_mul = [None, None]
            th = [A.last, V.last]

            def add(last):
                f, a, ta = pend
                dt, td, ud = rtile(wd, 512 * f, 4, D)
                t_act_read[f % 2] = down.add(dt, td, ud, a, ta, last=last)
            for f in range(7):
                gt, tg, ug = wtile(wg, 512 * f, 512)
                ut, tu_, uu = wtile(wu, 512 * f, 512)
                a = acts[f % 2]
                for j in range(4):
                    b, fw, users = banks.get(WORK)
                    c = slice(128 * j, 128 * j + 128)
                    tk1 = accum(b[:, 0:256], [(gt[:, k, c], hT[:, k, :]) for k in range(8)], w=[tg, *th, *fw])
                    tk2 = accum(b[:, 256:512], [(ut[:, k, c], hT[:, k, :]) for k in range(8)], w=[tu_])
                    s = sil[j % 2]
                    t = A(se.activation, s, b[:, 0:256], ACT.Silu, w=[tk2, t_mul[j % 2]])
                    ta = V(ve.tensor_tensor, a[:, j, :], s, b[:, 256:512], ALU.mult, w=[t, t_act_read[f % 2]])
                    t_mul[j % 2] = ta
                    users.append(ta)
                ug.append(tk1)
                uu.append(tk2)
                background(WORK)
                if pend is not None:
                    add(False)
                pend = (f, a, ta)
                background(WORK)
            add(True)
            tok = P.last
            for m in range(8):
                t = V(ve.scalar_tensor_tensor, xT[:, m, :], acc(m), gate[:, m:m + 1], xT[:, m, :],
                      ALU.mult, ALU.add, w=[tok])
            for i in range(4):
                banks.free[i].append(t)

        def moe(gate):
            rw = pvc("router", 0, 64).rearrange("p (k e) -> p k e", k=8)
            htm = v4(buf(2048), 2)
            lg, e8, g8, m8, oh, pos = (buf(16) for _ in range(6))
            ix, fx, sm = buf(16).bitcast(U32), buf(16), buf(8)
            flag = buf(2)
            gath = [buf(256).rearrange("p (t c) -> p t c", t=2) for _ in range(2)]
            scat = buf(512).rearrange("p (e t c) -> p e t c", e=2, t=2)
            pwt = buf(2048).rearrange("p (e t) -> p e t", e=8)
            xg = [v4(buf(1024), 8) for _ in range(2)]
            ysb = buf(8192).rearrange("p (e n) -> p e n", e=8)
            acts = [v4(buf(512), 4) for _ in range(2)]
            sil = [buf(256).rearrange("p (j c) -> p j c", j=2) for _ in range(2)]
            t_h = [A.last, V.last]
            b, fw, users = banks.get()
            for t in range(2):
                tok = accum(b[:, 8 * t:8 * t + 8],
                            [(hT[:, k, 128 * t:128 * t + 128], rw[:, k, :]) for k in range(8)], w=[*t_h, *fw])
            users.append(V(ve.tensor_copy, lg, b[:, 0:16], w=[tok]))
            for t in range(2):
                for q in range(2):
                    b, tok, users = transposes([hT[:, 4 * q + k, 128 * t:128 * t + 128] for k in range(4)])
                    th = A(se.activation, htm[:, t, 512 * q:512 * q + 512], b, ACT.Copy, w=[tok])
                    users.append(th)
            for t in range(2):
                s = slice(8 * t, 8 * t + 8)
                V(ve.max, e8[:, s], lg[:, s])
                V(ve.max_index, ix[:, s], e8[:, s], lg[:, s])
                V(ve.tensor_copy, fx[:, s], ix[:, s])
                tv = V(ve.tensor_tensor, sm[:, 4 * t:4 * t + 1], e8[:, 8 * t + 1:8 * t + 2], e8[:, 8 * t:8 * t + 1],
                       ALU.subtract)
                ta = A(se.activation, sm[:, 4 * t + 1:4 * t + 2], sm[:, 4 * t:4 * t + 1], ACT.Exp, w=[tv])
                V(ve.tensor_scalar, m8[:, s], cst("iota8"), fx[:, 8 * t:8 * t + 1], None, ALU.is_equal)
                V(ve.tensor_scalar, oh[:, s], cst("iota8"), fx[:, 8 * t + 1:8 * t + 2], None, ALU.is_equal)
                V(ve.tensor_scalar, sm[:, 4 * t:4 * t + 1], sm[:, 4 * t + 1:4 * t + 2], 1.0, None, ALU.add, w=[ta])
                V(ve.reciprocal, sm[:, 4 * t + 2:4 * t + 3], sm[:, 4 * t:4 * t + 1])
                V(ve.tensor_tensor, sm[:, 4 * t + 3:4 * t + 4], sm[:, 4 * t + 1:4 * t + 2],
                  sm[:, 4 * t + 2:4 * t + 3], ALU.mult)
                V(ve.tensor_scalar, g8[:, s], m8[:, s], sm[:, 4 * t + 2:4 * t + 3], None, ALU.mult)
                V(ve.scalar_tensor_tensor, g8[:, s], oh[:, s], sm[:, 4 * t + 3:4 * t + 4], g8[:, s],
                  ALU.mult, ALU.add)
                tm = V(ve.tensor_tensor, m8[:, s], m8[:, s], oh[:, s], ALU.add)
            b, fw, users = banks.get()
            accum(b[:, 0:8], [(cst("tri"), m8[:, 0:8])], w=[tm, *fw])
            accum(b[:, 8:16], [(ones, m8[:, 0:8]), (cst("tri"), m8[:, 8:16])])
            tok = accum(b[:, 16:24], [(ones, m8[:, 0:8]), (ones, m8[:, 8:16])])
            V(ve.tensor_copy, fx, b[:, 0:16], w=[tok])
            V(ve.scalar_tensor_tensor, pos, fx, 1.0, m8, ALU.add, ALU.mult)
            V(ve.tensor_scalar, pos, pos, -1.0, None, ALU.add)
            users.append(V(ve.tensor_reduce, flag[:, 0:1], b[:, 16:24], AX.X, ALU.max))
            flag_at[0] = flag[0:1, 1:2].bitcast(I32)
            t_flag = V(ve.tensor_scalar, flag[:, 1:2].bitcast(I32), flag[:, 0:1], 128.0, None, ALU.is_gt)

            def one_pass(first):
                if not first:
                    V(ve.tensor_scalar, pos, pos, -128.0, None, ALU.add)
                for e2 in range(4):
                    for i in range(2):
                        e = 2 * e2 + i
                        for t in range(2):
                            tv = V(ve.tensor_scalar, scat[:, i, t, :], cst("iota"), pos[:, 8 * t + e:8 * t + e + 1],
                                   g8[:, 8 * t + e:8 * t + e + 1], ALU.is_equal, ALU.mult, w=[P.last])
                    b, tok, users = transposes([scat[:, i, t, :] for i in range(2) for t in range(2)], w=[tv])
                    tpw = V(ve.tensor_copy, pwt[:, 2 * e2:2 * e2 + 2, :], b.rearrange("p (e t) -> p e t", e=2),
                            w=[tok])
                    users.append(tpw)
                t_gath = [None, None]
                t_xg = [None, None]
                t_xg_read = [None, None]

                def onehots(e):
                    for t in range(2):
                        tv = V(ve.tensor_scalar, gath[e % 2][:, t, :], cst("iota"), pos[:, 8 * t + e:8 * t + e + 1],
                               None, ALU.is_equal, w=[t_gath[e % 2]])
                    return tv

                def gather(e, tv):
                    for q in range(2):
                        b, fw, users = banks.get(WORK)
                        for m in range(4):
                            mm = 4 * q + m
                            tok = accum(b[:, 128 * m:128 * m + 128],
                                        [(htm[:, t, 128 * mm:128 * mm + 128], gath[e % 2][:, t, :])
                                         for t in range(2)], w=[tv, th, *fw])
                        ta = A(se.activation, xg[e % 2][:, 4 * q:4 * q + 4, :], b.rearrange("p (m c) -> p m c", m=4),
                               ACT.Copy, w=[tok, t_xg_read[e % 2]])
                        users.append(ta)
                    t_gath[e % 2] = tok
                    t_xg[e % 2] = ta
                gather(0, onehots(0))
                t_act_read = [None, None]
                t_mul = [None, None]
                ywait = [[t for i in (2 * p, 2 * p + 1) for t in banks.free[i]] for p in range(2)]
                for i in range(4):
                    banks.free[i] = []
                pend = None
                ty = None

                def down(e, f, a, ta):
                    wd = T["moe_w_down"][e]
                    dt, td, ud = rtile(wd, 512 * f, 4, D)
                    for j in range(4):
                        for h in range(2):
                            tok = P(te.matmul, banks.banks[2 * (e % 2) + h], a[:, j, :],
                                    dt[:, j, 512 * h:512 * h + 512], start=(f == 0 and j == 0),
                                    stop=(f == 6 and j == 3), w=[td, ta, *(ywait[e % 2] if f == 0 else [])],
                                    inc=(j == 3 and h == 1))
                    ud.append(tok)
                    t_act_read[f_of[0] % 2] = tok
                    if f < 6:
                        return None
                    for h in range(2):
                        t = A(se.activation, ysb[:, e, 512 * h:512 * h + 512], banks.banks[2 * (e % 2) + h], ACT.Copy,
                              w=[tok])
                    ywait[e % 2] = [t]
                    return t
                f_of = [0]
                i = 0
                for e in range(8):
                    x = xg[e % 2]
                    for f in range(7):
                        gt, tg, ug = wtile(T["moe_w_gate"][e], 512 * f, 512)
                        ut, tu_, uu = wtile(T["moe_w_up"][e], 512 * f, 512)
                        a = acts[i % 2]
                        if f == 3 and e < 7:
                            toh = onehots(e + 1)
                        for p in range(2):
                            b, fw, users = banks.get(WORK)
                            v = b.rearrange("p (j u c) -> p j u c", j=2, u=2)
                            for j in range(2):
                                c = slice(128 * (2 * p + j), 128 * (2 * p + j) + 128)
                                tk1 = accum(v[:, j, 0, :], [(gt[:, k, c], x[:, k, :]) for k in range(8)],
                                            w=[tg, t_xg[e % 2], *fw])
                                tk2 = accum(v[:, j, 1, :], [(ut[:, k, c], x[:, k, :]) for k in range(8)], w=[tu_])
                            s = sil[p]
                            t = A(se.activation, s, v[:, :, 0, :], ACT.Silu, w=[tk2, t_mul[p]])
                            ta = V(ve.tensor_tensor, a[:, 2 * p:2 * p + 2, :], s, v[:, :, 1, :], ALU.mult,
                                   w=[t, t_act_read[i % 2]])
                            t_mul[p] = ta
                            users.append(ta)
                        ug.append(tk1)
                        uu.append(tk2)
                        if f == 6:
                            t_xg_read[e % 2] = tk2
                        if pend is not None:
                            f_of[0] = i - 1
                            down(*pend)
                        if f == 4 and e < 7:
                            gather(e + 1, toh)
                        pend = (e, f, a, ta)
                        i += 1
                        if first:
                            background(WORK)
                f_of[0] = i - 1
                ty = down(*pend)
                for i in range(4):
                    banks.free[i].append(ty)
                for p in range(4):
                    b, fw, users = banks.get()
                    for j in range(2):
                        m = 2 * p + j
                        tok = accum(b[:, 256 * j:256 * j + 256],
                                    [(ysb[:, e, 128 * m:128 * m + 128], pwt[:, e, :]) for e in range(8)],
                                    w=[ty, tpw, *fw])
                    for j in range(2):
                        m = 2 * p + j
                        t = V(ve.scalar_tensor_tensor, xT[:, m, :], b[:, 256 * j:256 * j + 256], gate[:, m:m + 1],
                              xT[:, m, :], ALU.mult, ALU.add, w=[tok])
                    users.append(t)

            one_pass(True)
            background_end()
            everyone()
            SP.wait([x.last for x in (P, V, A, G)])
            for q, n in ring.sems:
                SP.wait([(q, n)])
            engines = (P, V, A, SP)
            before = [(x.n, dict(x.seen), x.queue) for x in engines]
            rings = [n for _, n in ring.sems]
            for x in engines:
                x.queue = []
            one_pass(False)
            everyone_but_pool()
            for x, (n, seen, queue) in zip(engines, before):
                taken, adds = x.queue, [(x.sem, x.n - n)]
                if x is SP:
                    adds = [(q, n1 - n0) for (q, n1), n0 in zip(ring.sems, rings)]
                queue.append(lambda x=x, taken=taken, adds=adds: branch(x, taken, adds))
                x.queue, x.seen = queue, seen

        def branch(x, taken, adds):
            with x.e.If(x.e.value_load(flag_at[0], min_val=0, max_val=1)):
                x.emit(taken)
            with x.e.Else():
                for q, n in adds:
                    if n:
                        x.e.sem_inc(q, n)

        flag_at = [None]

        def finish():
            everyone()
            SP.wait([x.last for x in (P, V, A, G)])
            SP.dma(T["out"].rearrange("(k p) t -> p k t", p=128), xT, s_out)
            SP.wait([(s_out, 16)])
            block = ctx.enter_context(nc.Block())
            block.tensor(lambda e: P.emit())
            block.vector(lambda e: V.emit())
            block.scalar(lambda e: A.emit())
            block.gpsimd(lambda e: G.emit())
            block.sync(lambda e: SP.emit())

        t_s = A(se.activation, small[:, 0:8], pvc("c", 0, 8), ACT.Silu)
        t_s2 = A(se.activation, small[:, 8:24], pvc("c2", 0, 16), ACT.Silu)
        m2 = mods[:, 96:192].rearrange("p (c m) -> p c m", c=2)

        def ada_layer(l, tiles):
            return [ada_tile(T["ada_w"][l], n, small[:, 0:8], 1, 1, f"ada_b{l}", [mods[:, 48 * l:48 * l + 48]], t_s)
                    for n in tiles]

        Background.todo = ada_layer(0, range(12))
        for l in range(2):
            fresh()
            mod = mods[:, 48 * l:48 * l + 48]
            scr = arena[:, ARENA - 2312:ARENA]
            tr = norm_stats(xT, [V.last, t_x], scr)
            while len(Background.todo) > (8 if l == 0 else 0):
                background()
            background()
            th = norm_apply(xT, pvc(f"norm1_w{l}", 0, 8), mod[:, 8:16], mod[:, 0:8], hT, tr, scr)
            mixer(l, mod, th)
            if STOP == f"mix{l}":
                return finish()
            fresh()
            norm_mod(xT, pvc(f"norm2_w{l}", 0, 8), mod[:, 32:40], mod[:, 24:32], hT, [V.last], scr)
            if l == 0:
                Background.todo = ada_layer(1, range(12))
                dense_ffn(T["ffn_w_gate"], T["ffn_w_up"], T["ffn_w_down"], mod[:, 40:48])
                background_end()
            else:
                Background.todo = [
                    ada_tile(T["w_ada"], n, small[:, 8:24], 2, 2 if n < 4 else 1, "b_ada", [m2[:, 0, :], m2[:, 1, :]],
                             t_s2) for n in range(12)]
                moe(mod[:, 40:48])
            if STOP == f"ffn{l}":
                return finish()
        fresh()
        norm_mod(xT, pvc("final_w", 0, 8), None, None, xT, [V.last], scr)
        if STOP == "first":
            return finish()

        limit[0] = ARENA - NHC
        mod, modc = m2[:, 0, :], m2[:, 1, :]
        fresh()
        qn, kn, kc = v4(buf(1024), 4), v4(buf(1024), 4), v4(buf(1024), 4)
        v_tm, vc_tm = v4(buf(1024), 2), v4(buf(1024), 2)
        ctx_ = buf(2048)
        ctxT = v4(ctx_, 8)
        zs = buf(13 * 258)
        zh = zs[:, 258:13 * 258].rearrange("p (k t) -> p k t", k=12)
        zc = zs[:, 0:12 * 258].rearrange("p (k t) -> p k t", k=12)[:, :, 0:256]
        filt = buf(4096)
        kre = [[filt[:, 1024 * o + 512 * k:1024 * o + 512 * k + 512] for k in range(2)] for o in range(2)]
        kim = [[filt[:, 2048 + 1024 * o + 512 * k:2048 + 1024 * o + 512 * k + 512] for k in range(2)]
               for o in range(2)]
        fb_ = buf(2048)
        fb = [fb_[:, 512 * i:512 * i + 512] for i in range(4)]
        rn, tmp, hab = buf(512), buf(512), buf(512)
        ha, hb = hab[:, 0:256], hab[:, 256:512]
        SP.wait([x.last for x in (P, V, A, G)])
        s_ctx = sem("s_ctx")
        s_hc = sem("s_hc")
        SP.dma(hc, T["hc"], s_hc)
        SP.dma(ctxT, T["ctxT"].rearrange("(k p) t -> p k t", p=128), s_ctx)
        t_hc = (s_hc, 16)
        scr = zs[:, 0:2312]
        scrc = arena[:, Arena.at - 2312:Arena.at]
        th = norm_mod(xT, pvc("norm1_g", 0, 8), mod[:, 8:16], mod[:, 0:8], hT, [V.last], scrc)
        tz = G(ge.memset, zh[:, :, 0:1], 0.0)
        tz = G(ge.memset, zh[:, :, 257:258], 0.0)
        w_in = T["w_in2"]
        pieces = []

        def fill(n=1):
            for _ in range(min(n, len(pieces))):
                pieces.pop(0)()

        def queue_proj(w, c0, rhs, wt_, take, take2=None, rhs2=None, wt2=None):
            held = {}

            def piece(i, r, w_, tk):
                def f():
                    if i == 0:
                        held["tile"] = wtile(w, c0, 512)
                    tile, tt, tu = held["tile"]
                    m0 = 2 * (i % 2)
                    b, fw, users = banks.get(held.get("among"))
                    for j in range(2):
                        c = 128 * (m0 + j)
                        tok = accum(b[:, 256 * j:256 * j + 256],
                                    [(tile[:, k, c:c + 128], r[:, k, :]) for k in range(8)],
                                    w=[tt, w_[0], *fw], inc=(j == 1))
                    users.append(tk(v4(b, 2), m0, 2, tok))
                    if i == (1 if rhs2 is None else 3):
                        tu.append(tok)
                return f
            for i in range(2):
                pieces.append(piece(i, rhs, wt_, take))
            if rhs2 is not None:
                for i in range(2, 4):
                    pieces.append(piece(i, rhs2, wt2, take2))

        def queue_proj_tm(w, c0, jobs, bias):
            held = {}

            def piece(n, t, r, w_, dst):
                def f():
                    if n == 0 and t == 0:
                        held["tile"] = wtile(w, c0, 512)
                    tile, tt, tu = held["tile"]
                    b, fw, users = banks.get()
                    tok = accum(b, [(r[:, k, 128 * t:128 * t + 128], tile[:, k, 0:512]) for k in range(8)]
                                + [(ones[0:1, :], bias)], w=[tt, w_[0], *fw])
                    users.append(A(se.activation, dst[:, t, :], b, ACT.Copy, w=[tok]))
                    if n == len(jobs) - 1 and t == 1:
                        tu.append(tok)
                return f
            for n, (r, w_, dst) in enumerate(jobs):
                for t in range(2):
                    pieces.append(piece(n, t, r, w_, dst))

        def biased(dst, col):
            def take(b, m0, n, tok):
                for j in range(n):
                    t = A(se.activation, dst[:, m0 + j, :], b[:, j, :], ACT.Identity,
                          bias=pvc("b_in", col + m0 + j), w=[tok])
                return t
            return take

        thw, thcw = [th], [None]
        for n in range(3):
            queue_proj(w_in, 512 * n, hT, thw, biased(zh[:, 4 * n:4 * n + 4, 1:257], 4 * n))
        queue_proj(w_in, 1536, hT, thw, biased(qn, 12))
        queue_proj(w_in, 2048, hT, thw, biased(kn, 16), biased(kc, 16), ctxT, thcw)
        queue_proj_tm(w_in, 2560, [(hT, thw, v_tm), (ctxT, thcw, vc_tm)], pvc("bv", 0, 512, rows=1))
        fill(1)

        thcw[0] = norm_mod(ctxT, pvc("norm1_g", 0, 8), modc[:, 8:16], modc[:, 0:8], ctxT,
                           [(s_ctx, 16), V.last], scrc)
        everyone()

        src, t = hcc("feats", rows=33), t_hc
        for i, (wname, bname, rows) in enumerate((("f1w", "f1b", 33), ("f2w", "f2b", 64), ("f3w", "f3b", 64))):
            b, fw, users = banks.get()
            tok = accum(b[0:64, 0:256], [(pvc(wname, 0, 64, rows=rows), src)], w=[t, t_wide, *fw])
            x, y = ha[0:64, :], hb[0:64, :]
            users.append(V(ve.tensor_scalar, x, b[0:64, 0:256], pvc(bname, rows=64), pvc("freq", rows=64),
                           ALU.add, ALU.mult, w=[tok]))
            V(ve.tensor_scalar, y, x, 1.0 / (2 * math.pi), 12582912.0, ALU.mult, ALU.add)
            V(ve.tensor_scalar, y, y, 12582912.0, None, ALU.subtract)
            p1, p2 = 6.28125, 0.0019350051879882812
            p3 = 2 * math.pi - p1 - p2
            for part in (p1, p2, p3):
                V(ve.scalar_tensor_tensor, x, y, -part, x, ALU.mult, ALU.add)
            V(ve.tensor_scalar, x, x, 3.1415925, -3.1415925, ALU.min, ALU.max)
            t = A(se.activation, x, x, ACT.Sin, w=[V.last])
            src = x
            fill(1)
        tsin = t

        f4, tf4, uf4 = ring.load(lambda base_: [(base_[0:64, 0:2048], T["f4w"])])
        dec_t = hcc("dec").rearrange("p (t c) -> p t c", t=2)
        DC, DS, DCI, DSI = (v4(hcc(n), 2) for n in ("C", "S", "CI", "SI"))
        V.wait([t_hc])
        for o in range(2):
            for dr in range(2):
                for t in range(2):
                    b, fw, users = banks.get()
                    c0 = 1024 * o + 512 * dr
                    tok = accum(b, [(ha[0:64, 128 * t:128 * t + 128], f4[0:64, c0:c0 + 512])],
                                w=[tf4, tsin, *fw])
                    tv = V(ve.tensor_tensor, fb[2 * dr + t], b, dec_t[:, t, :], ALU.mult, w=[tok])
                    users.append(tv)
            if o == 1:
                uf4.append(tok)
            fill(1)
            b, fw, users = banks.get()
            for i in range(4):
                ab = A(se.activation, (tmp, rn)[i % 2], fb[i], ACT.Abs, w=[tv, P.last])
                tok = P(te.matmul, b, ones, (tmp, rn)[i % 2], start=(i == 0), stop=(i == 3), w=[ab, *fw])
            users.append(V(ve.reciprocal, rn, b, w=[tok]))
            V(ve.memset, fb[2][0:1, :], 0.0)
            for t in range(2):
                V(ve.tensor_tensor, tmp, fb[t], fb[2 + t], ALU.add)
                V(ve.tensor_tensor, fb[2 + t], fb[2 + t], fb[t], ALU.subtract)
                tv = V(ve.tensor_copy, fb[t], tmp)
            fill(1)
            for k in range(2):
                s = slice(128 * k, 128 * k + 128)
                for dst, mat, x in ((kre, DC, 0), (kim, DS, 2)):
                    b, fw, users = banks.get()
                    tok = accum(b, [(mat[:, t, s], fb[x + t]) for t in range(2)], w=[tv, t_hc, *fw])
                    users.append(V(ve.tensor_tensor, dst[o][k], b, rn, ALU.mult, w=[tok]))
        if STOP == "proj2":
            return finish()

        while len(pieces) > 9:
            fill(1)
        tzh = A.last
        for k in range(12):
            V(ve.tensor_scalar, zc[:, k, :], zh[:, k, 0:256], pvc("hcw", k), pvc("hcb", k), ALU.mult, ALU.add,
              w=[tz, tzh])
            for j in range(1, 3):
                tv = V(ve.scalar_tensor_tensor, zc[:, k, :], zh[:, k, j:j + 256], pvc("hcw", 12 * j + k),
                       zc[:, k, :], ALU.mult, ALU.add)
            if k == 3:
                tz03 = tv
            if k % 4 == 3:
                fill(1)
        y_tm = [rn, hab]
        yre, yim = v4(fb_[:, 0:1024], 2), v4(fb_[:, 1024:2048], 2)
        for o in range(2):
            for t in range(2):
                b, tok, users = transposes([zc[:, c, 128 * t:128 * t + 128] for c in range(4)],
                                           w=[tz03 if o == 0 else V.last])
                ty = V(ve.tensor_copy, y_tm[t], b, w=[tok])
                users.append(ty)
            for k in range(2):
                s = slice(128 * k, 128 * k + 128)
                br, fw, ur = banks.get()
                tok = accum(br, [(DC[:, t, s], y_tm[t]) for t in range(2)], w=[ty, *fw])
                bi, fw, ui = banks.get()
                tok = accum(bi, [(DS[:, t, s], y_tm[t]) for t in range(2)], w=[ty, *fw])
                V(ve.tensor_tensor, yre[:, k, :], br, kre[o][k], ALU.mult, w=[tok])
                V(ve.tensor_tensor, tmp, bi, kim[o][k], ALU.mult)
                V(ve.tensor_tensor, yre[:, k, :], yre[:, k, :], tmp, ALU.add)
                V(ve.tensor_tensor, yim[:, k, :], br, kim[o][k], ALU.mult)
                tv = V(ve.tensor_tensor, tmp, bi, kre[o][k], ALU.mult)
                ur.append(tv)
                ui.append(tv)
                tv = V(ve.tensor_tensor, yim[:, k, :], yim[:, k, :], tmp, ALU.subtract)
                fill(1)
            fill(1)
            for c in range(4):
                s = slice(128 * c, 128 * c + 128)
                b, fw, users = banks.get()
                tok = accum(b[:, 0:256], [(yre[:, k, s], DCI[:, k, :]) for k in range(2)]
                            + [(yim[:, k, s], DSI[:, k, :]) for k in range(2)], w=[tv, *fw])
                users.append(V(ve.scalar_tensor_tensor, zc[:, c, :], zc[:, c, :], pvc("skip", 4 * o + c),
                               b[:, 0:256], ALU.mult, ALU.add, w=[tok]))
                V(ve.tensor_tensor, zc[:, c, :], zc[:, c, :], zc[:, 4 + 4 * o + c, :], ALU.mult)
        fill(len(pieces))
        if STOP == "hyena":
            return finish()

        everyone()
        gate = v4(filt, 16)
        kp = v4(zs[:, 4 * 258:4 * 258 + 2048], 8)
        kcp = v4(fb_, 8)
        yna = v4(ctx_[:, 0:1024], 4)
        sq = v4(ctx_[:, 1024:2048], 4)
        rr = v4(arena[:, ARENA - NHC:ARENA - NHC + 1024], 4)
        hct = arena[:, ARENA - NHC + 1024:ARENA - NHC + 2048]
        tmpb, st = hct[:, 0:256], hct[:, 256:264]
        for n in range(4):
            queue_proj(w_in, 3072 + 512 * n, hT, thw, biased(gate[:, 4 * n:4 * n + 4, :], 24 + 4 * n))
        G(ge.memset, kp, 0.0)
        tz = G(ge.memset, kcp, 0.0)
        for x, g in ((qn, "qg"), (kn, "kg"), (kc, "kg")):
            t = A(se.activation, sq, x, ACT.Square, w=[V.last, P.last])
            for p in range(2):
                b, fw, users = banks.get()
                tok = accum(b, [(bones, sq[:, 2 * p:2 * p + 2, :])], w=[t, *fw])
                tr, t0 = rstd_of(b.rearrange("p (k t) -> p k t", k=2), 1.0 / 64, 0, rr[:, 2 * p:2 * p + 2, :], tok)
                users.append(t0)
            fill(1)
            tv = V(ve.scalar_tensor_tensor, x, x, pvc(g), rr, ALU.mult, ALU.mult, w=[tr])
            if x is not kc:
                rc, rs = hcc("ropeC"), hcc("ropeS")
                for p in range(2):
                    b, fw, users = banks.get()
                    xx = x[:, 2 * p:2 * p + 2, :]
                    tok = accum(b, [(cst("perm"), xx)], w=[tv, *fw])
                    tv2 = V(ve.tensor_tensor, rr[:, 2 * p:2 * p + 2, :], b.rearrange("p (k t) -> p k t", k=2),
                            rs.unsqueeze(1).to_broadcast([128, 2, 256]), ALU.mult, w=[tok])
                    users.append(tv2)
                    V(ve.tensor_tensor, xx, xx, rc.unsqueeze(1).to_broadcast([128, 2, 256]), ALU.mult)
                    tv = V(ve.tensor_tensor, xx, xx, rr[:, 2 * p:2 * p + 2, :], ALU.add)
        for h in range(8):
            r = slice(64 * (h % 2), 64 * (h % 2) + 64)
            V(ve.tensor_copy, kp[r, h, :], kn[r, h // 2, :], w=[tz])
            tkp = A(se.activation, kcp[r, h, :], kc[r, h // 2, :], ACT.Copy, w=[tz, tv])
        tkp2 = V.last
        V.wait([tkp])
        A.wait([tkp2])
        sc = [kn.rearrange("p k t -> p (k t)")[:, 0:512], kn.rearrange("p k t -> p (k t)")[:, 512:1024]]
        pt = [kc.rearrange("p k t -> p (k t)")[:, 0:512], kc.rearrange("p k t -> p (k t)")[:, 512:1024]]
        for s in sc:
            V(ve.memset, s[:, 0:256], -1.0e30)
        bias_b, tbias, ubias = ring.load(lambda base_: [(base_[:, 0:4096], T["bias"])])
        biasv = bias_b[:, 0:4096].rearrange("p (t h k) -> p t h k", t=2, h=8)
        mcol = ms[:, MS["col"][0]:MS["col"][0] + 256]
        its = [(h, t) for h in range(8) for t in range(2)]
        def scores(i):
            h, t = its[i]
            b, fw, users = banks.get()
            q = qn[:, h // 2, 128 * t:128 * t + 128]
            P(te.matmul, b[:, 0:256], q, kp[:, h, :], start=True, stop=True, w=[tkp, tkp2, *fw], inc=False)
            tok = P(te.matmul, b[:, 256:512], q, kcp[:, h, :], start=True, stop=True)
            return b, tok, users

        cur = scores(0)
        t_pt = [None, None]
        for i, (h, t) in enumerate(its):
            b, tok, users = cur
            s, p_ = sc[i % 2], pt[i % 2]
            t_ctx = A(se.activation, s[:, 256:512], b[:, 256:512], ACT.Copy, scale=0.125, w=[tok])
            V(ve.scalar_tensor_tensor, tmpb, b[:, 0:256], 0.125, biasv[:, t, h, :], ALU.mult, ALU.add,
              w=[t_ctx, tbias])
            users.append(V.last)
            V(ve.copy_predicated, s[:, 0:256], mcol, tmpb)
            c3 = 4 * (i % 2)
            tv = V(ve.tensor_reduce, st[:, c3:c3 + 1], s, AX.X, ALU.max, negate=True)
            ta = A(se.activation, p_, s, ACT.Exp, bias=st[:, c3:c3 + 1], accum_out=st[:, c3 + 1:c3 + 2],
                   w=[tv, t_pt[i % 2]])
            V(ve.reciprocal, st[:, c3 + 2:c3 + 3], st[:, c3 + 1:c3 + 2], w=[ta])
            tp = V(ve.tensor_scalar, p_, p_, st[:, c3 + 2:c3 + 3], None, ALU.mult)
            if i + 1 < len(its):
                cur = scores(i + 1)
            if i % 3 == 0:
                fill(1)
            bt, tok, ut = transposes([p_[:, 128 * k:128 * k + 128] for k in range(4)], w=[tp])
            ta = A(se.activation, p_, bt, ACT.Copy, w=[tok])
            ut.append(ta)
            yb, fwy, uy = banks.get()
            r = slice(64 * (h % 2), 64 * (h % 2) + 64)
            vs = [v_tm[:, 0, :], v_tm[:, 1, :], vc_tm[:, 0, :], vc_tm[:, 1, :]]
            for k in range(4):
                tok = P(te.matmul, yb[r, 0:128], vs[k][:, 64 * h:64 * h + 64],
                        p_[:, 128 * k:128 * k + 128], start=(k == 0), stop=(k == 3), w=[ta, *fwy], inc=(k == 3))
            t_pt[i % 2] = tok
            tyn = A(se.activation, yna[r, h // 2, 128 * t:128 * t + 128], yb[r, 0:128], ACT.Copy, w=[tok])
            uy.append(tyn)
        ubias.append(V.last)
        fill(len(pieces))
        tsg = A(se.activation, filt, filt, ACT.Sigmoid)

        def half_merge(w, src, base_k, tsrc):
            for n in range(2):
                def parts(base_, n=n):
                    v = base_[:, 0:2048].rearrange("p (k n) -> p k n", k=4)
                    return [(v, w[:, 512 * n:512 * n + 512].rearrange("(k p) n -> p k n", p=128))]
                base_, tt, tu = ring.load(parts)
                wt = base_[:, 0:2048].rearrange("p (k n) -> p k n", k=4)
                for p in range(2):
                    b, fw, users = banks.get()
                    for j in range(2):
                        m = 2 * p + j
                        tok = accum(b[:, 256 * j:256 * j + 256],
                                    [(wt[:, k, 128 * m:128 * m + 128], src[:, k, :]) for k in range(4)],
                                    w=[tt, tsrc, *fw])
                    m = base_k + 4 * n + 2 * p
                    tm = V(ve.tensor_tensor, gate[:, m:m + 2, :], gate[:, m:m + 2, :], v4(b, 2), ALU.mult,
                           w=[tok, tsg])
                    users.append(tm)
                    if base_k:
                        tm = V(ve.tensor_tensor, gate[:, m - 8:m - 6, :], gate[:, m - 8:m - 6, :],
                               gate[:, m:m + 2, :], ALU.add)
                tu.append(tok)
            return tm
        half_merge(T["w_hy"], zc, 0, tkp2)
        tm = half_merge(T["w_na"], yna, 8, tyn)
        for n in range(2):
            tile, tt, tu = wtile(T["w_out2"], 512 * n, 512)
            proj(tile, tt, tu, 0, 4, gate, [tm], residual(0, mod[:, 16:24], 4 * n))
        if STOP == "mix2":
            return finish()

        fresh()
        limit[0] = ARENA
        NSL = 9
        slots = [v4(buf(1024), 4) for _ in range(NSL)]
        region = Arena.at
        scr = arena[:, region:region + 2312]
        th = norm_mod(xT, pvc("norm2_g", 0, 8), mod[:, 32:40], mod[:, 24:32], hT, [V.last], scr)
        wgt = buf(8192).rearrange("p (i t) -> p i t", i=32)
        ojs = [buf(1024).bitcast(BF16).rearrange("p (t j) -> p t j", t=16) for _ in range(2)]
        ois = [buf(768).bitcast(BF16).rearrange("p (t q i) -> p t q i", t=16, q=3) for _ in range(2)]
        kept = Arena.at
        i01 = buf(256).bitcast(BF16).rearrange("p (q t) -> p q t", q=2)
        gp = buf(384).bitcast(BF16).rearrange("p (t q) -> p t q", q=3)
        work = [region]

        def wb(n):
            a = work[0]
            work[0] += n
            assert work[0] <= kept
            return arena[:, a:a + n]

        qt_ = wb(4096)
        qt = v4(qt_, 16)
        sbufs = [wb(2048).rearrange("p (g n) -> p g n", g=16) for _ in range(2)]
        cand = wb(2048).rearrange("p (h n) -> p h n", h=8)
        tv16 = wb(256).rearrange("p (g k) -> p g k", g=16)
        ti16 = wb(256).bitcast(U32).rearrange("p (g k) -> p g k", g=16)
        tif = wb(256).rearrange("p (g k) -> p g k", g=16)
        bs = wb(128).rearrange("p (h k) -> p h k", h=8)
        bp = wb(128).bitcast(U32).rearrange("p (h k) -> p h k", h=8)
        pa = wb(128).bitcast(U32).rearrange("p (h k) -> p h k", h=8)
        pf = wb(128).rearrange("p (h k) -> p h k", h=8)
        iotab = accb[:, 0:64].bitcast(BF16)
        eqb = accb[:, 64:320].bitcast(BF16).rearrange("p (t i) -> p t i", t=16)
        res = [accb[:, 320 + 128 * i:448 + 128 * i] for i in range(3)]
        sm = res[0][:, 0:16]
        eq = qt_[:, 0:2048].rearrange("p (h k a) -> p h k a", h=8, k=16)
        gt3 = qt_[:, 2048:2432]
        for n in range(4):
            tile, tt, tu = wtile(T["w_pq"], 512 * n, 512)
            proj(tile, tt, tu, 0, 4, hT, [th], copy_to(qt[:, 4 * n:4 * n + 4, :], "A"))
        tq = A.last
        keys, tkeys, ukeys = ring.load(lambda base_: [(base_[:, 0:2048], T["keysT"])])
        t_sc = [None, None]
        for t in range(2):
            for g4 in range(4):
                b, fw, users = banks.get()
                for j in range(4):
                    g = 4 * g4 + j
                    tok = P(te.matmul, b[:, 128 * j:128 * j + 128], qt[:, g, 128 * t:128 * t + 128],
                            keys[:, 128 * g:128 * g + 128], start=True, stop=True, w=[tq, tkeys, *fw])
                t_sc[t] = A(se.activation, sbufs[t][:, 4 * g4:4 * g4 + 4, :],
                            b.rearrange("p (g n) -> p g n", g=4), ACT.Copy, w=[tok])
                users.append(t_sc[t])
        ukeys.append(tok)
        tkq = tok
        down = Down()
        t_slot = [None] * NSL
        t_gelu = [None] * 32
        t_mult = [None] * 32
        t_w = [None]

        def first_half(i):
            ut, tt, tu = wtile(T["uT"], 512 * i, 512)
            a = slots[i % NSL]
            for p in range(2):
                b, fw, users = banks.get(WORK)
                for j in range(2):
                    c = slice(128 * (2 * p + j), 128 * (2 * p + j) + 128)
                    tok = accum(b[:, 256 * j:256 * j + 256], [(ut[:, k, c], hT[:, k, :]) for k in range(8)],
                                w=[tt, th, *fw])
                ta = A(se.activation, a[:, 2 * p:2 * p + 2, :], b.rearrange("p (m t) -> p m t", m=2), ACT.Gelu,
                       w=[tok, t_slot[i % NSL]])
                users.append(ta)
            tu.append(tok)
            t_gelu[i] = ta

        def second_half(i):
            vt, tt, tu = rtile(T["v"], 512 * i, 4, D)
            t_slot[i % NSL] = down.add(vt, tt, tu, slots[i % NSL], t_mult[i], last=(i == 31))

        def top16(vals, out_v, out_i, w=()):
            V(ve.max, out_v[:, 0:8], vals, w=w)
            V(ve.max_index, out_i[:, 0:8], out_v[:, 0:8], vals)
            V(ve.match_replace, vals, out_v[:, 0:8], vals, BIG)
            V(ve.max, out_v[:, 8:16], vals)
            V(ve.max_index, out_i[:, 8:16], out_v[:, 8:16], vals)

        def choose(t):
            sb_ = sbufs[t]
            for g in range(16):
                top16(sb_[:, g, :], tv16[:, g, :], ti16[:, g, :], w=[t_sc[t]])
            V(ve.tensor_copy, tif, ti16)
            for h in range(8):
                V(ve.tensor_tensor, cand[:, h, :].rearrange("p (a b) -> p a b", a=16),
                  tv16[:, 2 * h, :].unsqueeze(2).to_broadcast([128, 16, 16]),
                  tv16[:, 2 * h + 1, :].unsqueeze(1).to_broadcast([128, 16, 16]), ALU.add)
                top16(cand[:, h, :], bs[:, h, :], bp[:, h, :])
            tr4 = tif.rearrange("p (h q) k -> p h q k", q=2)
            g3 = res[2].rearrange("p (h k) -> p h k", h=8)
            tv = V(ve.tensor_tensor, g3, bs, bs[:, :, 0:1].to_broadcast([128, 8, 16]), ALU.subtract,
                   w=[P.last if t else tkq])
            ta = A(se.activation, g3, g3, ACT.Exp, w=[tv])
            V(ve.tensor_reduce, sm[:, 0:8], g3, AX.X, ALU.add, w=[ta])
            V(ve.reciprocal, sm[:, 8:16], sm[:, 0:8])
            V(ve.tensor_tensor, g3, g3, sm[:, 8:16].unsqueeze(2).to_broadcast([128, 8, 16]), ALU.mult)
            for q, (sv, op) in enumerate(((4, ALU.logical_shift_right), (15, ALU.bitwise_and))):
                V(ve.tensor_scalar, pa, bp, sv, None, op)
                V(ve.tensor_copy, pf, pa)
                for h in range(8):
                    V(ve.tensor_tensor, eq[:, h], pf[:, h, :].unsqueeze(2).to_broadcast([128, 16, 16]),
                      cst("iota16").unsqueeze(1).to_broadcast([128, 16, 16]), ALU.is_equal)
                    V(ve.tensor_tensor, eq[:, h], eq[:, h],
                      tr4[:, h, q, :].unsqueeze(1).to_broadcast([128, 16, 16]), ALU.mult)
                tv = V(ve.tensor_reduce, res[q].rearrange("p (h k) -> p h k", h=8), eq, AX.X, ALU.add)
            return tv

        def turn(t, tv):
            b, tok, users = transposes(res, w=[tv])
            c = slice(128 * t, 128 * t + 128)
            V(ve.tensor_copy, i01[:, :, c], b[:, 0:256].rearrange("p (q t) -> p q t", q=2), w=[tok])
            tr_ = V(ve.tensor_copy, gt3[:, 0:128], b[:, 256:384])
            users.append(tr_)
            for q in range(3):
                V(ve.tensor_copy, gp[:, c, q], gt3[:, 0:128])
                if q < 2:
                    tv = V(ve.tensor_tensor, gt3[:, 0:128], gt3[:, 0:128], gp[:, c, q], ALU.subtract)
            return V.last

        for i in range(4):
            first_half(i)
        tv = choose(0)
        first_half(4)
        turn(0, tv)
        for i in range(5, 8):
            first_half(i)
        turn(1, choose(1))
        if STOP == "topk":
            return finish()
        everyone()
        V(ve.tensor_copy, iotab, cst("iota"))
        t_oj = [None, None]
        nb = [0]

        def build_w(qd, bt):
            n = nb[0] % 2
            nb[0] += 1
            oj, oi = ojs[n], ois[n]
            c = slice(16 * bt, 16 * bt + 16)
            V(ve.tensor_tensor, oj, i01[:, 1, c].unsqueeze(2).to_broadcast([128, 16, 128]),
              iotab[:, 0:128].unsqueeze(1).to_broadcast([128, 16, 128]), ALU.is_equal, w=[t_oj[n]])
            V(ve.tensor_tensor, eqb, i01[:, 0, c].unsqueeze(2).to_broadcast([128, 16, 32]),
              iotab[:, 32 * qd:32 * qd + 32].unsqueeze(1).to_broadcast([128, 16, 32]), ALU.is_equal)
            for q in range(3):
                tv = V(ve.tensor_tensor, oi[:, :, q, :], eqb,
                       gp[:, c, q].unsqueeze(2).to_broadcast([128, 16, 32]), ALU.mult)

            def rest():
                b, fw, users = banks.get(WORK)
                for j in range(16):
                    for q in range(3):
                        tok = P(te.matmul, b[:, 32 * j:32 * j + 32], oj[:, j, :], oi[:, j, q, :], start=(q == 0),
                                stop=(q == 2), w=[tv, *fw], inc=(j == 15 and q == 2))
                t_oj[n] = tok
                t_w[0] = A(se.activation, wgt[:, :, c], b.rearrange("p (t i) -> p i t", t=16), ACT.Copy,
                           w=[tok, t_free[0]])
                users.append(t_w[0])
            return rest

        t_free = [None]
        rest = build_w(0, 0)
        for bt in range(1, 16):
            nxt = build_w(0, bt)
            rest()
            rest = nxt
        rest()
        for i in range(8, 40):
            q = i // 8 - 1
            if i < 32:
                first_half(i)
            if i % 8 == 0:
                for n in range(8 * q, 8 * q + 8):
                    g = n - 8 * q
                    t_mult[n] = V(ve.tensor_tensor, slots[n % NSL], slots[n % NSL], wgt[:, 4 * g:4 * g + 4, :],
                                  ALU.mult, w=[t_w[0], t_gelu[n]])
                t_free[0] = V.last
            rests = [build_w(q + 1, 2 * (i % 8) + b_) for b_ in range(2)] if q < 3 else []
            second_half(i - 8)
            for r_ in rests:
                r_()
        tok = P.last
        for m in range(8):
            V(ve.scalar_tensor_tensor, xT[:, m, :], acc(m), mod[:, 40 + m:41 + m], xT[:, m, :], ALU.mult, ALU.add,
              w=[tok])
        finish()


def constants():
    f = np.float32
    cs = np.zeros((128, NCS), f)

    def put(dst, table, name, x):
        o, n = table[name]
        dst[:x.shape[0], o:o + n] = x
    p = np.arange(128)
    put(cs, CS, "ident", np.eye(128, dtype=f))
    put(cs, CS, "ones", np.ones((128, 128), f))
    put(cs, CS, "bones", (p[:, None] // 64 == p[None, :] // 64).astype(f))
    partner = np.where(p % 32 < 16, p + 16, p - 16)
    put(cs, CS, "perm", (p[:, None] == partner[None, :]).astype(f))
    put(cs, CS, "tri", (p[:, None] < p[None, :]).astype(f))
    put(cs, CS, "iota", np.tile(np.arange(128, dtype=f), (128, 1)))
    put(cs, CS, "iota16", np.tile(np.arange(16, dtype=f), (128, 1)))
    put(cs, CS, "iota8", np.tile(np.arange(8, dtype=f), (128, 1)))
    t = np.arange(256)
    put(cs, CS, "scan64", np.tile((t % 64 != 0).astype(f), (128, 1)))
    put(cs, CS, "scan128", np.tile((t % 128 != 0).astype(f), (128, 1)))
    ms = np.zeros((128, NMS), np.uint32)
    j, i = p[:, None], p[None, :]
    put(ms, MS, "gla", ((j <= i) & (j // 64 == i // 64)).astype(np.uint32))
    put(ms, MS, "ssd", (j <= i).astype(np.uint32))
    col = np.arange(64)
    start = np.clip(col - 8, 0, 48)
    cm = (col[None, :] >= start[:, None]) & (col[None, :] < start[:, None] + 16)
    put(ms, MS, "col", np.tile(cm, (2, 4)).astype(np.uint32))
    hc = np.zeros((128, NHC), f)
    w = np.pi * np.outer(t, 2 * t + 1) / 512.0
    for name, m in (("C", np.cos(w)), ("S", np.sin(w)), ("CI", np.cos(w).T / 256), ("SI", -np.sin(w).T / 256)):
        put(hc, HC, name, m.reshape(2, 128, 256).transpose(1, 0, 2).reshape(128, 512).astype(f))
    tt = np.linspace(0.0, 1.0, L, dtype=f)
    deltas = np.abs(np.linspace(math.log(1e-2) / 1.5, math.log(1e-2) / 0.3, 512, dtype=f))
    dec = np.exp(-tt[:, None] * deltas)
    put(hc, HC, "dec", dec.reshape(2, 128, 512).transpose(1, 0, 2).reshape(128, 1024).astype(f))
    wv = f(2.0 * math.pi / L) * np.arange(L, dtype=f)[:, None]
    bands = np.linspace(1e-4, 15.0, 16, dtype=f)[None, :]
    feats = np.concatenate([tt[:, None], np.cos(bands * wv), -np.sin(bands * wv)], axis=-1)
    put(hc, HC, "feats", feats.T.astype(f))
    inv = (f(10000.0) ** (-np.arange(16, dtype=f) / 16)).astype(f)
    d = p % 64
    pos = np.where((d < 32)[:, None], (t // 64)[None, :], (t % 64)[None, :]).astype(f)
    ang = pos * inv[d % 16][:, None]
    put(hc, HC, "ropeC", np.cos(ang).astype(f))
    put(hc, HC, "ropeS", (np.where((d % 32 < 16)[:, None], -1, 1) * np.sin(ang)).astype(f))
    sel = np.repeat(np.eye(8, dtype=f), 128, axis=1)
    return cs, ms, hc, sel


def kernel(**x):
    import concourse.bacc as bacc
    from concourse.bass_utils import run_bass_kernel_spmd

    x = {k: np.asarray(v) for k, v in x.items()}
    f = np.float32
    cs, ms, hc, sel = constants()
    pv = np.zeros((128, NPV), f)

    def vec(name, v):
        v = v.reshape(-1)
        o, n = PV[name]
        pv[:, o:o + n] = v.reshape(n, 128).T

    def rows(name, m):
        o, n = PV[name]
        pv[:m.shape[0], o:o + n] = m

    for l in range(2):
        vec(f"ada_b{l}", x["ada_b"][l])
        vec(f"norm1_w{l}", x["norm1_w"][l])
        vec(f"norm2_w{l}", x["norm2_w"][l])
        vec(f"gla_a_b{l}", x["gla_a_b"][l])
        vec(f"gla_norm_w{l}", x["gla_norm_w"][l])
        vec(f"conv_w{l}", x["conv_w"][l])
        vec(f"conv_b{l}", x["conv_b"][l])
        rows(f"dt_bias{l}", x["dt_bias"][l][:, None])
        rows(f"a_log{l}", x["a_log"][l][:, None])
        vec(f"d_skip{l}", np.repeat(x["d_skip"][l], 64))
        vec(f"ssd_norm_w{l}", x["ssd_norm_w"][l])
        rows(f"gla_a_w{l}", x["gla_a_w"][l])
    vec("c", x["c"][0])
    o, n = PV["c2"]
    pv[:, o:o + n:2] = x["c_2"][0].reshape(8, 128).T
    pv[:, o + 1:o + n:2] = x["c_ctx_2"].reshape(8, 128).T
    vec("final_w", x["final_norm_w"])
    vec("norm1_g", x["norm1_g_2"][0])
    vec("norm2_g", x["norm2_g_2"][0])
    vec("b_ada", x["b_ada_2"][0])
    vec("b_in", x["b_in_2"][0])
    vec("hcw", x["hy_conv_w_2"][0])
    vec("hcb", x["hy_conv_b_2"][0])
    for name, key in (("f1b", "hy_f1_b_2"), ("f2b", "hy_f2_b_2"), ("f3b", "hy_f3_b_2"), ("freq", "hy_sin_freq_2")):
        rows(name, x[key][0][:, None])
    vec("skip", x["hy_skip_2"][0])
    vec("qg", np.concatenate([x["q_norm_g_2"][0]] * 2))
    vec("kg", np.concatenate([x["k_norm_g_2"][0]] * 2))
    rows("router", x["router_w"][0].reshape(8, 128, 8).transpose(1, 0, 2).reshape(128, 64))
    rows("f1w", x["hy_f1_w_2"][0])
    rows("f2w", x["hy_f2_w_2"][0])
    rows("f3w", x["hy_f3_w_2"][0])
    rows("bv", x["b_in_2"][0][None, 2560:3072])

    r, qc, i, kc = np.arange(4), np.arange(64), np.arange(4), np.arange(64)
    dr = (i[None, :] - r[:, None] + 7)[:, None, :, None]
    dcx = (np.clip(kc[None, :] - qc[:, None], -15, 15) + 15)[None, :, None, :]
    bias = x["na_rpb_2"][0][:, dr, dcx].reshape(8, 2, 128, 256).transpose(2, 1, 0, 3).reshape(128, 4096)

    arrays = {
        "pv": pv, "cs": cs, "ms": ms, "hc": hc, "sel": sel, "xT": x["x"][0].T, "ctxT": x["ctx_2"][0].T,
        "ada_w": x["ada_w"], "w_in": x["w_in"], "w_out": x["w_out"],
        "ffn_w_gate": x["ffn_w_gate"][0], "ffn_w_up": x["ffn_w_up"][0], "ffn_w_down": x["ffn_w_down"][0],
        "moe_w_gate": x["moe_w_gate"][0], "moe_w_up": x["moe_w_up"][0], "moe_w_down": x["moe_w_down"][0],
        "w_ada": x["w_ada_2"][0], "w_in2": x["w_in_2"][0], "f4w": x["hy_f4_w_2"][0],
        "w_hy": x["w_hy_out_2"][0], "w_na": x["w_na_out_2"][0], "w_out2": x["w_out_2"][0],
        "w_pq": x["peer_w_q_2"][0],
        "keysT": x["peer_keys_2"][0].transpose(3, 0, 1, 2).reshape(128, 2048),
        "uT": x["peer_u_2"][0].T, "v": x["peer_v_2"][0], "bias": bias,
    }
    nc = bacc.Bacc("TRN2", target_bir_lowering=False, num_devices=1)
    ins, T = {}, {}
    for name, a in arrays.items():
        a = np.ascontiguousarray(a)
        ins[f"in_{name}"] = a
        T[name] = nc.dram_tensor(f"in_{name}", a.shape, mybir.dt.from_np(a.dtype), kind="ExternalInput").ap()
    T["out"] = nc.dram_tensor("out_x", (1024, 256), F32, kind="ExternalOutput").ap()
    program(nc, T)
    res = run_bass_kernel_spmd(nc, [ins], core_ids=[0])
    return np.ascontiguousarray(res.results[0]["out_x"].T)[None]
```

```python
import math
from contextlib import ExitStack

import numpy as np

import concourse.bass as bass
from concourse import mybir

ALU = mybir.AluOpType
ACT = mybir.ActivationFunctionType
AX = mybir.AxisListType
F32 = mybir.dt.float32
U32 = mybir.dt.uint32
BF16 = mybir.dt.bfloat16
I32 = mybir.dt.int32
F32R = mybir.dt.float32r

D = 1024
L = 256
EPS = 1e-6
SLOT = 4224
NSLOT = 5
ARENA = 22208
BIG = -3.0e38
STOP = None


def layout(items):
    at, out = 0, {}
    for name, n in items:
        out[name] = (at, n)
        at += n
    return out, at


NARROW = ([("c", 8), ("c2", 16)]
          + [(f"{n}{l}", w) for l in range(2) for n, w in (
              ("norm1_w", 8), ("ada_b", 48), ("norm2_w", 8), ("gla_a_b", 2), ("gla_norm_w", 1), ("conv_w", 24),
              ("conv_b", 6), ("dt_bias", 1), ("a_log", 1), ("d_skip", 4), ("ssd_norm_w", 4))]
          + [("final_w", 8), ("norm1_g", 8), ("norm2_g", 8), ("b_ada", 48), ("b_in", 40), ("hcw", 36), ("hcb", 12),
             ("f1b", 1), ("f2b", 1), ("f3b", 1), ("freq", 1), ("skip", 8), ("qg", 1), ("kg", 1), ("router", 64)])
WIDE = [("gla_a_w0", 256), ("gla_a_w1", 256), ("f1w", 64), ("f2w", 64), ("f3w", 64), ("bv", 512)]
PV, NPV = layout(NARROW + WIDE)
NNARROW = sum(n for _, n in NARROW)
CS, NCS = layout([("ident", 128), ("ones", 128), ("bones", 128), ("perm", 128), ("tri", 128), ("iota", 128),
                  ("iota16", 16), ("scan64", 256), ("scan128", 256), ("iota8", 8)])
MS, NMS = layout([("gla", 128), ("ssd", 128), ("col", 256)])
HC, NHC = layout([("C", 512), ("S", 512), ("CI", 512), ("SI", 512), ("dec", 1024), ("ropeC", 256),
                  ("ropeS", 256), ("feats", 256)])


class Eng:

    def __init__(self, e, sem, chained):
        self.e, self.sem, self.n, self.chained, self.seen = e, sem, 0, chained, {}
        self.queue = []

    def emit(self, queue=None):
        for instruction in self.queue if queue is None else queue:
            instruction()

    def dma(self, out, in_, sem):
        self.queue.append(lambda: self.e.dma_start(out, in_).then_inc(sem, 16))

    def wait(self, toks):
        for t in toks:
            if t is None:
                continue
            sem, v = t
            if self.seen.get(id(sem), 0) < v:
                self.queue.append(lambda sem=sem, v=v: self.e.wait_ge(sem, v))
                self.seen[id(sem)] = v

    def __call__(self, fn, *args, w=(), inc=True, **kw):
        self.wait(w)
        if self.chained and self.n:
            self.wait([(self.sem, self.n)])
        if not inc:
            self.queue.append(lambda: fn(*args, **kw))
            return None
        self.n += 1
        self.queue.append(lambda: fn(*args, **kw).then_inc(self.sem, 1))
        return (self.sem, self.n)

    @property
    def last(self):
        return (self.sem, self.n) if self.n else None


class Banks:

    def __init__(self, banks):
        self.banks, self.free, self.at = banks, [[] for _ in banks], 0

    def get(self, among=None):
        if among is None:
            i = self.at % len(self.banks)
        else:
            i = among[self.at % len(among)]
        self.at += 1
        w, self.free[i] = self.free[i], []
        return self.banks[i], w, self.free[i]


class Ring:

    def __init__(self, eng, bufs, sems):
        self.eng, self.bufs, self.sems, self.n = eng, bufs, sems, 0
        self.users = [[] for _ in sems]

    def load(self, parts):
        s = self.n % len(self.sems)
        self.n += 1
        assert self.users[s] or self.n <= len(self.sems), "a slot that nobody has freed"
        self.eng.wait(self.users[s])
        self.users[s] = []
        base = self.bufs[s]
        for view, src in parts(base):
            self.eng.dma(view, src, self.sems[s][0])
            self.sems[s][1] += 16
        return base, (self.sems[s][0], self.sems[s][1]), self.users[s]


def program(nc, T):
    with ExitStack() as ctx:
        def sb(name, n, dt=F32):
            return ctx.enter_context(nc.sbuf_tensor(name, [128, n], dt))[:, :]

        def sem(name):
            return ctx.enter_context(nc.semaphore(name))

        te, ve, se, ge = nc.tensor, nc.vector, nc.scalar, nc.gpsimd
        P = Eng(te, sem("s_pe"), False)
        V = Eng(ve, sem("s_dve"), True)
        A = Eng(se, sem("s_act"), True)
        G = Eng(ge, sem("s_pool"), True)
        SP = Eng(nc.sync, sem("s_sp"), False)
        s_in = sem("s_in")
        s_out = sem("s_out")

        pv = sb("pv", NPV)
        cs = sb("cs", NCS)
        ms = sb("ms", NMS, U32)
        xT = sb("xT", 2048).rearrange("p (k t) -> p k t", k=8)
        mods = sb("mods", 4 * 48)
        small = sb("small", 32)
        accb = sb("accb", 1024)
        selb = sb("sel", 1024)
        with ExitStack() as stage:
            hT = stage.enter_context(nc.sbuf_tensor("hT", [128, 2048], F32))[:, :]
            ringbuf = stage.enter_context(nc.sbuf_tensor("ring", [128, NSLOT * SLOT], F32))[:, :]
            arena = stage.enter_context(nc.sbuf_tensor("arena", [128, ARENA], F32))[:, :]
        hT_r = sb("hT_r", 2048, F32R).rearrange("p (k t) -> p k t", k=8)
        ring_r = [sb(f"ring_r{i}", SLOT, F32R) for i in range(NSLOT)]
        arena_r = sb("arena_r", 9 * 1024, F32R)
        hT = hT.rearrange("p (k t) -> p k t", k=8)
        hc = arena[:, ARENA - NHC:ARENA]
        ring = Ring(SP, [ringbuf[:, i * SLOT:(i + 1) * SLOT] for i in range(NSLOT)], [[sem(f"s_ring{i}"), 0] for i in range(NSLOT)])
        banks = Banks([ctx.enter_context(nc.psum_tensor(f"ps{i}", [128, 512], F32))[:, :] for i in range(8)])

        def pvc(name, i=0, n=1, rows=128):
            o = PV[name][0] + i
            return pv[0:rows, o:o + n]

        def cst(name, rows=128, cols=None):
            o, n = CS[name]
            return cs[0:rows, o:o + (cols or n)]

        def hcc(name, rows=128):
            o, n = HC[name]
            return hc[0:rows, o:o + n]

        class Arena:
            at = 0

        limit = [ARENA]

        def buf(n):
            a = Arena.at
            Arena.at += n
            assert Arena.at <= limit[0], (Arena.at, limit[0])
            return arena[:, a:a + n]

        def everyone():
            toks = [x.last for x in (P, V, A, G)]
            for x in (P, V, A, G):
                x.wait([t for t in toks if t and t[0] is not x.sem])
            V.wait([V.last])
            A.wait([A.last])

        def everyone_but_pool():
            toks = [x.last for x in (P, V, A)]
            for x in (P, V, A, SP):
                x.wait([t for t in toks if t and t[0] is not x.sem])
            for x in (P, V, A):
                x.wait([x.last])

        def fresh():
            everyone()
            Arena.at = 0

        def v4(x, k):
            return x.rearrange("p (k t) -> p k t", k=k)

        ident, ones, bones = cst("ident"), cst("ones"), cst("bones")

        s_in = [sem(f"s_in{i}") for i in range(6)]
        for q, (dst, src) in zip(s_in, (
                (pv[:, 0:NNARROW], T["pv"][:, 0:NNARROW]), (xT, T["xT"].rearrange("(k p) t -> p k t", p=128)),
                (cs, T["cs"]), (pv[:, NNARROW:NPV], T["pv"][:, NNARROW:NPV]), (selb[0:8, :], T["sel"]),
                (ms, T["ms"]))):
            A.dma(dst, src, q)
        t_pv, t_x, t_cs, t_wide, t_sel, t_ms = [(q, 16) for q in s_in]
        V.wait([t_pv])
        A.wait([t_pv])

        def wtile(w, c0, n):
            def parts(base):
                v = base[:, 0:8 * n].rearrange("p (k n) -> p k n", k=8)
                return [(v, w[:, c0:c0 + n].rearrange("(k p) n -> p k n", p=128))]
            base, tok, users = ring.load(parts)
            return base[:, 0:8 * n].rearrange("p (k n) -> p k n", k=8), tok, users

        def rtile(w, r0, n, cols):
            def parts(base):
                v = base[:, 0:n * cols].rearrange("p (k n) -> p k n", k=n)
                return [(v, w[r0:r0 + 128 * n, :].rearrange("(k p) n -> p k n", p=128))]
            base, tok, users = ring.load(parts)
            return base[:, 0:n * cols].rearrange("p (k n) -> p k n", k=n), tok, users

        def accum(out, pairs, w=(), inc=True):
            tok = None
            for i, (a, b) in enumerate(pairs):
                tok = P(te.matmul, out, a, b, start=(i == 0), stop=(i == len(pairs) - 1),
                        w=w, inc=(inc and i == len(pairs) - 1))
            return tok

        def transposes(ins, w=()):
            b, fw, users = banks.get()
            tok = None
            at = 0
            for i, x in enumerate(ins):
                k, m = x.shape
                tok = P(te.transpose, b[0:m, at:at + k], x, ident[0:k, 0:k], w=[*w, *fw],
                        inc=(i == len(ins) - 1))
                at += k
            return b, tok, users

        def ada_tile(w, n, s, stride, ncond, bias, outs, t_s):
            state = {}

            def rows_():
                tile, tt, tu = wtile(w, 512 * n, 512)
                for c in range(ncond):
                    a = accb[:, 512 * c:512 * c + 512]
                    V(ve.tensor_scalar, a, tile[:, 0, :], s[:, c:c + 1], None, ALU.mult, w=[tt, t_s, t_acc[0]])
                    for k in range(1, 8):
                        t = V(ve.scalar_tensor_tensor, a, tile[:, k, :], s[:, stride * k + c:stride * k + c + 1], a,
                              ALU.mult, ALU.add)
                tu.append(t)
                state["t"] = t

            def columns(among=None):
                b, fw, users = banks.get(among)
                for c in range(ncond):
                    for m in range(4):
                        tok = P(te.matmul, b[:, 4 * c + m:4 * c + m + 1],
                                accb[:, 512 * c + 128 * m:512 * c + 128 * m + 128], ones[:, 0:1],
                                start=True, stop=True, w=[state["t"], t_cs, *fw])
                t_acc[0] = tok
                for c in range(ncond):
                    t = V(ve.tensor_tensor, outs[c][:, 4 * n:4 * n + 4], b[:, 4 * c:4 * c + 4],
                          pvc(bias, 4 * n, 4), ALU.add, w=[tok])
                users.append(t)
                return t
            return rows_, columns

        def ada_tile_pe(w, n, s, bias, out, t_s):
            tile, tt, tu = wtile(w, 512 * n, 512)
            b, fw, users = banks.get()
            for m in range(4):
                tok = accum(b[:, m:m + 1], [(tile[:, k, 128 * m:128 * m + 128], s[:, k:k + 1]) for k in range(8)],
                            w=[tt, t_s, *fw])
            tu.append(tok)
            t = V(ve.tensor_tensor, out[:, 4 * n:4 * n + 4], b[:, 0:4], pvc(bias, 4 * n, 4), ALU.add, w=[tok])
            users.append(t)

        t_acc = [None]

        class Background:
            todo, half = [], None

        def background(among=None):
            if Background.half is not None:
                Background.half(among)
                Background.half = None
            if Background.todo:
                rows_, Background.half = Background.todo.pop(0)
                rows_()

        def background_end():
            while Background.todo or Background.half is not None:
                background()

        def rstd_of(ps, scale, n, out, tok):
            t0 = V(ve.tensor_scalar, out, ps, scale, EPS, ALU.mult, ALU.add, w=[tok])
            t1 = V(ve.reciprocal, out, out)
            return A(se.activation, out, out, ACT.Sqrt, w=[t1]), t0

        def norm_stats(src, t_src, scratch):
            sq, r = scratch[:, 0:2048].rearrange("p (k t) -> p k t", k=8), scratch[:, 2048:2304]
            t = A(se.activation, sq, src, ACT.Square, w=t_src)
            b, fw, users = banks.get()
            tok = accum(b[:, 0:256], [(ones, sq[:, k, :]) for k in range(8)], w=[t, t_cs, *fw])
            tr, t0 = rstd_of(b[:, 0:256], 1.0 / D, 256, r, tok)
            users.append(t0)
            return tr

        def norm_apply(src, g, sc, sh, dst, tr, scratch):
            r, gs = scratch[:, 2048:2304], scratch[:, 2304:2312]
            if sc is not None:
                V(ve.scalar_tensor_tensor, gs, sc, 1.0, g, ALU.add, ALU.mult, w=[tr])
            else:
                V(ve.tensor_copy, gs, g, w=[tr])
            t = None
            for k in range(8):
                t = V(ve.scalar_tensor_tensor, dst[:, k, :], src[:, k, :], gs[:, k:k + 1], r, ALU.mult, ALU.mult)
                if sc is not None:
                    t = A(se.activation, dst[:, k, :], dst[:, k, :], ACT.Identity, bias=sh[:, k:k + 1], w=[t])
            return t

        def norm_mod(src, g, sc, sh, dst, t_src, scratch):
            return norm_apply(src, g, sc, sh, dst, norm_stats(src, t_src, scratch), scratch)

        def proj(tile, tt, tu, c0, nch, rhs, w, take):
            tok = None
            for m0 in range(0, nch, 2):
                n = min(2, nch - m0)
                b, fw, users = banks.get()
                for j in range(n):
                    c = c0 + 128 * (m0 + j)
                    tok = accum(b[:, 256 * j:256 * j + 256],
                                [(tile[:, k, c:c + 128], rhs[:, k, :]) for k in range(8)], w=[tt, *w, *fw],
                                inc=(j == n - 1))
                users.append(take(b[:, 0:256 * n].rearrange("p (m t) -> p m t", m=n), m0, n, tok))
            tu.append(tok)
            return tok

        def proj_tm(tile, tt, tu, rhs, w, take, bias=None):
            for t in range(2):
                b, fw, users = banks.get()
                pairs = [(rhs[:, k, 128 * t:128 * t + 128], tile[:, k, 0:512]) for k in range(8)]
                if bias is not None:
                    pairs.append((ones[0:1, :], bias))
                tok = accum(b, pairs, w=[tt, *w, *fw])
                users.append(take(b, t, tok))
            tu.append(tok)

        def copy_to(dst, eng="A"):
            def take(b, m0, n, tok):
                if eng == "A":
                    return A(se.activation, dst[:, m0:m0 + n, :], b, ACT.Copy, w=[tok])
                return V(ve.tensor_copy, dst[:, m0:m0 + n, :], b, w=[tok])
            return take

        def residual(tile_c0, gate, n0):
            def take(b, m0, n, tok):
                for j in range(n):
                    m = n0 + m0 + j
                    t = V(ve.scalar_tensor_tensor, xT[:, m, :], b[:, j, :], gate[:, m:m + 1], xT[:, m, :],
                          ALU.mult, ALU.add, w=[tok])
                return t
            return take

        def log1pexp_neg_abs(x, tmp, w):
            t = A(se.activation, tmp, x, ACT.Abs, w=[V.last, *w])
            t = A(se.activation, tmp, tmp, ACT.Exp, scale=-1.0, w=[t])
            t = V(ve.tensor_scalar, tmp, tmp, 1.0, None, ALU.add, w=[t])
            return A(se.activation, tmp, tmp, ACT.Ln, w=[t])

        WORK = [4, 5, 6, 7]

        def mixer(l, mod, th):
            w_in, w_out = T["w_in"][l], T["w_out"][l]
            zT = v4(buf(1024), 4)
            merged = v4(buf(2048), 8)
            xbc = buf(6 * 259).rearrange("p (k t) -> p k t", k=6)
            dts, sp, cum, alr, btm = buf(256), buf(256), buf(256), buf(256), buf(128)
            qkT = buf(1024)
            qT, kT, oT = v4(qkT[:, 0:512], 2), v4(qkT[:, 512:1024], 2), v4(qkT, 4)
            gT = v4(buf(1024), 4)
            v_tm = v4(buf(1024), 2)
            qe_, la_, lt_, ktail_ = (buf(512) for _ in range(4))
            qe, la, lt, ktail = (v4(x, 2) for x in (qe_, la_, lt_, ktail_))
            kep_, ktp_ = buf(1024), buf(1024)
            kep, ktp = v4(kep_, 4), v4(ktp_, 4)
            spad = buf(4 * 3 * 128).rearrange("p (h n v) -> p h n v", h=4, n=3)
            attm = buf(1024).rearrange("p (h t i) -> p h t i", h=4, t=2)
            bl = buf(8).rearrange("p (c n) -> p c n", c=2)
            ebl = buf(8).rearrange("p (c n) -> p c n", c=2)
            xc = v4(buf(1536), 6)
            av = buf(1)
            dc = buf(32).rearrange("p (t c) -> p t c", t=2)
            xdt_ = buf(1024)
            xdt = xdt_.rearrange("p (t h q) -> p t h q", t=2, h=8)
            dec = buf(2048).rearrange("p (h t i) -> p h t i", h=8, t=2)
            ecb = buf(1024).rearrange("p (h i) -> p h i", h=8)
            fl = buf(8)
            hflat = hT.rearrange("p k t -> p (k t)")
            wx = la_.rearrange("p (h q) -> p h q", h=8)
            bpad = v4(lt_, 2)
            gm = hflat[:, 0:512].rearrange("p (g t i) -> p g t i", g=2, t=2)
            s1 = ktail_.rearrange("p (h q) -> p h q", h=8)
            rr1 = hflat[:, 512:768]
            yT = v4(xbc.rearrange("p k t -> p (k t)")[:, 0:1024], 4)

            for z in (xbc[:, :, 0:3], kep, ktp, attm, spad):
                tz = G(ge.memset, z, 0.0, w=[th])
            hw = [th]

            tile, tt, tu = wtile(w_in, 1536, 528)
            b, fw, users = banks.get()
            tok = accum(b[0:16, 0:256], [(tile[:, k, 0:16], hT[:, k, :]) for k in range(8)], w=[tt, *hw, *fw])
            t_alr = V(ve.tensor_copy, alr[0:16, :], b[0:16, 0:256], w=[tok])
            users.append(t_alr)
            proj(tile, tt, tu, 16, 4, hT, hw,
                 lambda b, m0, n, tok: A(se.activation, zT[:, m0:m0 + n, :], b, ACT.Silu, w=[tok]))
            b, fw, users = banks.get()
            for c in range(2):
                tok = P(te.matmul, b[:, 256 * c:256 * c + 256], pvc(f"gla_a_w{l}", 128 * c, 128, rows=16),
                        alr[0:16, :], start=True, stop=True, w=[t_alr, t_wide, *fw])
            for c in range(2):
                t = V(ve.tensor_scalar, la[:, c, :], b[:, 256 * c:256 * c + 256], pvc(f"gla_a_b{l}", c), None,
                      ALU.add, w=[tok])
            users.append(t)
            background()

            tile, tt, tu = wtile(w_in, 0, 512)

            def take_qk(b, m0, n, tok):
                if m0 == 0:
                    return V(ve.tensor_scalar, qT, b, 0.125, None, ALU.mult, w=[tok])
                return V(ve.tensor_copy, kT, b, w=[tok])
            proj(tile, tt, tu, 0, 4, hT, hw, take_qk)
            background()
            t = log1pexp_neg_abs(la, lt, [t])
            V(ve.scalar_tensor_tensor, lt, la, 0.0, lt, ALU.min, ALU.subtract, w=[t])
            for c in range(2):
                t = V(ve.tensor_tensor_scan, la[:, c, :], cst("scan64"), lt[:, c, :], 0.0, ALU.mult, ALU.add,
                      w=[t_cs])
            tla = t
            t = A(se.activation, lt, la, ACT.Exp, scale=1.0 / 16, w=[t])
            tq = V(ve.tensor_tensor, qe, qT, lt, ALU.mult, w=[t])
            t = A(se.activation, lt, la, ACT.Exp, scale=-1.0 / 16, w=[tq])
            for h in range(4):
                r = slice(64 * (h % 2), 64 * (h % 2) + 64)
                tk = V(ve.tensor_tensor, kep[r, h, :], kT[r, h // 2, :], lt[r, h // 2, :], ALU.mult, w=[t, tz])
            t = V(ve.tensor_scalar, bl, la[:, :, 63:256:64], 1.0 / 16, None, ALU.mult)
            tebl = A(se.activation, ebl, bl, ACT.Exp, w=[t])
            for c in range(2):
                for n in range(4):
                    t = A(se.activation, ktail[:, c, 64 * n:64 * n + 64], la[:, c, 64 * n:64 * n + 64], ACT.Exp,
                          bias=bl[:, c, n:n + 1], scale=-1.0 / 16)
            tkl = V(ve.tensor_tensor, ktail, ktail, kT, ALU.mult, w=[t])

            tile, tt, tu = wtile(w_in, 512, 512)
            proj_tm(tile, tt, tu, hT, hw, lambda b, t, tok: V(ve.tensor_copy, v_tm[:, t, :], b, w=[tok]))
            tv_tm = V.last
            background()
            xin = xbc[:, :, 3:259]
            tile, tt, tu = wtile(w_in, 2576, 264)
            b, fw, users = banks.get()
            tok = accum(b[0:8, 0:256], [(tile[:, k, 256:264], hT[:, k, :]) for k in range(8)], w=[tt, *fw])
            t_dt = V(ve.tensor_scalar, dts[0:8, :], b[0:8, 0:256], pvc(f"dt_bias{l}", rows=8), None, ALU.add,
                     w=[tok])
            users.append(t_dt)
            proj(tile, tt, tu, 0, 2, hT, hw, copy_to(xin[:, 4:6, :], "A"))
            background()
            tile, tt, tu = wtile(w_in, 2064, 512)
            proj(tile, tt, tu, 0, 4, hT, hw, copy_to(xin, "A"))
            txin = A.last
            background()

            for o in range(2):
                b, fw, users = banks.get()
                for c in range(2):
                    for t_ in range(2):
                        s = slice(128 * t_, 128 * t_ + 128)
                        at = 128 * (2 * c + t_)
                        tok = P(te.matmul, b[:, at:at + 128], kep[:, 2 * c + o, s], qe[:, c, s],
                                start=True, stop=True, w=[tk, tq, *fw])
                for c in range(2):
                    for t_ in range(2):
                        at = 128 * (2 * c + t_)
                        ta = V(ve.copy_predicated, attm[:, 2 * c + o, t_, :],
                               ms[:, MS["gla"][0]:MS["gla"][0] + 128], b[:, at:at + 128], w=[tok, tz, t_ms])
                users.append(ta)
            b, tok, users = transposes([ktail[:, c, 128 * s:128 * s + 128] for s in range(2) for c in range(2)],
                                       w=[tkl])
            for n in range(4):
                r = slice(64 * (n % 2), 64 * (n % 2) + 64)
                tkt = V(ve.tensor_copy, ktp[r, n, :], b[r, 256 * (n // 2):256 * (n // 2) + 256], w=[tok, tz])
            users.append(tkt)

            t = log1pexp_neg_abs(dts[0:8, :], sp[0:8, :], [t_dt])
            ta_ = A(se.activation, av[0:8, :], pvc(f"a_log{l}", rows=8), ACT.Exp)
            V(ve.scalar_tensor_tensor, dts[0:8, :], dts[0:8, :], 0.0, sp[0:8, :], ALU.max, ALU.add, w=[t])
            V(ve.tensor_scalar, sp[0:8, :], dts[0:8, :], av[0:8, :], -1.0, ALU.mult, ALU.mult, w=[ta_])
            tc = V(ve.tensor_tensor_scan, cum[0:8, :], cst("scan128", rows=8), sp[0:8, :], 0.0,
                   ALU.mult, ALU.add)

            tile, tt, tu = wtile(w_in, 1024, 512)
            proj(tile, tt, tu, 0, 4, hT, hw,
                 lambda b, m0, n, tok: A(se.activation, gT[:, m0:m0 + n, :], b, ACT.Silu, w=[tok]))
            tg = A.last
            for z, t in ((bpad, tkl), (s1, tkt), (gm, P.last)):
                tz2 = G(ge.memset, z, 0.0, w=[t])
            background()
            if l == 0:
                Background.todo = ada_layer(0, [9])
                background_end()
            for n in range(3):
                b, fw, users = banks.get()
                for c in range(2):
                    tok = P(te.matmul, b[:, 256 * c:256 * c + 256], ktp[:, n, 128 * c:128 * c + 128],
                            v_tm[:, n // 2, 256 * c:256 * c + 256], start=True, stop=True, w=[tkt, *fw])
                for h in range(4):
                    r = slice(64 * (h % 2), 64 * (h % 2) + 64)
                    src = b[r, 256 * (h // 2) + 128 * (h % 2):256 * (h // 2) + 128 * (h % 2) + 128]
                    if n == 0:
                        ts = V(ve.tensor_copy, spad[r, h, 0, :], src, w=[tok, tz])
                    else:
                        ts = V(ve.scalar_tensor_tensor, spad[r, h, n, :], spad[r, h, n - 1, :],
                               ebl[r, h // 2, n:n + 1], src, ALU.mult, ALU.add, w=[tok, tebl])
                users.append(ts)
            b, tok, users = transposes([x[0:8, 128 * t:128 * t + 128] for t in range(2) for x in (dts, cum)],
                                       w=[tc])
            users.append(V(ve.tensor_copy, dc, b[:, 0:32].rearrange("p (t c) -> p t c", t=2), w=[tok]))
            for p in range(4):
                b, fw, users = banks.get()
                for j in range(2):
                    h = 2 * p + j
                    tok = P(te.matmul, b[:, 256 * j:256 * j + 256], selb[0:8, 128 * h:128 * h + 128], cum[0:8, :],
                            start=True, stop=True, w=[tc, t_sel, *fw])
                for j in range(2):
                    h = 2 * p + j
                    for t in range(2):
                        V(ve.tensor_scalar, dec[:, h, t, :], b[:, 256 * j + 128 * t:256 * j + 128 * t + 128],
                          dc[:, t, 8 + h:9 + h], 0.0, ALU.subtract, ALU.min, w=[tok])
                    tv = V(ve.tensor_tensor, fl[:, h:h + 1], b[:, 256 * j + 127:256 * j + 128],
                           dc[:, 0, 8 + h:9 + h], ALU.subtract)
                te_ = A(se.activation, ecb[:, 2 * p:2 * p + 2, :],
                        b.rearrange("p (j t i) -> p j t i", j=2, t=2)[:, :, 1, :], ACT.Exp, w=[tok, tv])
                users += [tv, te_]
                if p == 1:
                    for h in range(4):
                        b, fw, users = banks.get()
                        for t in range(2):
                            s = slice(128 * t, 128 * t + 128)
                            P(te.matmul, b[:, s], v_tm[:, t, 128 * h:128 * h + 128], attm[:, h, t, :],
                              start=True, stop=False, w=[ta, ts, tv_tm, *fw], inc=False)
                            for n in range(max(1, 2 * t), 2 * t + 2):
                                tok = P(te.matmul, b[:, 64 * n:64 * n + 64], spad[:, h, n - 1, :],
                                        qe[:, h // 2, 64 * n:64 * n + 64], start=False, stop=(n == 2 * t + 1))
                        to = A(se.activation, oT[:, h, :], b[:, 0:256], ACT.Copy, w=[tok, tkl])
                        users.append(to)
            tdec = A(se.activation, dec, dec, ACT.Exp, w=[tv])
            tf = A(se.activation, fl, fl, ACT.Exp)
            for k in (4, 5, 0, 1, 2, 3):
                V(ve.tensor_scalar, xc[:, k, :], xbc[:, k, 0:256], pvc(f"conv_w{l}", k), pvc(f"conv_b{l}", k),
                  ALU.mult, ALU.add, w=[txin])
                for j in range(1, 4):
                    t = V(ve.scalar_tensor_tensor, xc[:, k, :], xbc[:, k, j:j + 256],
                          pvc(f"conv_w{l}", 6 * j + k), xc[:, k, :], ALU.mult, ALU.add)
                if k in (5, 1, 3):
                    tx = A(se.activation, xc[:, k - 1:k + 1, :], xc[:, k - 1:k + 1, :], ACT.Silu, w=[t])
                if k == 5:
                    tx45 = tx
            sq, rr = v4(kep_, 4), v4(ktp_, 4)
            t = A(se.activation, sq, oT, ACT.Square, w=[to])
            for p in range(2):
                b, fw, users = banks.get()
                tok = accum(b, [(ones, sq[:, 2 * p:2 * p + 2, :])], w=[t, *fw])
                tr, t0 = rstd_of(b.rearrange("p (k t) -> p k t", k=2), 1.0 / 128, 0, rr[:, 2 * p:2 * p + 2, :], tok)
                users.append(t0)
            for g in range(2):
                r = slice(64 * g, 64 * g + 64)
                tb = V(ve.tensor_copy, bpad[r, g, :], xc[r, 4, :], w=[tx45, tz2])
            V(ve.scalar_tensor_tensor, oT, oT, pvc(f"gla_norm_w{l}"), rr, ALU.mult, ALU.mult, w=[tr])
            tm = V(ve.tensor_tensor, merged[:, 0:4, :], oT, gT, ALU.mult, w=[tg])

            b, fw, users = banks.get()
            for g in range(2):
                for t in range(2):
                    s = slice(128 * t, 128 * t + 128)
                    at = 128 * (2 * g + t)
                    tok = P(te.matmul, b[:, at:at + 128], bpad[:, g, s], xc[:, 5, s], start=True, stop=True,
                            w=[tb, *fw])
            for g in range(2):
                for t in range(2):
                    at = 128 * (2 * g + t)
                    tv = V(ve.copy_predicated, gm[:, g, t, :], ms[:, MS["ssd"][0]:MS["ssd"][0] + 128],
                           b[:, at:at + 128], w=[tok])
            users.append(tv)
            for t in range(2):
                b, tok, users = transposes([xc[:, k, 128 * t:128 * t + 128] for k in range(4)], w=[tx])
                users.append(V(ve.tensor_tensor, xdt[:, t], b.rearrange("p (h q) -> p h q", h=8),
                               dc[:, t, 0:8].unsqueeze(2).to_broadcast([128, 8, 64]), ALU.mult, w=[tok]))
            b, tok, users = transposes([xc[:, 4, 0:128]])
            tbt = A(se.activation, btm, b[:, 0:128], ACT.Copy, w=[tok])
            users.append(tbt)
            twx = V(ve.tensor_tensor, wx, xdt[:, 0], fl.unsqueeze(2).to_broadcast([128, 8, 64]), ALU.mult, w=[tf])
            b, fw, users = banks.get(WORK)
            tok = accum(b, [(btm, wx)], w=[twx, tbt, *fw])
            wo = []
            ob = [banks.get([i]) for i in range(4)]
            ov = [ob[m // 2][0][:, 256 * (m % 2):256 * (m % 2) + 256] for m in range(8)]
            for n in range(2):
                tile, tt, tu = wtile(w_out, 512 * n, 512)
                wo.append((tile, tu))
                for m in range(4):
                    mm = 4 * n + m
                    for k in range(4):
                        P(te.matmul, ov[mm], tile[:, k, 128 * m:128 * m + 128], merged[:, k, :],
                          start=(k == 0 and mm % 2 == 0), stop=False, skip_group_check=True,
                          w=[tt, tm, *ob[mm // 2][1]], inc=False)
            for g in range(2):
                r = slice(64 * g, 64 * g + 64)
                ts = V(ve.tensor_copy, s1[r, 4 * g:4 * g + 4, :],
                       b[r, 256 * g:256 * g + 256].rearrange("p (h q) -> p h q", h=4), w=[tok, tz2])
            users.append(ts)
            tce = V(ve.tensor_tensor, ecb, ecb, xc[:, 5, 128:256].unsqueeze(1).to_broadcast([128, 8, 128]),
                    ALU.mult, w=[te_])
            for g in range(2):
                for t in range(2):
                    td = V(ve.tensor_tensor, dec[:, 4 * g:4 * g + 4, t, :], dec[:, 4 * g:4 * g + 4, t, :],
                           gm[:, g, t, :].unsqueeze(1).to_broadcast([128, 4, 128]), ALU.mult, w=[tdec])
            for c in range(4):
                b, fw, users = banks.get(WORK)
                for h in (2 * c, 2 * c + 1):
                    r = slice(64 * (h % 2), 64 * (h % 2) + 64)
                    P(te.matmul, b[r, 0:128], xdt[:, 0, h, :], dec[:, h, 0, :], start=True, stop=True,
                      w=[td, *fw], inc=False)
                    P(te.matmul, b[r, 128:256], xdt[:, 1, h, :], dec[:, h, 1, :], start=True, stop=False,
                      inc=False)
                    tok = P(te.matmul, b[r, 128:256], s1[:, h, :], ecb[:, h, :], start=False, stop=True)
                V(ve.scalar_tensor_tensor, yT[:, c, :], xc[:, c, :], pvc(f"d_skip{l}", c), b[:, 0:256],
                  ALU.mult, ALU.add, w=[tok])
                ty = V(ve.tensor_tensor, yT[:, c, :], yT[:, c, :], zT[:, c, :], ALU.mult)
                users.append(ty)
            sq = v4(xdt_, 4)
            t = A(se.activation, sq, yT, ACT.Square, w=[ty])
            b, fw, users = banks.get(WORK)
            tok = accum(b[:, 0:256], [(ones, sq[:, k, :]) for k in range(4)], w=[t, *fw])
            tr, t0 = rstd_of(b[:, 0:256], 1.0 / 512, 0, rr1, tok)
            users.append(t0)
            for c in range(4):
                tm = V(ve.scalar_tensor_tensor, merged[:, 4 + c, :], yT[:, c, :], pvc(f"ssd_norm_w{l}", c), rr1,
                       ALU.mult, ALU.mult, w=[tr])
            for mm in range(8):
                tile, tu = wo[mm // 4]
                m = mm % 4
                for k in range(4, 8):
                    tok = P(te.matmul, ov[mm], tile[:, k, 128 * m:128 * m + 128], merged[:, k, :],
                            start=False, stop=(k == 7), skip_group_check=True, w=[tm], inc=(k == 7))
                if m == 3:
                    tu.append(tok)
                if mm % 2:
                    for i in (mm - 1, mm):
                        t = V(ve.scalar_tensor_tensor, xT[:, i, :], ov[i], mod[:, 16 + i:17 + i], xT[:, i, :],
                              ALU.mult, ALU.add, w=[tok])
                    ob[mm // 2][2].append(t)

        def acc(m):
            return banks.banks[m // 2][:, 256 * (m % 2):256 * (m % 2) + 256]

        class Down:

            def __init__(self):
                self.first = True
                self.waits = [t for i in range(4) for t in banks.free[i]]
                for i in range(4):
                    banks.free[i] = []

            def add(self, tile, tt, tu, act, ta, last):
                tok = None
                for j in range(4):
                    for m in range(8):
                        tok = P(te.matmul, acc(m), tile[:, j, 128 * m:128 * m + 128], act[:, j, :],
                                start=(self.first and j == 0 and m % 2 == 0), stop=(last and j == 3),
                                skip_group_check=True, w=[tt, ta, *self.waits], inc=(j == 3 and m == 7))
                    self.waits = []
                self.first = False
                tu.append(tok)
                return tok

        def dense_ffn(wg, wu, wd, gate):
            acts = [v4(buf(1024), 4) for _ in range(2)]
            sil = [buf(256) for _ in range(2)]
            down = Down()
            pend = None
            t_act_read = [None, None]
            t_mul = [None, None]
            th = [A.last, V.last]

            def add(last):
                f, a, ta = pend
                dt, td, ud = rtile(wd, 512 * f, 4, D)
                t_act_read[f % 2] = down.add(dt, td, ud, a, ta, last=last)
            for f in range(7):
                gt, tg, ug = wtile(wg, 512 * f, 512)
                ut, tu_, uu = wtile(wu, 512 * f, 512)
                a = acts[f % 2]
                for j in range(4):
                    b, fw, users = banks.get(WORK)
                    c = slice(128 * j, 128 * j + 128)
                    tk1 = accum(b[:, 0:256], [(gt[:, k, c], hT[:, k, :]) for k in range(8)], w=[tg, *th, *fw])
                    tk2 = accum(b[:, 256:512], [(ut[:, k, c], hT[:, k, :]) for k in range(8)], w=[tu_])
                    s = sil[j % 2]
                    t = A(se.activation, s, b[:, 0:256], ACT.Silu, w=[tk2, t_mul[j % 2]])
                    ta = V(ve.tensor_tensor, a[:, j, :], s, b[:, 256:512], ALU.mult, w=[t, t_act_read[f % 2]])
                    t_mul[j % 2] = ta
                    users.append(ta)
                ug.append(tk1)
                uu.append(tk2)
                background(WORK)
                if pend is not None:
                    add(False)
                pend = (f, a, ta)
                background(WORK)
            add(True)
            tok = P.last
            for m in range(8):
                t = V(ve.scalar_tensor_tensor, xT[:, m, :], acc(m), gate[:, m:m + 1], xT[:, m, :],
                      ALU.mult, ALU.add, w=[tok])
            for i in range(4):
                banks.free[i].append(t)

        def moe(gate):
            rw = pvc("router", 0, 64).rearrange("p (k e) -> p k e", k=8)
            htm = v4(buf(2048), 2)
            lg, e8, g8, m8, oh, pos = (buf(16) for _ in range(6))
            ix, fx, sm = buf(16).bitcast(U32), buf(16), buf(8)
            flag = buf(2)
            gath = [buf(256).rearrange("p (t c) -> p t c", t=2) for _ in range(2)]
            scat = buf(512).rearrange("p (e t c) -> p e t c", e=2, t=2)
            pwt = buf(2048).rearrange("p (e t) -> p e t", e=8)
            xg = [v4(buf(1024), 8) for _ in range(2)]
            ysb = buf(8192).rearrange("p (e n) -> p e n", e=8)
            acts = [v4(buf(512), 4) for _ in range(2)]
            sil = [buf(256).rearrange("p (j c) -> p j c", j=2) for _ in range(2)]
            t_h = [A.last, V.last]
            b, fw, users = banks.get()
            for t in range(2):
                tok = accum(b[:, 8 * t:8 * t + 8],
                            [(hT[:, k, 128 * t:128 * t + 128], rw[:, k, :]) for k in range(8)], w=[*t_h, *fw])
            users.append(V(ve.tensor_copy, lg, b[:, 0:16], w=[tok]))
            for t in range(2):
                for q in range(2):
                    b, tok, users = transposes([hT[:, 4 * q + k, 128 * t:128 * t + 128] for k in range(4)])
                    th = A(se.activation, htm[:, t, 512 * q:512 * q + 512], b, ACT.Copy, w=[tok])
                    users.append(th)
            for t in range(2):
                s = slice(8 * t, 8 * t + 8)
                V(ve.max, e8[:, s], lg[:, s])
                V(ve.max_index, ix[:, s], e8[:, s], lg[:, s])
                V(ve.tensor_copy, fx[:, s], ix[:, s])
                tv = V(ve.tensor_tensor, sm[:, 4 * t:4 * t + 1], e8[:, 8 * t + 1:8 * t + 2], e8[:, 8 * t:8 * t + 1],
                       ALU.subtract)
                ta = A(se.activation, sm[:, 4 * t + 1:4 * t + 2], sm[:, 4 * t:4 * t + 1], ACT.Exp, w=[tv])
                V(ve.tensor_scalar, m8[:, s], cst("iota8"), fx[:, 8 * t:8 * t + 1], None, ALU.is_equal)
                V(ve.tensor_scalar, oh[:, s], cst("iota8"), fx[:, 8 * t + 1:8 * t + 2], None, ALU.is_equal)
                V(ve.tensor_scalar, sm[:, 4 * t:4 * t + 1], sm[:, 4 * t + 1:4 * t + 2], 1.0, None, ALU.add, w=[ta])
                V(ve.reciprocal, sm[:, 4 * t + 2:4 * t + 3], sm[:, 4 * t:4 * t + 1])
                V(ve.tensor_tensor, sm[:, 4 * t + 3:4 * t + 4], sm[:, 4 * t + 1:4 * t + 2],
                  sm[:, 4 * t + 2:4 * t + 3], ALU.mult)
                V(ve.tensor_scalar, g8[:, s], m8[:, s], sm[:, 4 * t + 2:4 * t + 3], None, ALU.mult)
                V(ve.scalar_tensor_tensor, g8[:, s], oh[:, s], sm[:, 4 * t + 3:4 * t + 4], g8[:, s],
                  ALU.mult, ALU.add)
                tm = V(ve.tensor_tensor, m8[:, s], m8[:, s], oh[:, s], ALU.add)
            b, fw, users = banks.get()
            accum(b[:, 0:8], [(cst("tri"), m8[:, 0:8])], w=[tm, *fw])
            accum(b[:, 8:16], [(ones, m8[:, 0:8]), (cst("tri"), m8[:, 8:16])])
            tok = accum(b[:, 16:24], [(ones, m8[:, 0:8]), (ones, m8[:, 8:16])])
            V(ve.tensor_copy, fx, b[:, 0:16], w=[tok])
            V(ve.scalar_tensor_tensor, pos, fx, 1.0, m8, ALU.add, ALU.mult)
            V(ve.tensor_scalar, pos, pos, -1.0, None, ALU.add)
            users.append(V(ve.tensor_reduce, flag[:, 0:1], b[:, 16:24], AX.X, ALU.max))
            flag_at[0] = flag[0:1, 1:2].bitcast(I32)
            t_flag = V(ve.tensor_scalar, flag[:, 1:2].bitcast(I32), flag[:, 0:1], 128.0, None, ALU.is_gt)

            def one_pass(first):
                if not first:
                    V(ve.tensor_scalar, pos, pos, -128.0, None, ALU.add)
                for e2 in range(4):
                    for i in range(2):
                        e = 2 * e2 + i
                        for t in range(2):
                            tv = V(ve.tensor_scalar, scat[:, i, t, :], cst("iota"), pos[:, 8 * t + e:8 * t + e + 1],
                                   g8[:, 8 * t + e:8 * t + e + 1], ALU.is_equal, ALU.mult, w=[P.last])
                    b, tok, users = transposes([scat[:, i, t, :] for i in range(2) for t in range(2)], w=[tv])
                    tpw = V(ve.tensor_copy, pwt[:, 2 * e2:2 * e2 + 2, :], b.rearrange("p (e t) -> p e t", e=2),
                            w=[tok])
                    users.append(tpw)
                t_gath = [None, None]
                t_xg = [None, None]
                t_xg_read = [None, None]

                def onehots(e):
                    for t in range(2):
                        tv = V(ve.tensor_scalar, gath[e % 2][:, t, :], cst("iota"), pos[:, 8 * t + e:8 * t + e + 1],
                               None, ALU.is_equal, w=[t_gath[e % 2]])
                    return tv

                def gather(e, tv):
                    for q in range(2):
                        b, fw, users = banks.get(WORK)
                        for m in range(4):
                            mm = 4 * q + m
                            tok = accum(b[:, 128 * m:128 * m + 128],
                                        [(htm[:, t, 128 * mm:128 * mm + 128], gath[e % 2][:, t, :])
                                         for t in range(2)], w=[tv, th, *fw])
                        ta = A(se.activation, xg[e % 2][:, 4 * q:4 * q + 4, :], b.rearrange("p (m c) -> p m c", m=4),
                               ACT.Copy, w=[tok, t_xg_read[e % 2]])
                        users.append(ta)
                    t_gath[e % 2] = tok
                    t_xg[e % 2] = ta
                gather(0, onehots(0))
                t_act_read = [None, None]
                t_mul = [None, None]
                ywait = [[t for i in (2 * p, 2 * p + 1) for t in banks.free[i]] for p in range(2)]
                for i in range(4):
                    banks.free[i] = []
                pend = None
                ty = None

                def down(e, f, a, ta):
                    wd = T["moe_w_down"][e]
                    dt, td, ud = rtile(wd, 512 * f, 4, D)
                    for j in range(4):
                        for h in range(2):
                            tok = P(te.matmul, banks.banks[2 * (e % 2) + h], a[:, j, :],
                                    dt[:, j, 512 * h:512 * h + 512], start=(f == 0 and j == 0),
                                    stop=(f == 6 and j == 3), w=[td, ta, *(ywait[e % 2] if f == 0 else [])],
                                    inc=(j == 3 and h == 1))
                    ud.append(tok)
                    t_act_read[f_of[0] % 2] = tok
                    if f < 6:
                        return None
                    for h in range(2):
                        t = A(se.activation, ysb[:, e, 512 * h:512 * h + 512], banks.banks[2 * (e % 2) + h], ACT.Copy,
                              w=[tok])
                    ywait[e % 2] = [t]
                    return t
                f_of = [0]
                i = 0
                for e in range(8):
                    x = xg[e % 2]
                    for f in range(7):
                        gt, tg, ug = wtile(T["moe_w_gate"][e], 512 * f, 512)
                        ut, tu_, uu = wtile(T["moe_w_up"][e], 512 * f, 512)
                        a = acts[i % 2]
                        if f == 3 and e < 7:
                            toh = onehots(e + 1)
                        for p in range(2):
                            b, fw, users = banks.get(WORK)
                            v = b.rearrange("p (j u c) -> p j u c", j=2, u=2)
                            for j in range(2):
                                c = slice(128 * (2 * p + j), 128 * (2 * p + j) + 128)
                                tk1 = accum(v[:, j, 0, :], [(gt[:, k, c], x[:, k, :]) for k in range(8)],
                                            w=[tg, t_xg[e % 2], *fw])
                                tk2 = accum(v[:, j, 1, :], [(ut[:, k, c], x[:, k, :]) for k in range(8)], w=[tu_])
                            s = sil[p]
                            t = A(se.activation, s, v[:, :, 0, :], ACT.Silu, w=[tk2, t_mul[p]])
                            ta = V(ve.tensor_tensor, a[:, 2 * p:2 * p + 2, :], s, v[:, :, 1, :], ALU.mult,
                                   w=[t, t_act_read[i % 2]])
                            t_mul[p] = ta
                            users.append(ta)
                        ug.append(tk1)
                        uu.append(tk2)
                        if f == 6:
                            t_xg_read[e % 2] = tk2
                        if pend is not None:
                            f_of[0] = i - 1
                            down(*pend)
                        if f == 4 and e < 7:
                            gather(e + 1, toh)
                        pend = (e, f, a, ta)
                        i += 1
                        if first:
                            background(WORK)
                f_of[0] = i - 1
                ty = down(*pend)
                for i in range(4):
                    banks.free[i].append(ty)
                for p in range(4):
                    b, fw, users = banks.get()
                    for j in range(2):
                        m = 2 * p + j
                        tok = accum(b[:, 256 * j:256 * j + 256],
                                    [(ysb[:, e, 128 * m:128 * m + 128], pwt[:, e, :]) for e in range(8)],
                                    w=[ty, tpw, *fw])
                    for j in range(2):
                        m = 2 * p + j
                        t = V(ve.scalar_tensor_tensor, xT[:, m, :], b[:, 256 * j:256 * j + 256], gate[:, m:m + 1],
                              xT[:, m, :], ALU.mult, ALU.add, w=[tok])
                    users.append(t)

            one_pass(True)
            background_end()
            everyone()
            SP.wait([x.last for x in (P, V, A, G)])
            for q, n in ring.sems:
                SP.wait([(q, n)])
            engines = (P, V, A, SP)
            before = [(x.n, dict(x.seen), x.queue) for x in engines]
            rings = [n for _, n in ring.sems]
            for x in engines:
                x.queue = []
            one_pass(False)
            everyone_but_pool()
            for x, (n, seen, queue) in zip(engines, before):
                taken, adds = x.queue, [(x.sem, x.n - n)]
                if x is SP:
                    adds = [(q, n1 - n0) for (q, n1), n0 in zip(ring.sems, rings)]
                queue.append(lambda x=x, taken=taken, adds=adds: branch(x, taken, adds))
                x.queue, x.seen = queue, seen

        def branch(x, taken, adds):
            with x.e.If(x.e.value_load(flag_at[0], min_val=0, max_val=1)):
                x.emit(taken)
            with x.e.Else():
                for q, n in adds:
                    if n:
                        x.e.sem_inc(q, n)

        flag_at = [None]

        def finish():
            everyone()
            SP.wait([x.last for x in (P, V, A, G)])
            SP.dma(T["out"].rearrange("(k p) t -> p k t", p=128), xT, s_out)
            SP.wait([(s_out, 16)])
            block = ctx.enter_context(nc.Block())
            block.tensor(lambda e: P.emit())
            block.vector(lambda e: V.emit())
            block.scalar(lambda e: A.emit())
            block.gpsimd(lambda e: G.emit())
            block.sync(lambda e: SP.emit())

        t_s = A(se.activation, small[:, 0:8], pvc("c", 0, 8), ACT.Silu)
        t_s2 = A(se.activation, small[:, 8:24], pvc("c2", 0, 16), ACT.Silu)
        m2 = mods[:, 96:192].rearrange("p (c m) -> p c m", c=2)

        def ada_layer(l, tiles):
            return [ada_tile(T["ada_w"][l], n, small[:, 0:8], 1, 1, f"ada_b{l}", [mods[:, 48 * l:48 * l + 48]], t_s)
                    for n in tiles]

        for n in (0, 2):
            (rows_, columns), = ada_layer(0, [n])
            rows_()
            ada_tile_pe(T["ada_w"][0], n + 1, small[:, 0:8], "ada_b0", mods[:, 0:48], t_s)
            columns()
        Background.todo = ada_layer(0, range(4, 9))
        for l in range(2):
            fresh()
            mod = mods[:, 48 * l:48 * l + 48]
            scr = arena[:, ARENA - 2312:ARENA]
            tr = norm_stats(xT, [V.last, t_x], scr)
            if l == 1:
                background_end()
            th = norm_apply(xT, pvc(f"norm1_w{l}", 0, 8), mod[:, 8:16], mod[:, 0:8], hT, tr, scr)
            mixer(l, mod, th)
            if STOP == f"mix{l}":
                return finish()
            fresh()
            norm_mod(xT, pvc(f"norm2_w{l}", 0, 8), mod[:, 32:40], mod[:, 24:32], hT, [V.last], scr)
            if l == 0:
                Background.todo = ada_layer(0, range(10, 12)) + ada_layer(1, range(12))
                dense_ffn(T["ffn_w_gate"], T["ffn_w_up"], T["ffn_w_down"], mod[:, 40:48])
                background_end()
            else:
                Background.todo = [
                    ada_tile(T["w_ada"], n, small[:, 8:24], 2, 2 if n < 4 else 1, "b_ada", [m2[:, 0, :], m2[:, 1, :]],
                             t_s2) for n in range(12)]
                moe(mod[:, 40:48])
            if STOP == f"ffn{l}":
                return finish()
        fresh()
        norm_mod(xT, pvc("final_w", 0, 8), None, None, xT, [V.last], scr)
        if STOP == "first":
            return finish()

        limit[0] = ARENA - NHC
        mod, modc = m2[:, 0, :], m2[:, 1, :]
        fresh()
        qn, kn, kc = v4(buf(1024), 4), v4(buf(1024), 4), v4(buf(1024), 4)
        v_tm, vc_tm = v4(buf(1024), 2), v4(buf(1024), 2)
        ctx_ = buf(2048)
        ctxT = v4(ctx_, 8)
        zs = buf(13 * 258)
        zh = zs[:, 258:13 * 258].rearrange("p (k t) -> p k t", k=12)
        zc = zs[:, 0:12 * 258].rearrange("p (k t) -> p k t", k=12)[:, :, 0:256]
        filt = buf(4096)
        kre = [[filt[:, 1024 * o + 512 * k:1024 * o + 512 * k + 512] for k in range(2)] for o in range(2)]
        kim = [[filt[:, 2048 + 1024 * o + 512 * k:2048 + 1024 * o + 512 * k + 512] for k in range(2)]
               for o in range(2)]
        fb_ = buf(2048)
        fb = [fb_[:, 512 * i:512 * i + 512] for i in range(4)]
        rn, tmp, hab = buf(512), buf(512), buf(512)
        ha, hb = hab[:, 0:256], hab[:, 256:512]
        SP.wait([x.last for x in (P, V, A, G)])
        s_ctx = sem("s_ctx")
        s_hc = sem("s_hc")
        SP.dma(hc, T["hc"], s_hc)
        SP.dma(ctxT, T["ctxT"].rearrange("(k p) t -> p k t", p=128), s_ctx)
        t_hc = (s_hc, 16)
        scrc = arena[:, Arena.at - 2312:Arena.at]
        th = norm_mod(xT, pvc("norm1_g", 0, 8), mod[:, 8:16], mod[:, 0:8], hT, [V.last], scrc)
        tz = G(ge.memset, zh[:, :, 0:1], 0.0)
        tz = G(ge.memset, zh[:, :, 257:258], 0.0)
        w_in = T["w_in2"]
        pieces = []

        def fill(n=1):
            for _ in range(min(n, len(pieces))):
                pieces.pop(0)()

        def queue_proj(w, c0, rhs, wt_, take, take2=None, rhs2=None, wt2=None):
            held = {}

            def piece(i, r, w_, tk):
                def f():
                    if i == 0:
                        held["tile"] = wtile(w, c0, 512)
                    tile, tt, tu = held["tile"]
                    m0 = 2 * (i % 2)
                    b, fw, users = banks.get(held.get("among"))
                    for j in range(2):
                        c = 128 * (m0 + j)
                        tok = accum(b[:, 256 * j:256 * j + 256],
                                    [(tile[:, k, c:c + 128], r[:, k, :]) for k in range(8)],
                                    w=[tt, w_[0], *fw], inc=(j == 1))
                    users.append(tk(v4(b, 2), m0, 2, tok))
                    if i == (1 if rhs2 is None else 3):
                        tu.append(tok)
                return f
            for i in range(2):
                pieces.append(piece(i, rhs, wt_, take))
            if rhs2 is not None:
                for i in range(2, 4):
                    pieces.append(piece(i, rhs2, wt2, take2))

        def queue_proj_tm(w, c0, jobs, bias):
            held = {}

            def piece(n, t, r, w_, dst):
                def f():
                    if n == 0 and t == 0:
                        held["tile"] = wtile(w, c0, 512)
                    tile, tt, tu = held["tile"]
                    b, fw, users = banks.get()
                    tok = accum(b, [(r[:, k, 128 * t:128 * t + 128], tile[:, k, 0:512]) for k in range(8)]
                                + [(ones[0:1, :], bias)], w=[tt, w_[0], *fw])
                    users.append(A(se.activation, dst[:, t, :], b, ACT.Copy, w=[tok]))
                    if n == len(jobs) - 1 and t == 1:
                        tu.append(tok)
                return f
            for n, (r, w_, dst) in enumerate(jobs):
                for t in range(2):
                    pieces.append(piece(n, t, r, w_, dst))

        def biased(dst, col):
            def take(b, m0, n, tok):
                for j in range(n):
                    t = A(se.activation, dst[:, m0 + j, :], b[:, j, :], ACT.Identity,
                          bias=pvc("b_in", col + m0 + j), w=[tok])
                return t
            return take

        thw, thcw = [th], [None]
        for n in range(3):
            queue_proj(w_in, 512 * n, hT, thw, biased(zh[:, 4 * n:4 * n + 4, 1:257], 4 * n))
        queue_proj(w_in, 1536, hT, thw, biased(qn, 12))
        queue_proj(w_in, 2048, hT, thw, biased(kn, 16), biased(kc, 16), ctxT, thcw)
        queue_proj_tm(w_in, 2560, [(hT, thw, v_tm), (ctxT, thcw, vc_tm)], pvc("bv", 0, 512, rows=1))
        fill(1)

        thcw[0] = norm_mod(ctxT, pvc("norm1_g", 0, 8), modc[:, 8:16], modc[:, 0:8], ctxT,
                           [(s_ctx, 16), V.last], scrc)
        everyone()

        src, t = hcc("feats", rows=33), t_hc
        for i, (wname, bname, rows) in enumerate((("f1w", "f1b", 33), ("f2w", "f2b", 64), ("f3w", "f3b", 64))):
            b, fw, users = banks.get()
            tok = accum(b[0:64, 0:256], [(pvc(wname, 0, 64, rows=rows), src)], w=[t, t_wide, *fw])
            x, y = ha[0:64, :], hb[0:64, :]
            users.append(V(ve.tensor_scalar, x, b[0:64, 0:256], pvc(bname, rows=64), pvc("freq", rows=64),
                           ALU.add, ALU.mult, w=[tok]))
            V(ve.tensor_scalar, y, x, 1.0 / (2 * math.pi), 12582912.0, ALU.mult, ALU.add)
            V(ve.tensor_scalar, y, y, 12582912.0, None, ALU.subtract)
            p1, p2 = 6.28125, 0.0019350051879882812
            p3 = 2 * math.pi - p1 - p2
            for part in (p1, p2, p3):
                V(ve.scalar_tensor_tensor, x, y, -part, x, ALU.mult, ALU.add)
            V(ve.tensor_scalar, x, x, 3.1415925, -3.1415925, ALU.min, ALU.max)
            t = A(se.activation, x, x, ACT.Sin, w=[V.last])
            src = x
            fill(1)
        tsin = t

        f4, tf4, uf4 = ring.load(lambda base_: [(base_[0:64, 0:2048], T["f4w"])])
        dec_t = hcc("dec").rearrange("p (t c) -> p t c", t=2)
        DC, DS, DCI, DSI = (v4(hcc(n), 2) for n in ("C", "S", "CI", "SI"))
        V.wait([t_hc])
        for o in range(2):
            for dr in range(2):
                for t in range(2):
                    b, fw, users = banks.get()
                    c0 = 1024 * o + 512 * dr
                    tok = accum(b, [(ha[0:64, 128 * t:128 * t + 128], f4[0:64, c0:c0 + 512])],
                                w=[tf4, tsin, *fw])
                    tv = V(ve.tensor_tensor, fb[2 * dr + t], b, dec_t[:, t, :], ALU.mult, w=[tok])
                    users.append(tv)
            if o == 1:
                uf4.append(tok)
            fill(1)
            b, fw, users = banks.get()
            for i in range(4):
                ab = A(se.activation, (tmp, rn)[i % 2], fb[i], ACT.Abs, w=[tv, P.last])
                tok = P(te.matmul, b, ones, (tmp, rn)[i % 2], start=(i == 0), stop=(i == 3), w=[ab, *fw])
            users.append(V(ve.reciprocal, rn, b, w=[tok]))
            V(ve.memset, fb[2][0:1, :], 0.0)
            for t in range(2):
                V(ve.tensor_tensor, tmp, fb[t], fb[2 + t], ALU.add)
                V(ve.tensor_tensor, fb[2 + t], fb[2 + t], fb[t], ALU.subtract)
                tv = V(ve.tensor_copy, fb[t], tmp)
            fill(1)
            for k in range(2):
                s = slice(128 * k, 128 * k + 128)
                for dst, mat, x in ((kre, DC, 0), (kim, DS, 2)):
                    b, fw, users = banks.get()
                    tok = accum(b, [(mat[:, t, s], fb[x + t]) for t in range(2)], w=[tv, t_hc, *fw])
                    users.append(V(ve.tensor_tensor, dst[o][k], b, rn, ALU.mult, w=[tok]))
        if STOP == "proj2":
            return finish()

        while len(pieces) > 9:
            fill(1)
        tzh = A.last
        for k in range(12):
            V(ve.tensor_scalar, zc[:, k, :], zh[:, k, 0:256], pvc("hcw", k), pvc("hcb", k), ALU.mult, ALU.add,
              w=[tz, tzh])
            for j in range(1, 3):
                tv = V(ve.scalar_tensor_tensor, zc[:, k, :], zh[:, k, j:j + 256], pvc("hcw", 12 * j + k),
                       zc[:, k, :], ALU.mult, ALU.add)
            if k == 3:
                tz03 = tv
            if k % 4 == 3:
                fill(1)
        y_tm = [rn, hab]
        yre, yim = v4(fb_[:, 0:1024], 2), v4(fb_[:, 1024:2048], 2)
        for o in range(2):
            for t in range(2):
                b, tok, users = transposes([zc[:, c, 128 * t:128 * t + 128] for c in range(4)],
                                           w=[tz03 if o == 0 else V.last])
                ty = V(ve.tensor_copy, y_tm[t], b, w=[tok])
                users.append(ty)
            for k in range(2):
                s = slice(128 * k, 128 * k + 128)
                br, fw, ur = banks.get()
                tok = accum(br, [(DC[:, t, s], y_tm[t]) for t in range(2)], w=[ty, *fw])
                bi, fw, ui = banks.get()
                tok = accum(bi, [(DS[:, t, s], y_tm[t]) for t in range(2)], w=[ty, *fw])
                V(ve.tensor_tensor, yre[:, k, :], br, kre[o][k], ALU.mult, w=[tok])
                V(ve.tensor_tensor, tmp, bi, kim[o][k], ALU.mult)
                V(ve.tensor_tensor, yre[:, k, :], yre[:, k, :], tmp, ALU.add)
                V(ve.tensor_tensor, yim[:, k, :], br, kim[o][k], ALU.mult)
                tv = V(ve.tensor_tensor, tmp, bi, kre[o][k], ALU.mult)
                ur.append(tv)
                ui.append(tv)
                tv = V(ve.tensor_tensor, yim[:, k, :], yim[:, k, :], tmp, ALU.subtract)
                fill(1)
            fill(1)
            for c in range(4):
                s = slice(128 * c, 128 * c + 128)
                b, fw, users = banks.get()
                tok = accum(b[:, 0:256], [(yre[:, k, s], DCI[:, k, :]) for k in range(2)]
                            + [(yim[:, k, s], DSI[:, k, :]) for k in range(2)], w=[tv, *fw])
                users.append(V(ve.scalar_tensor_tensor, zc[:, c, :], zc[:, c, :], pvc("skip", 4 * o + c),
                               b[:, 0:256], ALU.mult, ALU.add, w=[tok]))
                V(ve.tensor_tensor, zc[:, c, :], zc[:, c, :], zc[:, 4 + 4 * o + c, :], ALU.mult)
        fill(len(pieces))
        if STOP == "hyena":
            return finish()

        everyone()
        gate = v4(filt, 16)
        kp = v4(zs[:, 4 * 258:4 * 258 + 2048], 8)
        kcp = v4(fb_, 8)
        yna = v4(ctx_[:, 0:1024], 4)
        sq = v4(ctx_[:, 1024:2048], 4)
        rr = v4(arena[:, ARENA - NHC:ARENA - NHC + 1024], 4)
        hct = arena[:, ARENA - NHC + 1024:ARENA - NHC + 2048]
        tmpb, st = hct[:, 0:256], hct[:, 256:264]
        for n in range(4):
            queue_proj(w_in, 3072 + 512 * n, hT, thw, biased(gate[:, 4 * n:4 * n + 4, :], 24 + 4 * n))
        G(ge.memset, kp, 0.0)
        tz = G(ge.memset, kcp, 0.0)
        for x, g in ((qn, "qg"), (kn, "kg"), (kc, "kg")):
            t = A(se.activation, sq, x, ACT.Square, w=[V.last, P.last])
            for p in range(2):
                b, fw, users = banks.get()
                tok = accum(b, [(bones, sq[:, 2 * p:2 * p + 2, :])], w=[t, *fw])
                tr, t0 = rstd_of(b.rearrange("p (k t) -> p k t", k=2), 1.0 / 64, 0, rr[:, 2 * p:2 * p + 2, :], tok)
                users.append(t0)
            fill(1)
            tv = V(ve.scalar_tensor_tensor, x, x, pvc(g), rr, ALU.mult, ALU.mult, w=[tr])
            if x is not kc:
                rc, rs = hcc("ropeC"), hcc("ropeS")
                for p in range(2):
                    b, fw, users = banks.get()
                    xx = x[:, 2 * p:2 * p + 2, :]
                    tok = accum(b, [(cst("perm"), xx)], w=[tv, *fw])
                    tv2 = V(ve.tensor_tensor, rr[:, 2 * p:2 * p + 2, :], b.rearrange("p (k t) -> p k t", k=2),
                            rs.unsqueeze(1).to_broadcast([128, 2, 256]), ALU.mult, w=[tok])
                    users.append(tv2)
                    V(ve.tensor_tensor, xx, xx, rc.unsqueeze(1).to_broadcast([128, 2, 256]), ALU.mult)
                    tv = V(ve.tensor_tensor, xx, xx, rr[:, 2 * p:2 * p + 2, :], ALU.add)
        for h in range(8):
            r = slice(64 * (h % 2), 64 * (h % 2) + 64)
            V(ve.tensor_copy, kp[r, h, :], kn[r, h // 2, :], w=[tz])
            tkp = A(se.activation, kcp[r, h, :], kc[r, h // 2, :], ACT.Copy, w=[tz, tv])
        tkp2 = V.last
        V.wait([tkp])
        A.wait([tkp2])
        sc = [kn.rearrange("p k t -> p (k t)")[:, 0:512], kn.rearrange("p k t -> p (k t)")[:, 512:1024]]
        pt = [kc.rearrange("p k t -> p (k t)")[:, 0:512], kc.rearrange("p k t -> p (k t)")[:, 512:1024]]
        for s in sc:
            V(ve.memset, s[:, 0:256], -1.0e30)
        bias_b, tbias, ubias = ring.load(lambda base_: [(base_[:, 0:4096], T["bias"])])
        biasv = bias_b[:, 0:4096].rearrange("p (t h k) -> p t h k", t=2, h=8)
        mcol = ms[:, MS["col"][0]:MS["col"][0] + 256]
        its = [(h, t) for h in range(8) for t in range(2)]
        def scores(i):
            h, t = its[i]
            b, fw, users = banks.get()
            q = qn[:, h // 2, 128 * t:128 * t + 128]
            P(te.matmul, b[:, 0:256], q, kp[:, h, :], start=True, stop=True, w=[tkp, tkp2, *fw], inc=False)
            tok = P(te.matmul, b[:, 256:512], q, kcp[:, h, :], start=True, stop=True)
            return b, tok, users

        def peak(i):
            h, t = its[i]
            b, tok, users = got[i]
            s = sc[i % 2]
            t_ctx = A(se.activation, s[:, 256:512], b[:, 256:512], ACT.Copy, scale=0.125, w=[tok])
            V(ve.scalar_tensor_tensor, tmpb, b[:, 0:256], 0.125, biasv[:, t, h, :], ALU.mult, ALU.add,
              w=[t_ctx, tbias])
            users.append(V.last)
            V(ve.copy_predicated, s[:, 0:256], mcol, tmpb)
            return V(ve.tensor_reduce, st[:, 4 * (i % 2):4 * (i % 2) + 1], s, AX.X, ALU.max, negate=True)

        def weights(i, tv):
            s, p_, c3 = sc[i % 2], pt[i % 2], 4 * (i % 2)
            return A(se.activation, p_, s, ACT.Exp, bias=st[:, c3:c3 + 1], accum_out=st[:, c3 + 1:c3 + 2],
                     w=[tv, t_pt[i % 2]])

        def scaled(i, ta):
            p_, c3 = pt[i % 2], 4 * (i % 2)
            V(ve.reciprocal, st[:, c3 + 2:c3 + 3], st[:, c3 + 1:c3 + 2], w=[ta])
            return V(ve.tensor_scalar, p_, p_, st[:, c3 + 2:c3 + 3], None, ALU.mult)

        def turned(i, tp):
            p_ = pt[i % 2]
            bt, tok, ut = transposes([p_[:, 128 * k:128 * k + 128] for k in range(4)], w=[tp])
            ta = A(se.activation, p_, bt, ACT.Copy, w=[tok])
            ut.append(ta)
            return ta

        def attended(i, ta):
            h, t = its[i]
            p_ = pt[i % 2]
            yb, fwy, uy = banks.get()
            r = slice(64 * (h % 2), 64 * (h % 2) + 64)
            vs = [v_tm[:, 0, :], v_tm[:, 1, :], vc_tm[:, 0, :], vc_tm[:, 1, :]]
            for k in range(4):
                tok = P(te.matmul, yb[r, 0:128], vs[k][:, 64 * h:64 * h + 64],
                        p_[:, 128 * k:128 * k + 128], start=(k == 0), stop=(k == 3), w=[ta, *fwy], inc=(k == 3))
            t_pt[i % 2] = tok
            t = A(se.activation, yna[r, h // 2, 128 * t:128 * t + 128], yb[r, 0:128], ACT.Copy, w=[tok])
            uy.append(t)
            return t

        t_pt = [None, None]
        got = [scores(i) for i in range(3)]
        tmax = [peak(0)]
        tp = scaled(0, weights(0, tmax[0]))
        tmax.append(peak(1))
        for i in range(len(its)):
            if i + 1 < len(its):
                te_ = weights(i + 1, tmax[i + 1])
            ta = turned(i, tp)
            if i + 2 < len(its):
                tmax.append(peak(i + 2))
            if i + 1 < len(its):
                tp = scaled(i + 1, te_)
            if i + 3 < len(its):
                got.append(scores(i + 3))
            fill(1)
            tyn = attended(i, ta)
        ubias.append(V.last)
        fill(len(pieces))
        tsg = A(se.activation, filt, filt, ACT.Sigmoid)

        def half_merge(w, src, base_k, tsrc):
            for n in range(2):
                def parts(base_, n=n):
                    v = base_[:, 0:2048].rearrange("p (k n) -> p k n", k=4)
                    return [(v, w[:, 512 * n:512 * n + 512].rearrange("(k p) n -> p k n", p=128))]
                base_, tt, tu = ring.load(parts)
                wt = base_[:, 0:2048].rearrange("p (k n) -> p k n", k=4)
                for p in range(2):
                    b, fw, users = banks.get()
                    for j in range(2):
                        m = 2 * p + j
                        tok = accum(b[:, 256 * j:256 * j + 256],
                                    [(wt[:, k, 128 * m:128 * m + 128], src[:, k, :]) for k in range(4)],
                                    w=[tt, tsrc, *fw])
                    m = base_k + 4 * n + 2 * p
                    tm = V(ve.tensor_tensor, gate[:, m:m + 2, :], gate[:, m:m + 2, :], v4(b, 2), ALU.mult,
                           w=[tok, tsg])
                    users.append(tm)
                    if base_k:
                        tm = V(ve.tensor_tensor, gate[:, m - 8:m - 6, :], gate[:, m - 8:m - 6, :],
                               gate[:, m:m + 2, :], ALU.add)
                tu.append(tok)
            return tm
        half_merge(T["w_hy"], zc, 0, tkp2)
        tm = half_merge(T["w_na"], yna, 8, tyn)
        for n in range(2):
            tile, tt, tu = wtile(T["w_out2"], 512 * n, 512)
            proj(tile, tt, tu, 0, 4, gate, [tm], residual(0, mod[:, 16:24], 4 * n))
        if STOP == "mix2":
            return finish()

        fresh()
        limit[0] = ARENA
        NSL = 9
        slots = [v4(buf(1024), 4) for _ in range(NSL)]
        region = Arena.at
        scr = arena[:, region:region + 2312]
        th = norm_mod(xT, pvc("norm2_g", 0, 8), mod[:, 32:40], mod[:, 24:32], hT, [V.last], scr)
        wgt_ = buf(8192)
        wgt = wgt_.rearrange("p (s i t) -> p s i t", s=2, i=32)
        o_ = buf(3584)
        ojs = [o_[:, 1024 * i:1024 * i + 1024].bitcast(BF16).rearrange("p (j t) -> p j t", j=128)
               for i in range(2)]
        ois = [o_[:, 2048 + 768 * i:2816 + 768 * i].bitcast(BF16).rearrange("p (q i t) -> p q i t", q=3, i=32)
               for i in range(2)]
        i01 = buf(256).bitcast(BF16).rearrange("p (q t) -> p q t", q=2)
        gp = buf(384).bitcast(BF16).rearrange("p (q t) -> p q t", q=3)
        tv16 = buf(256).rearrange("p (g k) -> p g k", g=16)
        gt3 = buf(128)
        pa = buf(128).bitcast(U32).rearrange("p (h k) -> p h k", h=8)
        sm = buf(16)
        qt = arena[:, 5 * 1024:9 * 1024].rearrange("p (g t) -> p g t", g=16)
        sbufs = [wgt_[:, 2048 * t:2048 * t + 2048].rearrange("p (g n) -> p g n", g=16) for t in range(2)]
        cand = o_[:, 0:2048].rearrange("p (h n) -> p h n", h=8)
        eq = wgt_[:, 4096:6144].rearrange("p (h k a) -> p h k a", h=8, k=16)

        def own(t, at, n, k):
            return wgt_[:, 6144 + 1024 * t + at:6144 + 1024 * t + at + n].rearrange("p (h k) -> p h k", h=k)
        ti16 = [own(t, 0, 256, 16).bitcast(U32) for t in range(2)]
        tif = [own(t, 256, 256, 16) for t in range(2)]
        bs = [own(t, 512, 128, 8) for t in range(2)]
        bp = [own(t, 640, 128, 8).bitcast(U32) for t in range(2)]
        pf = [[own(t, 768 + 128 * q, 128, 8) for q in range(2)] for t in range(2)]
        eqb = accb[:, 0:256].bitcast(BF16).rearrange("p (i t) -> p i t", i=32)
        res = [[accb[:, 256 + 384 * t + 128 * i:384 + 384 * t + 128 * i] for i in range(3)] for t in range(2)]
        iotab = selb.bitcast(BF16).rearrange("p (j t) -> p j t", j=128)
        t_iota = G(ge.tensor_copy, iotab, cst("iota").unsqueeze(2).to_broadcast([128, 128, 16]))
        for n in range(4):
            tile, tt, tu = wtile(T["w_pq"], 512 * n, 512)
            proj(tile, tt, tu, 0, 4, hT, [th], copy_to(qt[:, 4 * n:4 * n + 4, :], "A"))
        tq = A.last
        keys, tkeys, ukeys = ring.load(lambda base_: [(base_[:, 0:2048], T["keysT"])])
        t_sc = [None, None]
        for t in range(2):
            for g4 in range(4):
                b, fw, users = banks.get()
                for j in range(4):
                    g = 4 * g4 + j
                    tok = P(te.matmul, b[:, 128 * j:128 * j + 128], qt[:, g, 128 * t:128 * t + 128],
                            keys[:, 128 * g:128 * g + 128], start=True, stop=True, w=[tq, tkeys, *fw])
                t_sc[t] = A(se.activation, sbufs[t][:, 4 * g4:4 * g4 + 4, :],
                            b.rearrange("p (g n) -> p g n", g=4), ACT.Copy, w=[tok])
                users.append(t_sc[t])
        ukeys.append(tok)
        down = Down()
        t_slot = [None] * NSL
        t_gelu = [None] * 32
        t_mult = [None] * 32
        t_w = [None]

        def first_half(i):
            ut, tt, tu = wtile(T["uT"], 512 * i, 512)
            a = slots[i % NSL]
            for p in range(2):
                b, fw, users = banks.get(WORK)
                for j in range(2):
                    c = slice(128 * (2 * p + j), 128 * (2 * p + j) + 128)
                    tok = accum(b[:, 256 * j:256 * j + 256], [(ut[:, k, c], hT[:, k, :]) for k in range(8)],
                                w=[tt, th, *fw])
                ta = A(se.activation, a[:, 2 * p:2 * p + 2, :], b.rearrange("p (m t) -> p m t", m=2), ACT.Gelu,
                       w=[tok, t_slot[i % NSL]])
                users.append(ta)
            tu.append(tok)
            t_gelu[i] = ta

        def top16(vals, out_v, out_i, w=()):
            V(ve.max, out_v[:, 0:8], vals, w=w)
            V(ve.max_index, out_i[:, 0:8], out_v[:, 0:8], vals)
            V(ve.match_replace, vals, out_v[:, 0:8], vals, BIG)
            V(ve.max, out_v[:, 8:16], vals)
            V(ve.max_index, out_i[:, 8:16], out_v[:, 8:16], vals)

        def ranks(t, gs):
            for g in gs:
                top16(sbufs[t][:, g, :], tv16[:, g, :], ti16[t][:, g, :], w=[t_sc[t]])

        def pairs(t):
            tv4 = tv16.rearrange("p (h q) k -> p h q k", q=2)
            c4 = cand.rearrange("p h (a b) -> p h a b", a=16)
            V(ve.tensor_tensor, c4, tv4[:, :, 0, :].unsqueeze(3).to_broadcast([128, 8, 16, 16]),
              tv4[:, :, 1, :].unsqueeze(2).to_broadcast([128, 8, 16, 16]), ALU.add)
            for h in range(8):
                top16(cand[:, h, :], bs[t][:, h, :], bp[t][:, h, :])
            V(ve.tensor_copy, tif[t], ti16[t])
            for q, (sv, op) in enumerate(((4, ALU.logical_shift_right), (15, ALU.bitwise_and))):
                V(ve.tensor_scalar, pa, bp[t], sv, None, op)
                V(ve.tensor_copy, pf[t][q], pa)
            g3 = res[t][2].rearrange("p (h k) -> p h k", h=8)
            tv = V(ve.tensor_tensor, g3, bs[t], bs[t][:, :, 0:1].to_broadcast([128, 8, 16]), ALU.subtract)
            return A(se.activation, g3, g3, ACT.Exp, w=[tv])

        def gates_of(t, ta):
            g3 = res[t][2].rearrange("p (h k) -> p h k", h=8)
            V(ve.tensor_reduce, sm[:, 0:8], g3, AX.X, ALU.add, w=[ta])
            V(ve.reciprocal, sm[:, 8:16], sm[:, 0:8])
            V(ve.tensor_tensor, g3, g3, sm[:, 8:16].unsqueeze(2).to_broadcast([128, 8, 16]), ALU.mult)

        def select(t, q):
            tv = V(ve.tensor_tensor, eq, pf[t][q].unsqueeze(3).to_broadcast([128, 8, 16, 16]),
                   cst("iota16").unsqueeze(1).unsqueeze(1).to_broadcast([128, 8, 16, 16]), ALU.is_equal)
            tr4 = tif[t].rearrange("p (h q) k -> p h q k", q=2)
            return G(ge.tensor_tensor, eq, eq, tr4[:, :, q, :].unsqueeze(2).to_broadcast([128, 8, 16, 16]),
                     ALU.mult, w=[tv])

        def selected(t, q, tg):
            return V(ve.tensor_reduce, res[t][q].rearrange("p (h k) -> p h k", h=8), eq, AX.X, ALU.add, w=[tg])

        def turn(t, tv):
            b, tok, users = transposes(res[t], w=[tv])
            c = slice(128 * t, 128 * t + 128)
            V(ve.tensor_copy, i01[:, :, c], b[:, 0:256].rearrange("p (q t) -> p q t", q=2), w=[tok])
            users.append(V(ve.tensor_copy, gt3, b[:, 256:384]))
            for q in range(3):
                V(ve.tensor_copy, gp[:, q, c], gt3)
                if q < 2:
                    V(ve.tensor_tensor, gt3, gt3, gp[:, q, c], ALU.subtract)

        t_oj = [None, None]
        t_free = [None]
        nb = [0]

        def build_w(qd, bt):
            n = nb[0] % 2
            nb[0] += 1
            oj, oi = ojs[n], ois[n]
            c = slice(16 * bt, 16 * bt + 16)
            V(ve.tensor_tensor, oj, i01[:, 1, c].unsqueeze(1).to_broadcast([128, 128, 16]), iotab, ALU.is_equal,
              w=[t_oj[n], t_iota])
            V(ve.tensor_tensor, eqb, i01[:, 0, c].unsqueeze(1).to_broadcast([128, 32, 16]),
              iotab[:, 32 * qd:32 * qd + 32, :], ALU.is_equal)
            for q in range(3):
                tv = V(ve.tensor_tensor, oi[:, q], eqb, gp[:, q, c].unsqueeze(1).to_broadcast([128, 32, 16]),
                       ALU.mult)

            def rest():
                b, fw, users = banks.get(WORK)
                for j in range(16):
                    for q in range(3):
                        tok = P(te.matmul, b[:, 32 * j:32 * j + 32], oj[:, :, j], oi[:, q, :, j], start=(q == 0),
                                stop=(q == 2), w=[tv, *fw], inc=(j == 15 and q == 2))
                t_oj[n] = tok
                cc = slice(16 * (bt % 8), 16 * (bt % 8) + 16)
                t_w[0] = A(se.activation, wgt[:, bt // 8, :, cc], b.rearrange("p (t i) -> p i t", t=16), ACT.Copy,
                           w=[tok, t_free[0]])
                users.append(t_w[0])
            return rest

        for i in range(4):
            first_half(i)
        ranks(0, range(16))
        te0 = pairs(0)
        tg = select(0, 0)
        ranks(1, range(8))
        gates_of(0, te0)
        selected(0, 0, tg)
        tg = select(0, 1)
        for i in range(4, 6):
            first_half(i)
        ranks(1, range(8, 16))
        tv = selected(0, 1, tg)
        turn(0, tv)
        te1 = pairs(1)
        tg = select(1, 0)
        first_half(6)
        rests = [build_w(0, 0)]

        def built(bts):
            for bt in bts:
                rests.append(build_w(0, bt))
                rests.pop(0)()

        built(range(1, 4))
        first_half(7)
        gates_of(1, te1)
        selected(1, 0, tg)
        tg = select(1, 1)
        built(range(4, 8))
        tv = selected(1, 1, tg)
        turn(1, tv)
        if STOP == "topk":
            return finish()
        built(range(8, 16))
        rests.pop(0)()
        first_half(8)
        old, order = ring, [(ring.n + i) % NSLOT for i in (0, 1, 4, 2, 3)]
        slots_r = [ring_r[s] for s in order]
        high = [slots_r[3][:, 2048 * i:2048 * i + 2048] for i in range(2)]
        hTh = v4(slots_r[4][:, 0:2048], 8)
        slot_h = [v4(slots_r[4][:, 2048 + 1024 * i:3072 + 1024 * i], 4) for i in range(2)]
        t_high = [[], []]
        t_slot_h = [None, None]
        V.wait([t for s in order[3:] for t in old.users[s]])
        ring = Ring(SP, [old.bufs[s] for s in order[:3]], [old.sems[s] for s in order[:3]])
        ring.n, ring.users = 3, [old.users[s] for s in order[:3]]

        def split(x, low, hi, w=()):
            V(ve.tensor_copy, hi, x, w=w)
            return V(ve.tensor_tensor, low, x, hi.bitcast(F32), ALU.subtract)

        def three(out, ah, al, bh, bl, start, stop, w=(), inc=True):
            P(te.matmul, out, ah, bh, start=start, stop=False, w=w, inc=False, skip_group_check=True)
            P(te.matmul, out, ah, bl, start=False, stop=False, inc=False, skip_group_check=True)
            return P(te.matmul, out, al, bh, start=False, stop=stop, inc=inc, skip_group_check=True)

        def low_tile(k):
            return slots_r[(ring.n - 1) % 3][:, 0:4096].rearrange("p (k n) -> p k n", k=k)

        t_hT = None

        def first_split(i):
            ut, tt, tu = wtile(T["uT"], 512 * i, 512)
            low = low_tile(8)
            toks = []
            for p in range(2):
                hi = high[p].rearrange("p (k n) -> p k n", k=8)
                s = slice(256 * p, 256 * p + 256)
                toks.append(split(ut[:, :, s], low[:, :, s], hi, w=[tt, *t_high[p]]))

            def go():
                a = slots[i % NSL]
                for p in range(2):
                    hi = high[p].rearrange("p (k n) -> p k n", k=8)
                    b, fw, users = banks.get(WORK)
                    for j in range(2):
                        c = slice(128 * (2 * p + j), 128 * (2 * p + j) + 128)
                        for k in range(8):
                            tok = three(b[:, 256 * j:256 * j + 256], hi[:, k, 128 * j:128 * j + 128], low[:, k, c],
                                        hTh[:, k, :], hT_r[:, k, :], k == 0, k == 7, w=[toks[p], t_hT, *fw],
                                        inc=(j == 1 and k == 7))
                    t_high[p] = [tok]
                    ta = A(se.activation, a[:, 2 * p:2 * p + 2, :], b.rearrange("p (m t) -> p m t", m=2), ACT.Gelu,
                           w=[tok, t_slot[i % NSL]])
                    users.append(ta)
                tu.append(tok)
                t_gelu[i] = ta
            return go

        def second_split(i):
            vt, tt, tu = rtile(T["v"], 512 * i, 4, D)
            low = low_tile(4)
            ah = slot_h[i % 2]
            al = v4(arena_r[:, 1024 * (i % NSL):1024 * (i % NSL) + 1024], 4)
            t_a = split(slots[i % NSL], al, ah, w=[t_mult[i], t_slot_h[i % 2]])
            toks = []
            for p in range(2):
                hi = high[p].rearrange("p (k n) -> p k n", k=2)
                s = slice(2 * p, 2 * p + 2)
                toks.append(split(vt[:, s, :], low[:, s, :], hi, w=[tt, *t_high[p]]))

            def go():
                for j in range(4):
                    hi = high[j // 2].rearrange("p (k n) -> p k n", k=2)[:, j % 2, :]
                    for m in range(8):
                        c = slice(128 * m, 128 * m + 128)
                        tok = three(acc(m), hi[:, c], low[:, j, c], ah[:, j, :], al[:, j, :],
                                    down.first and j == 0 and m % 2 == 0, i == 31 and j == 3,
                                    w=[toks[j // 2], t_a, *down.waits], inc=(j % 2 == 1 and m == 7))
                    down.waits = []
                    if j % 2:
                        t_high[j // 2] = [tok]
                down.first = False
                tu.append(tok)
                t_slot[i % NSL] = t_slot_h[i % 2] = tok
            return go

        def gated(n):
            for s in range(2):
                half = slots[n % NSL][:, :, 128 * s:128 * s + 128]
                t_mult[n] = V(ve.tensor_tensor, half, half, wgt[:, s, 4 * (n % 8):4 * (n % 8) + 4, :], ALU.mult,
                              w=[t_w[0], t_gelu[n]])

        BATCHES = [(), (0, 1, 2), (3, 4, 5), (6, 7), (8, 9), (10, 11), (12, 13), (14, 15)]
        for i in range(8, 40):
            q = i // 8 - 1
            if 8 < i < 32:
                first_split(i)()
            if i % 8 == 0:
                gated(8 * q)
                second_split(i - 8)()
                for n in range(8 * q + 1, 8 * q + 8):
                    gated(n)
                t_free[0] = V.last
                if i == 8:
                    t_hT = split(hT, hT_r, hTh, w=[t_gelu[8]])
                continue
            if q == 3:
                second_split(i - 8)()
                continue
            bts = BATCHES[i % 8]
            rest = build_w(q + 1, bts[0])
            go = second_split(i - 8)
            rest()
            rests = [build_w(q + 1, bts[1])]
            go()
            rests += [build_w(q + 1, bt) for bt in bts[2:]]
            for rest in rests:
                rest()
        tok = P.last
        for m in range(8):
            V(ve.scalar_tensor_tensor, xT[:, m, :], acc(m), mod[:, 40 + m:41 + m], xT[:, m, :], ALU.mult, ALU.add,
              w=[tok])
        finish()


def constants():
    f = np.float32
    cs = np.zeros((128, NCS), f)

    def put(dst, table, name, x):
        o, n = table[name]
        dst[:x.shape[0], o:o + n] = x
    p = np.arange(128)
    put(cs, CS, "ident", np.eye(128, dtype=f))
    put(cs, CS, "ones", np.ones((128, 128), f))
    put(cs, CS, "bones", (p[:, None] // 64 == p[None, :] // 64).astype(f))
    partner = np.where(p % 32 < 16, p + 16, p - 16)
    put(cs, CS, "perm", (p[:, None] == partner[None, :]).astype(f))
    put(cs, CS, "tri", (p[:, None] < p[None, :]).astype(f))
    put(cs, CS, "iota", np.tile(np.arange(128, dtype=f), (128, 1)))
    put(cs, CS, "iota16", np.tile(np.arange(16, dtype=f), (128, 1)))
    put(cs, CS, "iota8", np.tile(np.arange(8, dtype=f), (128, 1)))
    t = np.arange(256)
    put(cs, CS, "scan64", np.tile((t % 64 != 0).astype(f), (128, 1)))
    put(cs, CS, "scan128", np.tile((t % 128 != 0).astype(f), (128, 1)))
    ms = np.zeros((128, NMS), np.uint32)
    j, i = p[:, None], p[None, :]
    put(ms, MS, "gla", ((j <= i) & (j // 64 == i // 64)).astype(np.uint32))
    put(ms, MS, "ssd", (j <= i).astype(np.uint32))
    col = np.arange(64)
    start = np.clip(col - 8, 0, 48)
    cm = (col[None, :] >= start[:, None]) & (col[None, :] < start[:, None] + 16)
    put(ms, MS, "col", np.tile(cm, (2, 4)).astype(np.uint32))
    hc = np.zeros((128, NHC), f)
    w = np.pi * np.outer(t, 2 * t + 1) / 512.0
    for name, m in (("C", np.cos(w)), ("S", np.sin(w)), ("CI", np.cos(w).T / 256), ("SI", -np.sin(w).T / 256)):
        put(hc, HC, name, m.reshape(2, 128, 256).transpose(1, 0, 2).reshape(128, 512).astype(f))
    tt = np.linspace(0.0, 1.0, L, dtype=f)
    deltas = np.abs(np.linspace(math.log(1e-2) / 1.5, math.log(1e-2) / 0.3, 512, dtype=f))
    dec = np.exp(-tt[:, None] * deltas)
    put(hc, HC, "dec", dec.reshape(2, 128, 512).transpose(1, 0, 2).reshape(128, 1024).astype(f))
    wv = f(2.0 * math.pi / L) * np.arange(L, dtype=f)[:, None]
    bands = np.linspace(1e-4, 15.0, 16, dtype=f)[None, :]
    feats = np.concatenate([tt[:, None], np.cos(bands * wv), -np.sin(bands * wv)], axis=-1)
    put(hc, HC, "feats", feats.T.astype(f))
    inv = (f(10000.0) ** (-np.arange(16, dtype=f) / 16)).astype(f)
    d = p % 64
    pos = np.where((d < 32)[:, None], (t // 64)[None, :], (t % 64)[None, :]).astype(f)
    ang = pos * inv[d % 16][:, None]
    put(hc, HC, "ropeC", np.cos(ang).astype(f))
    put(hc, HC, "ropeS", (np.where((d % 32 < 16)[:, None], -1, 1) * np.sin(ang)).astype(f))
    sel = np.repeat(np.eye(8, dtype=f), 128, axis=1)
    return cs, ms, hc, sel


def kernel(**x):
    import concourse.bacc as bacc
    from concourse.bass_utils import run_bass_kernel_spmd

    x = {k: np.asarray(v) for k, v in x.items()}
    f = np.float32
    cs, ms, hc, sel = constants()
    pv = np.zeros((128, NPV), f)

    def vec(name, v):
        v = v.reshape(-1)
        o, n = PV[name]
        pv[:, o:o + n] = v.reshape(n, 128).T

    def rows(name, m):
        o, n = PV[name]
        pv[:m.shape[0], o:o + n] = m

    for l in range(2):
        vec(f"ada_b{l}", x["ada_b"][l])
        vec(f"norm1_w{l}", x["norm1_w"][l])
        vec(f"norm2_w{l}", x["norm2_w"][l])
        vec(f"gla_a_b{l}", x["gla_a_b"][l])
        vec(f"gla_norm_w{l}", x["gla_norm_w"][l])
        vec(f"conv_w{l}", x["conv_w"][l])
        vec(f"conv_b{l}", x["conv_b"][l])
        rows(f"dt_bias{l}", x["dt_bias"][l][:, None])
        rows(f"a_log{l}", x["a_log"][l][:, None])
        vec(f"d_skip{l}", np.repeat(x["d_skip"][l], 64))
        vec(f"ssd_norm_w{l}", x["ssd_norm_w"][l])
        rows(f"gla_a_w{l}", x["gla_a_w"][l])
    vec("c", x["c"][0])
    o, n = PV["c2"]
    pv[:, o:o + n:2] = x["c_2"][0].reshape(8, 128).T
    pv[:, o + 1:o + n:2] = x["c_ctx_2"].reshape(8, 128).T
    vec("final_w", x["final_norm_w"])
    vec("norm1_g", x["norm1_g_2"][0])
    vec("norm2_g", x["norm2_g_2"][0])
    vec("b_ada", x["b_ada_2"][0])
    vec("b_in", x["b_in_2"][0])
    vec("hcw", x["hy_conv_w_2"][0])
    vec("hcb", x["hy_conv_b_2"][0])
    for name, key in (("f1b", "hy_f1_b_2"), ("f2b", "hy_f2_b_2"), ("f3b", "hy_f3_b_2"), ("freq", "hy_sin_freq_2")):
        rows(name, x[key][0][:, None])
    vec("skip", x["hy_skip_2"][0])
    vec("qg", np.concatenate([x["q_norm_g_2"][0]] * 2))
    vec("kg", np.concatenate([x["k_norm_g_2"][0]] * 2))
    rows("router", x["router_w"][0].reshape(8, 128, 8).transpose(1, 0, 2).reshape(128, 64))
    rows("f1w", x["hy_f1_w_2"][0])
    rows("f2w", x["hy_f2_w_2"][0])
    rows("f3w", x["hy_f3_w_2"][0])
    rows("bv", x["b_in_2"][0][None, 2560:3072])

    r, qc, i, kc = np.arange(4), np.arange(64), np.arange(4), np.arange(64)
    dr = (i[None, :] - r[:, None] + 7)[:, None, :, None]
    dcx = (np.clip(kc[None, :] - qc[:, None], -15, 15) + 15)[None, :, None, :]
    bias = x["na_rpb_2"][0][:, dr, dcx].reshape(8, 2, 128, 256).transpose(2, 1, 0, 3).reshape(128, 4096)

    arrays = {
        "pv": pv, "cs": cs, "ms": ms, "hc": hc, "sel": sel, "xT": x["x"][0].T, "ctxT": x["ctx_2"][0].T,
        "ada_w": x["ada_w"], "w_in": x["w_in"], "w_out": x["w_out"],
        "ffn_w_gate": x["ffn_w_gate"][0], "ffn_w_up": x["ffn_w_up"][0], "ffn_w_down": x["ffn_w_down"][0],
        "moe_w_gate": x["moe_w_gate"][0], "moe_w_up": x["moe_w_up"][0], "moe_w_down": x["moe_w_down"][0],
        "w_ada": x["w_ada_2"][0], "w_in2": x["w_in_2"][0], "f4w": x["hy_f4_w_2"][0],
        "w_hy": x["w_hy_out_2"][0], "w_na": x["w_na_out_2"][0], "w_out2": x["w_out_2"][0],
        "w_pq": x["peer_w_q_2"][0],
        "keysT": x["peer_keys_2"][0].transpose(3, 0, 1, 2).reshape(128, 2048),
        "uT": x["peer_u_2"][0].T, "v": x["peer_v_2"][0], "bias": bias,
    }
    nc = bacc.Bacc("TRN2", target_bir_lowering=False, num_devices=1)
    ins, T = {}, {}
    for name, a in arrays.items():
        a = np.ascontiguousarray(a)
        ins[f"in_{name}"] = a
        T[name] = nc.dram_tensor(f"in_{name}", a.shape, mybir.dt.from_np(a.dtype), kind="ExternalInput").ap()
    T["out"] = nc.dram_tensor("out_x", (1024, 256), F32, kind="ExternalOutput").ap()
    program(nc, T)
    res = run_bass_kernel_spmd(nc, [ins], core_ids=[0])
    return np.ascontiguousarray(res.results[0]["out_x"].T)[None]
```
